# Optimizing a Trainium2 kernel written in Bass

```python
import math
import jax, jax.numpy as jnp
from jax import lax
import numpy as np
import jax
import jax.numpy as jnp

D_MODEL = 1024
BATCH = 1
SEQ = 256
DEPTH = 1

M_HEADS = 4
M_HEAD_DIM = D_MODEL // (2 * M_HEADS)
M_CHUNK = 64
CONV_W = 4
A_HEADS = 8
A_KV_GROUPS = 2
A_HPG = A_HEADS // A_KV_GROUPS
A_HEAD_DIM = D_MODEL // (2 * A_HEADS)
CMP_BLOCK = 32
CMP_STRIDE = 16
SEL_BLOCK = 64
SEL_TOP_N = 16
WINDOW = 512
Q_BLOCK = 128
FORCED_BONUS = 1e3
NUM_BUCKETS = 32
MAX_DISTANCE = 128
N_EXPERTS = 32
TOP_K = 4
D_EXPERT = D_MODEL
SWIGLU_LIMIT = 7.0
SWIGLU_ALPHA = 1.702
EXPERT_ROWS = 128
EPS = 1e-6
D_MIX = M_HEADS * M_HEAD_DIM + A_HEADS * A_HEAD_DIM
SPLIT_SIZES = (
    M_HEADS * M_HEAD_DIM,
    M_HEADS * M_HEAD_DIM,
    M_HEADS * M_HEAD_DIM,
    M_HEADS * M_HEAD_DIM,
    M_HEADS,
    M_HEADS,
    A_HEADS * A_HEAD_DIM,
    A_KV_GROUPS * A_HEAD_DIM,
    A_KV_GROUPS * A_HEAD_DIM,
    A_KV_GROUPS * A_HEAD_DIM,
    A_KV_GROUPS * A_HEAD_DIM,
    A_KV_GROUPS * A_HEAD_DIM,
    A_KV_GROUPS * A_HEAD_DIM,
    A_HEADS * 3,
)
D_IN = sum(SPLIT_SIZES)


def rmsnorm(x, g):
    xf = x.astype(jnp.float32)
    y = xf * lax.rsqrt(jnp.mean(xf * xf, axis=-1, keepdims=True) + EPS)
    return (y * g.astype(jnp.float32)).astype(x.dtype)

def t5_bucket(dist):
    n = jnp.maximum(dist, 0)
    max_exact = NUM_BUCKETS // 2
    nf = jnp.maximum(n, 1).astype(jnp.float32)
    large = max_exact + (jnp.log(nf / max_exact) / math.log(MAX_DISTANCE / max_exact)
                         * (NUM_BUCKETS - max_exact)).astype(jnp.int32)
    large = jnp.minimum(large, NUM_BUCKETS - 1)
    return jnp.where(n < max_exact, n, large)

def masked_softmax(logits, valid):
    l = jnp.where(valid, logits, -jnp.inf)
    m = jnp.max(l, axis=-1, keepdims=True)
    m = jnp.where(jnp.isfinite(m), m, 0.0)
    e = jnp.where(valid, jnp.exp(l - m), 0.0)
    s = jnp.sum(e, axis=-1, keepdims=True)
    return e / jnp.where(s > 0, s, 1.0)

def causal_depthwise_conv(x, w):
    return lax.conv_general_dilated(
        x, w[:, None, :].astype(x.dtype), window_strides=(1,), padding=[(CONV_W - 1, 0)],
        dimension_numbers=('NWC', 'WIO', 'NWC'), feature_group_count=x.shape[-1])

def mlstm(q, k, v, i_pre, f_pre):
    dtype = q.dtype
    B_, S_, H_, Dh = q.shape
    nc = S_ // M_CHUNK
    f32 = jnp.float32

    def chunks(a):
        return a.astype(f32).reshape(B_, nc, M_CHUNK, H_, -1).transpose(0, 3, 1, 2, 4)

    qc = chunks(q)
    kc = chunks(k) * (Dh ** -0.5)
    vc = chunks(v)
    ig = i_pre.astype(f32).reshape(B_, nc, M_CHUNK, H_).transpose(0, 3, 1, 2)
    lf = jax.nn.log_sigmoid(f_pre.astype(f32)).reshape(B_, nc, M_CHUNK, H_).transpose(0, 3, 1, 2)
    g = jnp.cumsum(lf, axis=-1)
    G = g[..., -1]
    w_state = G[..., None] - g + ig

    def step(carry, xs):
        C, n, m = carry
        k_c, v_c, w_c, G_c = xs
        m_new = jnp.maximum(G_c + m, jnp.max(w_c, axis=-1))
        decay = jnp.exp(G_c + m - m_new)
        wexp = jnp.exp(w_c - m_new[..., None])
        C_new = decay[..., None, None] * C + jnp.einsum('bhl,bhld,bhle->bhde', wexp, k_c, v_c)
        n_new = decay[..., None] * n + jnp.einsum('bhl,bhld->bhd', wexp, k_c)
        return (C_new, n_new, m_new), (C, n, m)

    init = (jnp.zeros((B_, H_, Dh, Dh), f32), jnp.zeros((B_, H_, Dh), f32),
            jnp.full((B_, H_), -jnp.inf, f32))
    xs = (kc.transpose(2, 0, 1, 3, 4), vc.transpose(2, 0, 1, 3, 4),
          w_state.transpose(2, 0, 1, 3), G.transpose(2, 0, 1))
    _, (Cp, Np, Mp) = lax.scan(step, init, xs)
    Cp = Cp.transpose(1, 2, 0, 3, 4)
    Np = Np.transpose(1, 2, 0, 3)
    Mp = Mp.transpose(1, 2, 0)

    causal = jnp.tril(jnp.ones((M_CHUNK, M_CHUNK), bool))
    Dm = jnp.where(causal, g[..., :, None] - g[..., None, :] + ig[..., None, :], -jnp.inf)
    inter = g + Mp[..., None]
    m_tau = jnp.maximum(inter, jnp.max(Dm, axis=-1))
    Wm = jnp.exp(Dm - m_tau[..., None]) * jnp.einsum('bhcld,bhcsd->bhcls', qc, kc)
    inter_w = jnp.exp(inter - m_tau)
    num = (jnp.einsum('bhcls,bhcse->bhcle', Wm, vc)
           + inter_w[..., None] * jnp.einsum('bhcld,bhcde->bhcle', qc, Cp))
    den = jnp.sum(Wm, axis=-1) + inter_w * jnp.einsum('bhcld,bhcd->bhcl', qc, Np)
    h = num / jnp.maximum(jnp.abs(den), jnp.exp(-m_tau))[..., None]
    return h.transpose(0, 2, 3, 1, 4).reshape(B_, S_, H_ * Dh).astype(dtype)

def compress(k, pos_emb, w):
    S_ = k.shape[1]
    n_cmp = (S_ - CMP_BLOCK) // CMP_STRIDE + 1
    idx = jnp.arange(n_cmp)[:, None] * CMP_STRIDE + jnp.arange(CMP_BLOCK)[None, :]
    blocks = k[:, idx] + pos_emb[None, None, :, None, :]
    return jnp.einsum('bilgd,lde->bige', blocks, w)

def nsa(q, kc, vc, ks, vs, kw, vw, gates, rel_bias):
    B_, S_, G_, HPG_, Dh = q.shape
    scale = Dh ** -0.5
    f32 = jnp.float32
    n_cmp = kc.shape[1]
    n_sel = S_ // SEL_BLOCK
    top_n = min(SEL_TOP_N, n_sel)
    n_tok = top_n * SEL_BLOCK
    cmp_end = jnp.arange(n_cmp) * CMP_STRIDE + CMP_BLOCK - 1
    cmp_pos = jnp.arange(n_cmp)[:, None] * CMP_STRIDE + jnp.arange(CMP_BLOCK)[None, :]
    overlap = jnp.sum(jax.nn.one_hot(cmp_pos // SEL_BLOCK, n_sel, dtype=f32), axis=1) / CMP_BLOCK
    ks_blk = ks.reshape(B_, n_sel, SEL_BLOCK, G_, Dh).transpose(0, 3, 1, 2, 4).reshape(B_, G_, n_sel, SEL_BLOCK * Dh)
    vs_blk = vs.reshape(B_, n_sel, SEL_BLOCK, G_, Dh).transpose(0, 3, 1, 2, 4).reshape(B_, G_, n_sel, SEL_BLOCK * Dh)
    kw_pad = jnp.pad(kw, ((0, 0), (WINDOW, 0), (0, 0), (0, 0)))
    vw_pad = jnp.pad(vw, ((0, 0), (WINDOW, 0), (0, 0), (0, 0)))
    rb = rel_bias.reshape(NUM_BUCKETS, G_, HPG_)
    g_idx = jnp.arange(G_)[None, None, :, None]
    blk = jnp.arange(n_sel)
    sel_off = jnp.arange(SEL_BLOCK)
    win_off = jnp.arange(Q_BLOCK + WINDOW) - WINDOW

    def block(qb):
        q0 = qb * Q_BLOCK
        t = q0 + jnp.arange(Q_BLOCK)
        qq = lax.dynamic_slice_in_dim(q, q0, Q_BLOCK, axis=1)
        lc = jnp.einsum('bqghd,bigd->bqghi', qq, kc, preferred_element_type=f32) * scale
        lc = lc + rb[t5_bucket(t[:, None] - cmp_end[None, :])].transpose(0, 2, 3, 1)[None]
        valid_c = (cmp_end[None, :] <= t[:, None])[None, :, None, None, :]
        pc = masked_softmax(lc, valid_c)
        oc = jnp.einsum('bqghi,bigd->bqghd', pc, vc)
        ps = jnp.einsum('bqghi,ij->bqgj', pc, overlap)
        cur = t // SEL_BLOCK
        forced = (blk[None, :] == 0) | (blk[None, :] == cur[:, None]) | (blk[None, :] == cur[:, None] - 1)
        valid_b = blk[None, :] * SEL_BLOCK <= t[:, None]
        score = jnp.where(valid_b[None, :, None, :],
                          ps + jnp.where(forced, FORCED_BONUS, 0.0)[None, :, None, :], -jnp.inf)
        _, sel = lax.top_k(score, top_n)
        sel_t = sel.transpose(0, 2, 1, 3).reshape(B_, G_, Q_BLOCK * top_n)[..., None]
        kg = jnp.take_along_axis(ks_blk, sel_t, axis=2).reshape(B_, G_, Q_BLOCK, n_tok, Dh)
        vg = jnp.take_along_axis(vs_blk, sel_t, axis=2).reshape(B_, G_, Q_BLOCK, n_tok, Dh)
        tok = (sel[..., None] * SEL_BLOCK + sel_off).reshape(B_, Q_BLOCK, G_, n_tok)
        ls = jnp.einsum('bqghd,bgqnd->bqghn', qq, kg, preferred_element_type=f32) * scale
        bs = rb[t5_bucket(t[None, :, None, None] - tok), g_idx]
        ls = ls + bs.transpose(0, 1, 2, 4, 3)
        pss = masked_softmax(ls, (tok <= t[None, :, None, None])[:, :, :, None, :])
        osel = jnp.einsum('bqghn,bgqnd->bqghd', pss, vg)
        kwb = lax.dynamic_slice_in_dim(kw_pad, q0, Q_BLOCK + WINDOW, axis=1)
        vwb = lax.dynamic_slice_in_dim(vw_pad, q0, Q_BLOCK + WINDOW, axis=1)
        j = q0 + win_off
        dist = t[:, None] - j[None, :]
        valid_w = (j[None, :] >= 0) & (dist >= 0) & (dist < WINDOW)
        lw = jnp.einsum('bqghd,bkgd->bqghk', qq, kwb, preferred_element_type=f32) * scale
        lw = lw + rb[t5_bucket(dist)].transpose(0, 2, 3, 1)[None]
        pw = masked_softmax(lw, valid_w[None, :, None, None, :])
        ow = jnp.einsum('bqghk,bkgd->bqghd', pw, vwb)
        gg = lax.dynamic_slice_in_dim(gates, q0, Q_BLOCK, axis=1).astype(f32)
        o = gg[..., 0:1] * oc + gg[..., 1:2] * osel + gg[..., 2:3] * ow
        return o.reshape(B_, Q_BLOCK, G_ * HPG_ * Dh).astype(q.dtype)

    out = lax.map(block, jnp.arange(S_ // Q_BLOCK))
    return out.transpose(1, 0, 2, 3).reshape(B_, S_, G_ * HPG_ * Dh)

def moe(h, w_router, b_router, w_up, b_up, w_down, b_down):
    B_, S_, D_ = h.shape
    N = B_ * S_
    NK = N * TOP_K
    xf = h.reshape(N, D_)
    logits = jnp.dot(xf, w_router, preferred_element_type=jnp.float32) + b_router.astype(jnp.float32)
    vals, idx = lax.top_k(logits, TOP_K)
    gate = jax.nn.softmax(vals, axis=-1)
    e_flat = idx.reshape(NK)
    tok_flat = jnp.arange(NK) // TOP_K
    gate_flat = gate.reshape(NK)
    order = jnp.argsort(e_flat)
    sorted_e = e_flat[order]
    counts = jnp.bincount(e_flat, length=N_EXPERTS)
    starts = jnp.cumsum(counts) - counts
    padded = (counts + EXPERT_ROWS - 1) // EXPERT_ROWS * EXPERT_ROWS
    pends = jnp.cumsum(padded)
    pstarts = pends - padded
    dest = pstarts[sorted_e] + (jnp.arange(NK) - starts[sorted_e])
    R = NK + N_EXPERTS * EXPERT_ROWS
    n_blk = R // EXPERT_ROWS
    row_tok = jnp.full((R,), N, jnp.int32).at[dest].set(tok_flat[order])
    row_gate = jnp.zeros((R,), jnp.float32).at[dest].set(gate_flat[order])
    blk_e = jnp.minimum(jnp.sum(jnp.arange(n_blk)[:, None] * EXPERT_ROWS >= pends[None, :], axis=1),
                        N_EXPERTS - 1)
    x_pad = jnp.concatenate([xf, jnp.zeros((1, D_), xf.dtype)], axis=0)
    xin = x_pad[row_tok].reshape(n_blk, EXPERT_ROWS, D_)

    def expert_block(args):
        xb, eb = args
        up = jnp.dot(xb, w_up[eb]) + b_up[eb]
        glu, lin = jnp.split(up, 2, axis=-1)
        glu = jnp.minimum(glu, SWIGLU_LIMIT)
        lin = jnp.clip(lin, -SWIGLU_LIMIT, SWIGLU_LIMIT)
        act = glu * jax.nn.sigmoid(SWIGLU_ALPHA * glu) * (lin + 1.0)
        return jnp.dot(act, w_down[eb]) + b_down[eb]

    yb = lax.map(expert_block, (xin, blk_e)).reshape(R, D_)
    out = jnp.zeros((N + 1, D_), h.dtype).at[row_tok].add(yb * row_gate[:, None].astype(h.dtype))
    return out[:N].reshape(B_, S_, D_)

def first_inputs(seed: int = 0) -> dict:
    key = jax.random.key(seed)
    ks = jax.random.split(key, 24)
    nrm = lambda k, shape, s: jax.random.normal(k, shape, jnp.float32) * s
    L = DEPTH
    gate_base = jnp.concatenate([jnp.zeros((M_HEADS,), jnp.float32),
                                 jnp.linspace(3.0, 6.0, M_HEADS, dtype=jnp.float32)])
    return {
        "x": nrm(ks[0], (BATCH, SEQ, D_MODEL), 1.0),
        "c": nrm(ks[1], (BATCH, D_MODEL), 1.0),
        "w_ada": nrm(ks[2], (L, D_MODEL, 6 * D_MODEL), 0.5 * D_MODEL ** -0.5),
        "b_ada": nrm(ks[3], (L, 6 * D_MODEL), 0.02),
        "g_pre_mix": 1.0 + nrm(ks[4], (L, D_MODEL), 0.05),
        "g_post_mix": 1.0 + nrm(ks[5], (L, D_MODEL), 0.05),
        "g_pre_ffn": 1.0 + nrm(ks[6], (L, D_MODEL), 0.05),
        "g_post_ffn": 1.0 + nrm(ks[7], (L, D_MODEL), 0.05),
        "w_in": nrm(ks[8], (L, D_MODEL, D_IN), D_MODEL ** -0.5),
        "b_gates": gate_base + nrm(ks[9], (L, 2 * M_HEADS), 0.1),
        "conv_qk": nrm(ks[10], (L, CONV_W, 2 * M_HEADS * M_HEAD_DIM), CONV_W ** -0.5),
        "w_cmp_k": nrm(ks[11], (L, CMP_BLOCK, A_HEAD_DIM, A_HEAD_DIM), (CMP_BLOCK * A_HEAD_DIM) ** -0.5),
        "w_cmp_v": nrm(ks[12], (L, CMP_BLOCK, A_HEAD_DIM, A_HEAD_DIM), (CMP_BLOCK * A_HEAD_DIM) ** -0.5),
        "pos_cmp_k": nrm(ks[13], (L, CMP_BLOCK, A_HEAD_DIM), 0.1),
        "pos_cmp_v": nrm(ks[14], (L, CMP_BLOCK, A_HEAD_DIM), 0.1),
        "rel_bias": nrm(ks[15], (NUM_BUCKETS, A_HEADS), 0.5),
        "w_out": nrm(ks[16], (L, D_MIX, D_MODEL), D_MIX ** -0.5),
        "w_router": nrm(ks[17], (L, D_MODEL, N_EXPERTS), D_MODEL ** -0.5),
        "b_router": nrm(ks[18], (L, N_EXPERTS), 0.01),
        "w_up": nrm(ks[19], (L, N_EXPERTS, D_MODEL, 2 * D_EXPERT), D_MODEL ** -0.5),
        "b_up": nrm(ks[20], (L, N_EXPERTS, 2 * D_EXPERT), 0.01),
        "w_down": nrm(ks[21], (L, N_EXPERTS, D_EXPERT, D_MODEL), D_EXPERT ** -0.5),
        "b_down": nrm(ks[22], (L, N_EXPERTS, D_MODEL), 0.01),
    }

def first_block(x, c, w_ada, b_ada, g_pre_mix, g_post_mix, g_pre_ffn, g_post_ffn, w_in, b_gates,
              conv_qk, w_cmp_k, w_cmp_v, pos_cmp_k, pos_cmp_v, rel_bias, w_out, w_router, b_router,
              w_up, b_up, w_down, b_down):
    B_, S_, _ = x.shape
    split_at = np.cumsum(SPLIT_SIZES)[:-1].tolist()
    for l in range(DEPTH):
        mod = jnp.dot(jax.nn.silu(c), w_ada[l]) + b_ada[l]
        sh1, sc1, gt1, sh2, sc2, gt2 = [m[:, None, :] for m in jnp.split(mod, 6, axis=-1)]
        h = rmsnorm(x, g_pre_mix[l]) * (1.0 + sc1) + sh1
        z = jnp.dot(h, w_in[l])
        (q_m, k_m, v_m, o_m, i_m, f_m, q_a, kc_a, vc_a, ks_a, vs_a, kw_a, vw_a, g_a) = \
            jnp.split(z, split_at, axis=-1)
        qk = jax.nn.silu(causal_depthwise_conv(jnp.concatenate([q_m, k_m], axis=-1), conv_qk[l]))
        q_m, k_m = jnp.split(qk, 2, axis=-1)
        mh = lambda a: a.reshape(B_, S_, M_HEADS, M_HEAD_DIM)
        y_m = mlstm(mh(q_m), mh(k_m), mh(v_m),
                    i_m + b_gates[l, :M_HEADS], f_m + b_gates[l, M_HEADS:])
        y_m = y_m * jax.nn.sigmoid(o_m)
        kv = lambda a: a.reshape(B_, S_, A_KV_GROUPS, A_HEAD_DIM)
        kc = compress(kv(kc_a), pos_cmp_k[l], w_cmp_k[l])
        vc = compress(kv(vc_a), pos_cmp_v[l], w_cmp_v[l])
        y_a = nsa(q_a.reshape(B_, S_, A_KV_GROUPS, A_HPG, A_HEAD_DIM), kc, vc,
                  kv(ks_a), kv(vs_a), kv(kw_a), kv(vw_a),
                  jax.nn.sigmoid(g_a).reshape(B_, S_, A_KV_GROUPS, A_HPG, 3), rel_bias)
        y = jnp.dot(jnp.concatenate([y_m, y_a], axis=-1), w_out[l])
        x = x + gt1 * rmsnorm(y, g_post_mix[l])
        h2 = rmsnorm(x, g_pre_ffn[l]) * (1.0 + sc2) + sh2
        y2 = moe(h2, w_router[l], b_router[l], w_up[l], b_up[l], w_down[l], b_down[l])
        x = x + gt2 * rmsnorm(y2, g_post_ffn[l])
    return x


ATT_HEADS = 8
ATT_KV_HEADS = 2
ATT_HEAD_DIM = 128
ATT_GROUP = ATT_HEADS // ATT_KV_HEADS
ROPE_THETA = 500000.0
ROPE_FRACTION = 4
IDX_HEADS = 4
IDX_DIM = 64
TOPK_MAX = 256
SSM_EXPAND = 2
SSM_D_INNER = SSM_EXPAND * D_MODEL
SSM_HEAD_DIM = 64
SSM_HEADS = SSM_D_INNER // SSM_HEAD_DIM
SSM_GROUPS = 4
SSM_STATE = 128
SSM_CONV = 4
SSM_CHUNK = 128
N_BRANCHES = 2

ATT_Q_DIM = ATT_HEADS * ATT_HEAD_DIM
ATT_KV_DIM = ATT_KV_HEADS * ATT_HEAD_DIM
ATT_ROT_DIM = ATT_HEAD_DIM // ROPE_FRACTION
IDX_ROT_DIM = IDX_DIM // ROPE_FRACTION
SSM_CONV_DIM = SSM_D_INNER + 2 * SSM_GROUPS * SSM_STATE
IN_SPLITS = (ATT_Q_DIM, ATT_KV_DIM, ATT_KV_DIM, ATT_Q_DIM, IDX_HEADS * IDX_DIM, IDX_DIM, IDX_HEADS,
             SSM_D_INNER, SSM_CONV_DIM, SSM_HEADS, N_BRANCHES * D_MODEL)
IN_DIM = sum(IN_SPLITS)


def _split_points():
    pts, acc = [], 0
    for s in IN_SPLITS[:-1]:
        acc += s
        pts.append(acc)
    return pts

def rms_norm(x, g):
    xf = x.astype(jnp.float32)
    y = xf * lax.rsqrt(jnp.mean(xf * xf, axis=-1, keepdims=True) + EPS)
    return y.astype(x.dtype) * g

def layer_norm(x, g, b):
    xf = x.astype(jnp.float32)
    mu = jnp.mean(xf, axis=-1, keepdims=True)
    var = jnp.mean(jnp.square(xf - mu), axis=-1, keepdims=True)
    return ((xf - mu) * lax.rsqrt(var + EPS)).astype(x.dtype) * g + b

def rope_tables(positions, rot_dim):
    inv = jnp.power(ROPE_THETA, -(jnp.arange(0, rot_dim, 2, dtype=jnp.float32) / rot_dim))
    ang = positions.astype(jnp.float32)[..., None] * inv
    return jnp.cos(ang)[:, :, None, :], jnp.sin(ang)[:, :, None, :]

def partial_rope(x, cos, sin):
    half = cos.shape[-1]
    rot = 2 * half
    x1 = x[..., :half].astype(jnp.float32)
    x2 = x[..., half:rot].astype(jnp.float32)
    r1 = x1 * cos - x2 * sin
    r2 = x2 * cos + x1 * sin
    return jnp.concatenate([r1.astype(x.dtype), r2.astype(x.dtype), x[..., rot:]], axis=-1)

def causal_depthwise_conv_2(u, w, b):
    ch = u.shape[-1]
    y = lax.conv_general_dilated(u, w[:, None, :].astype(u.dtype), window_strides=(1,),
                                 padding=[(SSM_CONV - 1, 0)],
                                 dimension_numbers=("NWC", "WIO", "NWC"),
                                 feature_group_count=ch)
    return y + b

def segsum(a):
    n = a.shape[-1]
    ar = jnp.broadcast_to(a[..., :, None], a.shape + (n,))
    ar = jnp.where(jnp.tril(jnp.ones((n, n), dtype=bool), -1), ar, 0.0)
    cs = jnp.cumsum(ar, axis=-2)
    return jnp.where(jnp.tril(jnp.ones((n, n), dtype=bool)), cs, -jnp.inf)

def ssd(xh, dt, a, bm, cm):
    bsz, s, h, p = xh.shape
    g, n = bm.shape[2], bm.shape[3]
    r = h // g
    nc, ln = s // SSM_CHUNK, SSM_CHUNK
    xc = (xh * dt[..., None]).reshape(bsz, nc, ln, g, r, p)
    adt = (dt * a).reshape(bsz, nc, ln, g, r).transpose(0, 1, 3, 4, 2)
    a_cum = jnp.cumsum(adt, axis=-1)
    bc = bm.reshape(bsz, nc, ln, g, n)
    cc = cm.reshape(bsz, nc, ln, g, n)
    decay = jnp.exp(segsum(adt))
    cb = jnp.einsum("bclgn,bcsgn->bcgls", cc, bc)
    y_diag = jnp.einsum("bcgls,bcgrls,bcsgrp->bclgrp", cb, decay, xc)
    decay_states = jnp.exp(a_cum[..., -1:] - a_cum)
    states = jnp.einsum("bclgn,bcgrl,bclgrp->bcgrpn", bc, decay_states, xc)
    chunk_decay = jnp.exp(a_cum[..., -1])

    def step(hstate, inp):
        st, dec = inp
        return dec[..., None, None] * hstate + st, hstate

    h0 = jnp.zeros((bsz, g, r, p, n), dtype=xc.dtype)
    _, prev = lax.scan(step, h0, (states.swapaxes(0, 1), chunk_decay.swapaxes(0, 1)))
    prev = prev.swapaxes(0, 1)
    y_off = jnp.einsum("bclgn,bcgrpn,bcgrl->bclgrp", cc, prev, jnp.exp(a_cum))
    return (y_diag + y_off).reshape(bsz, s, h, p)

def sparse_attention(q, k, v, q_idx, k_idx, w_idx):
    bsz, s = q.shape[0], q.shape[1]
    topk = min(TOPK_MAX, s // 4)
    nblk = s // Q_BLOCK
    scale = ATT_HEAD_DIM ** -0.5
    key_pos = jnp.arange(s)
    gather = jax.vmap(lambda arr, idx: arr[idx])

    def to_blocks(arr):
        return arr.reshape((bsz, nblk, Q_BLOCK) + arr.shape[2:]).swapaxes(0, 1)

    qg = q.reshape(bsz, s, ATT_KV_HEADS, ATT_GROUP, ATT_HEAD_DIM)

    def block(args):
        blk, qb, qib, wb = args
        qpos = blk * Q_BLOCK + jnp.arange(Q_BLOCK)
        causal = key_pos[None, :] <= qpos[:, None]
        logits = jnp.einsum("bthd,bsd->bths", qib, k_idx)
        score = jnp.einsum("bth,bths->bts", wb, jax.nn.relu(logits))
        score = jnp.where(causal[None], score, -jnp.inf)
        _, sel = lax.top_k(score, topk)
        valid = sel <= qpos[None, :, None]
        ks = gather(k, sel)
        vs = gather(v, sel)
        sc = jnp.einsum("btgrd,btjgd->btgrj", qb, ks).astype(jnp.float32) * scale
        sc = jnp.where(valid[:, :, None, None, :], sc, -jnp.inf)
        pr = jax.nn.softmax(sc, axis=-1).astype(vs.dtype)
        return jnp.einsum("btgrj,btjgd->btgrd", pr, vs)

    out = lax.map(block, (jnp.arange(nblk), to_blocks(qg), to_blocks(q_idx), to_blocks(w_idx)))
    return out.swapaxes(0, 1).reshape(bsz, s, ATT_Q_DIM)

def second_inputs(seed: int = 0) -> dict:
    key = jax.random.key(seed)
    ks = jax.random.split(key, 24)
    nrm = jax.random.normal
    f32 = jnp.float32
    dt0 = jnp.exp(jax.random.uniform(ks[14], (DEPTH, SSM_HEADS), dtype=f32)
                  * (np.log(0.1) - np.log(0.001)) + np.log(0.001))
    return {
        "x": nrm(ks[0], (BATCH, SEQ, D_MODEL), f32),
        "c": nrm(ks[1], (BATCH, D_MODEL), f32),
        "positions": jnp.broadcast_to(jnp.arange(SEQ, dtype=jnp.int32)[None, :], (BATCH, SEQ)),
        "ada_w": nrm(ks[2], (DEPTH, D_MODEL, 3 * D_MODEL), f32) * (0.5 * D_MODEL ** -0.5),
        "ada_b": nrm(ks[3], (DEPTH, 3 * D_MODEL), f32) * 0.01,
        "norm_g": 1.0 + 0.1 * nrm(ks[4], (DEPTH, D_MODEL), f32),
        "w_in": nrm(ks[5], (DEPTH, D_MODEL, IN_DIM), f32) * D_MODEL ** -0.5,
        "q_norm_g": 1.0 + 0.1 * nrm(ks[6], (DEPTH, ATT_HEAD_DIM), f32),
        "k_norm_g": 1.0 + 0.1 * nrm(ks[7], (DEPTH, ATT_HEAD_DIM), f32),
        "idx_k_ln_g": 1.0 + 0.1 * nrm(ks[8], (DEPTH, IDX_DIM), f32),
        "idx_k_ln_b": 0.01 * nrm(ks[9], (DEPTH, IDX_DIM), f32),
        "conv_w": nrm(ks[10], (DEPTH, SSM_CONV, SSM_CONV_DIM), f32) * SSM_CONV ** -0.5,
        "conv_b": 0.01 * nrm(ks[11], (DEPTH, SSM_CONV_DIM), f32),
        "dt_bias": dt0 + jnp.log(-jnp.expm1(-dt0)),
        "a_log": jnp.log(jax.random.uniform(ks[12], (DEPTH, SSM_HEADS), f32, 1.0, 16.0)),
        "d_skip": 1.0 + 0.1 * nrm(ks[13], (DEPTH, SSM_HEADS), f32),
        "ssm_norm_g": 1.0 + 0.1 * nrm(ks[15], (DEPTH, SSM_D_INNER), f32),
        "w_branch_att": nrm(ks[16], (DEPTH, ATT_Q_DIM, D_MODEL), f32) * ATT_Q_DIM ** -0.5,
        "w_branch_ssm": nrm(ks[17], (DEPTH, SSM_D_INNER, D_MODEL), f32) * SSM_D_INNER ** -0.5,
        "w_out": nrm(ks[18], (DEPTH, D_MODEL, D_MODEL), f32) * D_MODEL ** -0.5,
    }

def second_block(x, c, positions, ada_w, ada_b, norm_g, w_in, q_norm_g, k_norm_g, idx_k_ln_g, idx_k_ln_b,
              conv_w, conv_b, dt_bias, a_log, d_skip, ssm_norm_g, w_branch_att, w_branch_ssm, w_out):
    f32 = jnp.float32
    bsz, s, _ = x.shape
    cos_a, sin_a = rope_tables(positions, ATT_ROT_DIM)
    cos_i, sin_i = rope_tables(positions, IDX_ROT_DIM)
    pts = _split_points()
    for l in range(DEPTH):
        mod = jax.nn.silu(c) @ ada_w[l] + ada_b[l]
        shift, scale, gate = jnp.split(mod, 3, axis=-1)
        h = rms_norm(x, norm_g[l]) * (1.0 + scale[:, None, :]) + shift[:, None, :]
        proj = h @ w_in[l]
        (q, k, v, z_att, q_idx, k_idx, w_idx, z_ssm, xbc, dt_raw, gate_logits) = jnp.split(proj, pts, axis=-1)

        q = partial_rope(rms_norm(q.reshape(bsz, s, ATT_HEADS, ATT_HEAD_DIM), q_norm_g[l]), cos_a, sin_a)
        k = partial_rope(rms_norm(k.reshape(bsz, s, ATT_KV_HEADS, ATT_HEAD_DIM), k_norm_g[l]), cos_a, sin_a)
        v = v.reshape(bsz, s, ATT_KV_HEADS, ATT_HEAD_DIM)
        q_idx = partial_rope(q_idx.reshape(bsz, s, IDX_HEADS, IDX_DIM), cos_i, sin_i) * (IDX_DIM ** -0.5)
        k_idx = partial_rope(layer_norm(k_idx, idx_k_ln_g[l], idx_k_ln_b[l])[:, :, None, :], cos_i, sin_i)[:, :, 0, :]
        w_idx = w_idx * (IDX_HEADS ** -0.5)
        o_att = sparse_attention(q, k, v, q_idx, k_idx, w_idx) * jax.nn.silu(z_att)
        y_att = o_att @ w_branch_att[l]

        xbc = jax.nn.silu(causal_depthwise_conv_2(xbc, conv_w[l], conv_b[l]))
        xs, bm, cm = jnp.split(xbc, [SSM_D_INNER, SSM_D_INNER + SSM_GROUPS * SSM_STATE], axis=-1)
        xs = xs.reshape(bsz, s, SSM_HEADS, SSM_HEAD_DIM).astype(f32)
        dt = jax.nn.softplus(dt_raw.astype(f32) + dt_bias[l].astype(f32))
        a = -jnp.exp(a_log[l].astype(f32))
        y = ssd(xs, dt, a,
                bm.reshape(bsz, s, SSM_GROUPS, SSM_STATE).astype(f32),
                cm.reshape(bsz, s, SSM_GROUPS, SSM_STATE).astype(f32))
        y = y + d_skip[l].astype(f32)[:, None] * xs
        y = y.reshape(bsz, s, SSM_D_INNER).astype(x.dtype) * jax.nn.silu(z_ssm)
        y = rms_norm(y.reshape(bsz, s, SSM_GROUPS, SSM_D_INNER // SSM_GROUPS),
                     ssm_norm_g[l].reshape(SSM_GROUPS, SSM_D_INNER // SSM_GROUPS)).reshape(bsz, s, SSM_D_INNER)
        y_ssm = y @ w_branch_ssm[l]

        g_att, g_ssm = jnp.split(gate_logits, 2, axis=-1)
        merged = jax.nn.sigmoid(g_att) * y_att + jax.nn.sigmoid(g_ssm) * y_ssm
        x = x + gate[:, None, :] * (merged @ w_out[l])
    return x


def setup_inputs(seed=0):
    out = dict(first_inputs(seed))
    for name, value in second_inputs(seed + 1).items():
        if name != "x":
            out[name + "_2"] = value
    return out


def reference(
    x, c, w_ada, b_ada, g_pre_mix, g_post_mix, g_pre_ffn, g_post_ffn, w_in, b_gates, conv_qk,
    w_cmp_k, w_cmp_v, pos_cmp_k, pos_cmp_v, rel_bias, w_out, w_router, b_router, w_up, b_up,
    w_down, b_down, c_2, positions_2, ada_w_2, ada_b_2, norm_g_2, w_in_2, q_norm_g_2,
    k_norm_g_2, idx_k_ln_g_2, idx_k_ln_b_2, conv_w_2, conv_b_2, dt_bias_2, a_log_2, d_skip_2,
    ssm_norm_g_2, w_branch_att_2, w_branch_ssm_2, w_out_2,
):
    x = first_block(
        x, c, w_ada, b_ada, g_pre_mix, g_post_mix, g_pre_ffn, g_post_ffn, w_in, b_gates,
        conv_qk, w_cmp_k, w_cmp_v, pos_cmp_k, pos_cmp_v, rel_bias, w_out, w_router, b_router,
        w_up, b_up, w_down, b_down,
    )
    return second_block(
        x, c_2, positions_2, ada_w_2, ada_b_2, norm_g_2, w_in_2, q_norm_g_2, k_norm_g_2,
        idx_k_ln_g_2, idx_k_ln_b_2, conv_w_2, conv_b_2, dt_bias_2, a_log_2, d_skip_2,
        ssm_norm_g_2, w_branch_att_2, w_branch_ssm_2, w_out_2,
    )


_drawn_inputs = setup_inputs


def setup_inputs(seed=0):
    import zlib

    import numpy as np

    out = dict(_drawn_inputs(seed))
    spreads = {}
    factors = {'g_post_ffn': 4.075,
     'pos_cmp_k': 200.0,
     'b_router': 4.311,
     'b_up': 8.0,
     'b_down': 8.0,
     'ada_b_2': 8.0,
     'q_norm_g_2': 8.0,
     'k_norm_g_2': 8.0,
     'idx_k_ln_g_2': 83.279,
     'idx_k_ln_b_2': 200.0,
     'conv_b_2': 8.0,
     'd_skip_2': 5.772,
     'ssm_norm_g_2': 3.676,
     'a_log_2': 29.384}
    for name, (base, spread) in spreads.items():
        noise = np.random.default_rng([zlib.crc32(name.encode()), seed]).standard_normal(out[name].shape)
        drawn = base * np.exp(spread * noise) if base else spread * noise
        out[name] = jnp.asarray(drawn.astype(out[name].dtype))
    for name, factor in factors.items():
        out[name] = (out[name] * factor).astype(out[name].dtype)
    return out
```

```python
import math
from contextlib import ExitStack, nullcontext

import numpy as np
import concourse.bass as bass
from concourse import mybir

F32 = mybir.dt.float32
F32R = mybir.dt.float32r
BF16 = mybir.dt.bfloat16
I32 = mybir.dt.int32
ALU = mybir.AluOpType
ACT = mybir.ActivationFunctionType
AX = mybir.AxisListType

P = 128
SEQ = 256
TT = SEQ // P
D = 1024
KT = D // P
EPS = 1e-6
NEG = -1e30

MH, MD = 4, 128
AH, AD = 8, 64
CMP_BLOCK, CMP_STRIDE = 32, 16
NCMP = (SEQ - CMP_BLOCK) // CMP_STRIDE + 1
NBUCKET, MAXDIST = 32, 128
NE, TOPK = 32, 4
DE = D
LIMIT, ALPHA = 7.0, 1.702

QH, KVH, HD = 8, 2, 128
IH, ID = 4, 64
KEEP = min(256, SEQ // 4)
ROT, IROT = HD // 4, ID // 4
THETA = 500000.0
SH, SP, SG, SN = 32, 64, 4, 128
DI = SH * SP
XBC = DI + 2 * SG * SN

SLOTS = 6
SLAB = KT * 512
RV = 3 * P - 1


def t5_bucket(dist):
    n = np.maximum(dist, 0)
    max_exact = NBUCKET // 2
    nf = np.maximum(n, 1).astype(np.float32)
    large = max_exact + (np.log(nf / np.float32(max_exact)) / np.float32(math.log(MAXDIST / max_exact))
                         * np.float32(NBUCKET - max_exact)).astype(np.int32)
    return np.where(n < max_exact, n, np.minimum(large, NBUCKET - 1))


C_ID, C_ONES, C_TRI, C_TRIS, C_ZERO, C_CM, C_CMT, C_IOTA = (i * P for i in range(8))
C_FREQ = 8 * P
C_NEGC = C_FREQ + ROT // 2 + IROT // 2
C_VALC = C_NEGC + TT * NCMP
C_SEL3 = C_VALC + TT * NCMP
C_LATER = C_SEL3 + NE
C_FLIP = C_LATER + P
C_W = C_FLIP + P
K_RV = 0
K_NEG = RV
K_CMP = 2 * RV
K_W = K_CMP + NCMP * SEQ


def shape_constants():
    c = np.zeros((P, C_W), np.float32)
    i, j = np.arange(P)[:, None], np.arange(P)[None, :]
    c[:, C_ID:C_ID + P] = i == j
    c[:, C_ONES:C_ONES + P] = 1
    c[:, C_TRI:C_TRI + P] = i <= j
    c[:, C_TRIS:C_TRIS + P] = i < j
    c[:, C_LATER:C_LATER + P] = i > j
    c[:, C_FLIP:C_FLIP + P] = i + j == P - 1
    c[:, C_CM:C_CM + P] = np.where(j <= i, 0, NEG)
    c[:, C_CMT:C_CMT + P] = np.where(i <= j, 0, NEG)
    c[:, C_IOTA:C_IOTA + P] = j
    for at, rot in ((C_FREQ, ROT), (C_FREQ + ROT // 2, IROT)):
        c[:, at:at + rot // 2] = np.power(np.float32(THETA), -(np.arange(0, rot, 2, dtype=np.float32) / np.float32(rot)))
    for t in range(TT):
        ok = CMP_STRIDE * np.arange(NCMP)[None, :] + CMP_BLOCK - 1 <= t * P + i
        c[:, C_NEGC + t * NCMP:C_NEGC + (t + 1) * NCMP] = np.where(ok, 0, NEG)
        c[:, C_VALC + t * NCMP:C_VALC + (t + 1) * NCMP] = ok
    c[:96, C_SEL3:C_SEL3 + NE] = np.arange(96)[:, None] % 32 == np.arange(NE)[None, :]
    k = np.zeros((NBUCKET, K_W), np.float32)
    dist = 2 * P - 1 - np.arange(RV)
    b = np.arange(NBUCKET)[:, None]
    k[:, K_RV:K_RV + RV] = (t5_bucket(dist)[None, :] == b) & (dist >= 0)[None, :]
    k[:, K_NEG:K_NEG + RV] = np.where(dist >= 0, 0, NEG)
    end = CMP_STRIDE * np.arange(NCMP) + CMP_BLOCK - 1
    d = np.arange(SEQ)[None, :] - end[:, None]
    k[:, K_CMP:] = (t5_bucket(d).reshape(-1)[None, :] == b)
    return c, k


R1 = {"c": (0, 8), "c_2": (8, 8), "g_pre_mix": (16, 8), "g_post_mix": (24, 8), "g_pre_ffn": (32, 8),
      "g_post_ffn": (40, 8), "norm_g_2": (48, 8), "ssm_norm_g_2": (56, 16), "conv_b_2": (72, 24)}
R2 = {"b_ada": (0, 48), "ada_b_2": (48, 24)}
R3 = {"conv_qk": (0, 32), "conv_w_2": (32, 96)}
COLS = {}
for base, rows in ((0, R1), (96, R2), (168, R3)):
    for name, (at, n) in rows.items():
        COLS[name] = (base + at, n)
NCOLS = 168 + 128

Z_Q, Z_K, Z_V, Z_O, Z_IF, Z_QA, Z_KC, Z_VC, Z_KS, Z_VS, Z_KW, Z_VW, Z_GA = (
    0, 512, 1024, 1536, 2048, 2056, 2568, 2696, 2824, 2952, 3080, 3208, 3336)
SLABS1 = [("w_ada", 0, [(0, 512 * n, 512)]) for n in range(4)]
SLABS1 += [("w_in", 0, [(0, z, 512)]) for z in (Z_Q, Z_K, Z_V, Z_O, Z_QA)]
SLABS1 += [("w_in", 0, [(0, Z_IF, 8), (8, Z_VS, 128), (136, Z_VW, 128), (264, Z_GA, 24)]),
           ("w_in", 0, [(0, Z_KC, 384), (384, Z_KW, 128)])]
SLABS1 += [("w_ada", 0, [(0, 512 * n, 512)]) for n in range(4, 12)]
SLABS1 += [("ada_w_2", 0, [(0, 512 * n, 512)]) for n in range(6)]
SLABS1 += [("w_out", 0, [(0, 512 * n, 512)]) for n in range(2)]
N_ADA, N_IN, N_MOD, N_OUT = 0, 4, 11, 25

P_Q, P_K, P_V, P_ZA, P_QI, P_KI, P_WI, P_ZS, P_XBC, P_DT, P_G = (
    0, 1024, 1280, 1536, 2560, 2816, 2880, 2884, 4932, 8004, 8036)
SLABS2 = [("w_in_2", 0, [(0, c, 512)]) for c in (P_Q, P_Q + 512, P_K)]
SLABS2 += [("w_in_2", 0, [(0, P_QI, 324), (324, P_DT, 32)])]
SLABS2 += [("w_in_2", 0, [(0, P_ZA + 512 * n, 512)]) for n in range(2)]
SLABS2 += [("w_in_2", 0, [(0, P_XBC + 512 * n, 512)]) for n in range(6)]
SLABS2 += [("w_in_2", 0, [(0, P_ZS + 512 * n, 512)]) for n in range(4)]
SLABS2 += [("w_branch_ssm_2", D * k, [(0, 512 * n, 512)]) for n in range(2) for k in range(2)]
SLABS2 += [("w_in_2", 0, [(0, P_G + D + 512 * n, 512)]) for n in range(2)]
SLABS2 += [("w_branch_att_2", 0, [(0, 512 * n, 512)]) for n in range(2)]
SLABS2 += [("w_in_2", 0, [(0, P_G + 512 * n, 512)]) for n in range(2)]
SLABS2 += [("w_out_2", 0, [(0, 512 * n, 512)]) for n in range(2)]
M_ZA, M_XBC, M_ZS, M_SSM, M_GS, M_ATT, M_GA, M_OUT = 4, 6, 12, 16, 20, 22, 24, 26
BC = {"q_norm_g_2": (0, HD), "k_norm_g_2": (HD, HD), "idx_k_ln_g_2": (2 * HD, ID), "idx_k_ln_b_2": (2 * HD + ID, ID),
      "dt_bias_2": (2 * HD + 2 * ID, SH), "a_log_2": (2 * HD + 2 * ID + SH, SH), "d_skip_2": (2 * HD + 2 * ID + 2 * SH, SH)}
TWO_PI_HIGH = 6.28125
TWO_PI_LOW = 2 * math.pi - TWO_PI_HIGH
ROUNDER = 1.5 * 2 ** 23


class Steps:

    def __init__(self, order):
        self.order = order
        self.n = 0
        self.counts = {}

    def link(self, eng, ins):
        self.n += 1
        ins.then_inc(self.order, 1)
        eng.wait_ge(self.order, self.n)

    def done(self, eng, ins, sem):
        n = self.counts.get(sem.name, 0) + 1
        self.counts[sem.name] = n
        ins.then_inc(sem, 1)
        eng.wait_ge(sem, n)


def two_layers(nc, A, cst_in, c32_in, out):
    with ExitStack() as ctx:
        sems = {}

        def sb(name, shape, dt=F32, at=ctx):
            return at.enter_context(nc.sbuf_tensor(name, shape, dt))

        def sm(name):
            if name not in sems:
                sems[name] = nc.alloc_semaphore(name)
            return sems[name]

        def retire(names):
            nc.clear_and_free_semaphores([sems.pop(name) for name in names.split()])
            nc.all_engine_barrier()

        ps = ctx.enter_context(nc.psum_tensor("ps", [P, 8, 512], F32))
        cst = sb("cst", [P, C_W])
        cols = sb("cols", [P, NCOLS])
        ring_low = sb("ring_low", [P, 2, KT, 512])
        xT = sb("xT", [P, KT, SEQ])
        hT = sb("hT", [P, KT, SEQ])
        rstd = sb("rstd", [P, SEQ])
        mod = sb("mod", [P, 48])
        mod2 = sb("mod2", [P, 24])
        silc = sb("silc", [P, 2, KT])
        gain = sb("gain", [P, KT])
        mrow = sb("mrow", [P, 512])
        mrows = sb("mrows", [56, P])
        idn = cst[:, C_ID:C_ID + P]
        ones = cst[:, C_ONES:C_ONES + P]
        slots = [ring_low[:, i] for i in range(2)]

        def more_slots(name):
            stack = ctx.enter_context(ExitStack())
            ring_high = sb(name, [P, SLOTS - 2, KT, 512], at=stack)
            slots[2:] = [ring_high[:, i] for i in range(SLOTS - 2)]
            return stack

        first_ring = more_slots("first_ring")
        rv_dram = nc.dram_tensor("rv_dram", (AH, RV), F32).ap()

        V = Steps(sm("dve_order"))
        S = Steps(sm("act_order"))
        G = Steps(sm("pool_order"))

        def col(name, k):
            at, _ = COLS[name]
            return cols[:, at + k:at + k + 1]

        def colv(name):
            at, n = COLS[name]
            return cols[:, at:at + n]

        def load_slab(sp, n, spec, stream=""):
            slot = n % SLOTS
            if n >= SLOTS:
                sp.wait_ge(sm(f"{stream}slab_used"), n - SLOTS + 1)
            name, row, parts = spec
            for at, c0, w in parts:
                src = A[name][row:row + D, c0:c0 + w].rearrange("(k p) n -> p k n", p=P)
                sp.dma_start(slots[slot][:, :, at:at + w], src).then_inc(sm(f"{stream}slab_ready{slot}"), 16)

        def slab_count(specs, n):
            return 16 * sum(len(specs[m][2]) for m in range(n % SLOTS, n + 1, SLOTS))

        def tokens_by_columns(pe, n, w, bank):
            for t in range(TT):
                for k in range(KT):
                    mm = pe.matmul(ps[:, bank + t, 0:w], hT[:, k, t * P:(t + 1) * P], slots[n % SLOTS][:, k, 0:w],
                                   start=(k == 0), stop=(k == KT - 1))
            return mm

        def columns_by_tokens(pe, n, bank, src=None, first=True, last=True):
            src = hT if src is None else src
            for j in range(4):
                for k in range(KT):
                    mm = pe.matmul(ps[:, bank + j // 2, (j % 2) * SEQ:(j % 2 + 1) * SEQ],
                                   slots[n % SLOTS][:, k, j * P:(j + 1) * P], src[:, k, :],
                                   start=(first and k == 0), stop=(last and k == KT - 1), skip_group_check=not (first and last))
            return mm

        def mod_row(pe, n, which, m, bank):
            q = 32 * (m % 4)
            for k in range(KT):
                mm = pe.matmul(ps[q:q + 1, bank, :], silc[:, which, k:k + 1], slots[n % SLOTS][:, k, :],
                               start=(k == 0), stop=(k == KT - 1))
            mm.then_inc(sm("slab_used"), 1)

        def mod_row_copy(act, n, m, bank):
            q = 32 * (m % 4)
            act.wait_ge(sm("slab_used"), n + 1)
            if m >= 4:
                act.wait_ge(sm(f"mod_rows_in{m % 4}"), 16 * (m // 4))
            S.done(act, act.activation(mrow[q:q + 1, :], ps[q:q + 1, bank, :], ACT.Copy), sm("mod_row_ready"))

        def mod_row_send(sp, m, at):
            sp.wait_ge(sm("mod_row_ready"), m + 1)
            q = 32 * (m % 4)
            sp.dma_start(mrows[at:at + 4, :], mrow[q:q + 1, :].rearrange("a (j p) -> a j p", p=P))\
                .then_inc(sm(f"mod_rows_in{m % 4}"), 16)

        def bank2(b, shape="a"):
            return ps[:, b:b + 2, :].rearrange("p b n -> p (b n)")

        def norm_squares(act, src, sq, signal):
            S.done(act, act.activation(sq, src, ACT.Square), sm(signal))

        def norm_sums(pe, sq, bank, signal, after):
            pe.wait_ge(*after)
            for k in range(KT):
                mm = pe.matmul(ps[:, bank, 0:SEQ], ones, sq[:, k, :], start=(k == 0), stop=(k == KT - 1))
            mm.then_inc(sm(signal), 1)

        def norm_rstd(dve, bank, after):
            dve.wait_ge(*after)
            V.done(dve, dve.tensor_scalar(rstd[:], ps[:, bank, 0:SEQ], 1.0 / D, EPS, ALU.mult, ALU.add), sm("mean_square"))
            dve.wait_ge(sm("rms_ready"), V.counts["mean_square"])
            V.link(dve, dve.reciprocal(rstd[:], rstd[:]))

        def norm_root(act, nth):
            act.wait_ge(sm("mean_square"), nth)
            S.done(act, act.activation(rstd[:], rstd[:], ACT.Sqrt), sm("rms_ready"))

        with ExitStack() as pa:
            att = ctx.enter_context(ExitStack())
            TB = sb("TB", [P, AH, SEQ], at=att)
            cbias = sb("cbias", [P, TT, AH, NCMP], at=att)
            rows1 = sb("rows1", [96, P], at=pa)
            rows2 = sb("rows2", [72, P], at=pa)
            rows3 = sb("rows3", [128, P], at=pa)
            xtok = sb("xtok", [P, TT, D], at=pa)
            c32 = sb("c32", [NBUCKET, K_W], at=pa)
            relb = sb("relb", [NBUCKET, AH], at=pa)
            rv = sb("rv", [AH, RV], at=pa)
            sq = sb("sq", [P, KT, SEQ], at=pa)
            tbr = sb("tbr", [P, AH, SEQ], at=pa)

            with nc.Block() as block:
                @block.sync
                def _(sp):
                    for rows, where, name in ((rows1, R1, "rows1_in"), (rows2, R2, "rows2_in"), (rows3, R3, "rows3_in")):
                        for vec, (at, n) in where.items():
                            sp.dma_start(rows[at:at + n, :], A[vec]).then_inc(sm("rows_in"), 16)
                    sp.dma_start(xtok[:], A["x"].rearrange("(t p) d -> p t d", p=P)).then_inc(sm("x_in"), 16)
                    for n in range(SLOTS):
                        load_slab(sp, n, SLABS1[n])
                    sp.wait_ge(sm("rv_ready"), 1)
                    sp.dma_start(rv_dram, rv[:]).then_inc(sm("rv_stored"), 16)
                    sp.wait_ge(sm("rv_stored"), 16)
                    for par in range(2):
                        src = bass.AP(rv_dram.tensor, rv_dram.offset + par * RV, [[1, P], [2 * RV, AH // 2], [1, SEQ]])
                        sp.dma_start(tbr[:, par * 4:par * 4 + 4, :], src).then_inc(sm("tb_in"), 16)
                    for n in range(4):
                        load_slab(sp, SLOTS + n, SLABS1[SLOTS + n])
                        mod_row_send(sp, n, 4 * n)

                @block.scalar
                def _(act):
                    act.dma_start(cst[:], cst_in).then_inc(sm("cst_in"), 16)
                    act.dma_start(relb[:], A["rel_bias"]).then_inc(sm("c32_in"), 16)
                    act.dma_start(c32[:], c32_in).then_inc(sm("c32_in"), 16)
                    act.wait_ge(sm("cols_ready"), 1)
                    S.done(act, act.activation(silc[:].rearrange("p a k -> p (a k)"), cols[:, 0:16], ACT.Exp, scale=-1.0),
                           sm("c_exp"))
                    act.wait_ge(sm("x_ready"), 2)
                    norm_squares(act, xT[:].rearrange("p k t -> p (k t)"),
                                 sq[:].rearrange("p k t -> p (k t)"), "sq_ready")
                    for n in range(4):
                        mod_row_copy(act, n, n, 5)
                    norm_root(act, 1)
                    for k in range(KT):
                        act.wait_ge(sm("h_scaled"), k + 1)
                        ins = act.activation(hT[:, k, :], hT[:, k, :], ACT.Identity, bias=mod[:, k:k + 1])
                        ins.then_inc(sm("h_ready"), 1)
                    act.wait_ge(sm("tb_flipped"), 1)
                    act.activation(TB[:].rearrange("p s n -> p (s n)"), ps[:, 0:4, :].rearrange("p b n -> p (b n)"), ACT.Copy)\
                        .then_inc(sm("tb_ready"), 1)

                @block.tensor
                def _(pe):
                    pe.wait_ge(sm("cst_in"), 16)
                    pe.wait_ge(sm("rows_in"), 16 * (len(R1) + len(R2) + len(R3)))
                    for rows, n, at in ((rows1, 96, 0), (rows2, 72, 96), (rows3, 128, 168)):
                        mm = pe.transpose(ps[:, 4, at:at + n], rows[:, :], cst[0:n, C_ID:C_ID + n])
                    mm.then_inc(sm("rows_turned"), 1)
                    pe.wait_ge(sm("x_in"), 16)
                    for k in range(KT):
                        for t in range(TT):
                            mm = pe.transpose(ps[:, k // 2, (k % 2) * SEQ + t * P:(k % 2) * SEQ + (t + 1) * P],
                                              xtok[:, t, k * P:(k + 1) * P], idn)
                        if k % 4 == 3:
                            mm.then_inc(sm("x_turned"), 1)
                    pe.wait_ge(sm("c32_in"), 32)
                    pe.matmul(ps[0:AH, 6, 0:RV], relb[:], c32[:, K_RV:K_RV + RV], start=True, stop=True)\
                        .then_inc(sm("rv_summed"), 1)
                    for t in range(TT):
                        for i in range(NCMP):
                            at = (t * NCMP + i) * AH
                            mm = pe.matmul(ps[:, 7, at:at + AH], c32[:, K_CMP + i * SEQ + t * P:K_CMP + i * SEQ + (t + 1) * P],
                                           relb[:], start=True, stop=True)
                    mm.then_inc(sm("cbias_summed"), 1)
                    pe.wait_ge(sm("silc_ready"), 1)
                    for n in range(4):
                        pe.wait_ge(sm(f"slab_ready{n % SLOTS}"), slab_count(SLABS1, n))
                        mod_row(pe, n, 0, n, 5)
                    for q in range(4):
                        pe.wait_ge(sm(f"mod_rows_in{q}"), 16)
                    pe.transpose(ps[:, 4, 0:16], mrows[0:16, :], cst[0:16, C_ID:C_ID + 16]).then_inc(sm("mod_turned"), 1)
                    pe.wait_ge(sm("rv_ready"), 1)
                    norm_sums(pe, sq, 6, "x_summed", (sm("sq_ready"), 1))
                    pe.wait_ge(sm("x_ready"), 2)
                    pe.wait_ge(sm("tb_in"), 32)
                    for sl in range(AH):
                        mm = pe.matmul(ps[:, sl // 2, (sl % 2) * SEQ:(sl % 2 + 1) * SEQ], cst[:, C_FLIP:C_FLIP + P],
                                       tbr[:, sl, :], start=True, stop=True)
                    mm.then_inc(sm("tb_flipped"), 1)

                @block.vector
                def _(dve):
                    dve.wait_ge(sm("rows_turned"), 1)
                    V.done(dve, dve.tensor_copy(cols[:], ps[:, 4, 0:NCOLS]), sm("cols_ready"))
                    for h in range(2):
                        dve.wait_ge(sm("x_turned"), h + 1)
                        V.done(dve, dve.tensor_copy(xT[:, 4 * h:4 * h + 4, :].rearrange("p k t -> p (k t)"),
                                                    bank2(2 * h)), sm("x_ready"))
                    flat = silc[:].rearrange("p a k -> p (a k)")
                    dve.wait_ge(sm("c_exp"), 1)
                    V.link(dve, dve.tensor_scalar(flat, flat, 1.0, None, ALU.add))
                    V.link(dve, dve.reciprocal(flat, flat))
                    V.done(dve, dve.tensor_tensor(flat, flat, cols[:, 0:16], ALU.mult), sm("silc_ready"))
                    dve.wait_ge(sm("rv_summed"), 1)
                    V.done(dve, dve.tensor_tensor(rv[:], ps[0:AH, 6, 0:RV], c32[0:AH, K_NEG:K_NEG + RV], ALU.add),
                           sm("rv_ready"))
                    dve.wait_ge(sm("cbias_summed"), 1)
                    for t in range(TT):
                        src = ps[:, 7, t * NCMP * AH:(t + 1) * NCMP * AH].rearrange("p (i hh par) -> p par hh i", hh=4, par=2)
                        neg = cst[:, C_NEGC + t * NCMP:C_NEGC + (t + 1) * NCMP]
                        for par in range(2):
                            V.link(dve, dve.tensor_tensor(cbias[:, t, 4 * par:4 * par + 4, :], src[:, par],
                                                          neg.unsqueeze(1).to_broadcast([P, 4, NCMP]), ALU.add))
                    dve.wait_ge(sm("mod_turned"), 1)
                    V.link(dve, dve.tensor_tensor(mod[:, 0:16], ps[:, 4, 0:16], colv("b_ada")[:, 0:16], ALU.add))
                    V.link(dve, dve.scalar_tensor_tensor(gain[:], mod[:, 8:16], 1.0, colv("g_pre_mix"), ALU.add, ALU.mult))
                    norm_rstd(dve, 6, (sm("x_summed"), 1))
                    for k in range(KT):
                        dve.scalar_tensor_tensor(hT[:, k, :], xT[:, k, :], gain[:, k:k + 1], rstd[:], ALU.mult, ALU.mult)\
                            .then_inc(sm("h_scaled"), 1)

        qkT = sb("qkT", [P, 2 * MH, SEQ], at=att)
        vm = sb("vm", [P, TT, MH * MD], at=att)
        oT = sb("oT", [P, MH, SEQ], at=att)
        qaT = sb("qaT", [P, AH // 2, SEQ], at=att)
        tokz = sb("tokz", [P, TT, 288], at=att)
        kc4 = sb("kc4", [P, 4, SEQ], at=att)
        wck = sb("wck", [P, CMP_BLOCK, 2 * AD], at=att)
        wcv = sb("wcv", [P, CMP_BLOCK, AD], at=att)
        posT = sb("posT", [P, 2, CMP_BLOCK], at=att)
        bgate = sb("bgate", [P, 8], at=att)
        with ExitStack() as pb:
            zc = sb("zc", [P, 4, SEQ + 3], at=pb)
            cv = sb("cv", [P, 4, SEQ], at=pb)

            with nc.Block() as block:
                @block.sync
                def _(sp):
                    for n in range(SLOTS + 4, SLOTS + N_MOD):
                        load_slab(sp, n, SLABS1[n])

                @block.scalar
                def _(act):
                    act.dma_start(bgate[:], bass.AP(A["b_gates"].tensor, 0, [[0, P], [1, 8]])).then_inc(sm("small_in"), 16)
                    for half in range(2):
                        at = slice(64 * half, 64 * half + 64)
                        for twice in range(2):
                            act.dma_start(wck[at, :, 64 * twice:64 * twice + 64],
                                          A["w_cmp_k"].rearrange("l d e -> d l e")).then_inc(sm("small_in"), 16)
                        act.dma_start(wcv[at, :, :], A["w_cmp_v"].rearrange("l d e -> d l e")).then_inc(sm("small_in"), 16)
                        with nc.allow_non_contiguous_dma("64 x 32 position embedding"):
                            for kind, name in enumerate(("pos_cmp_k", "pos_cmp_v")):
                                act.dma_start(posT[at, kind, :], A[name].rearrange("l d -> d l"))\
                                    .then_inc(sm("small_in"), 16)
                    for m in range(2):
                        act.wait_ge(sm("conv_ready"), m + 1)
                        ins = act.activation(qkT[:, 4 * m:4 * m + 4, :], cv[:], ACT.Silu)
                        S.done(act, ins, sm("qk_ready"))
                    act.wait_ge(sm("z_copied"), 7)
                    S.link(act, act.activation(oT[:], oT[:], ACT.Sigmoid))
                    S.link(act, act.activation(tokz[:, :, 264:288], tokz[:, :, 264:288], ACT.Sigmoid))
                    act.wait_ge(sm("small_in"), 16 * 11)

                @block.tensor
                def _(pe):
                    for n in range(N_IN, N_MOD):
                        pe.wait_ge(sm(f"slab_ready{n % SLOTS}"), slab_count(SLABS1, n))
                        bank = 2 * (n % 4)
                        if n >= N_IN + 4:
                            pe.wait_ge(sm("z_copied"), n - N_IN - 3)
                        name = n - N_IN
                        if name in (2, 5):
                            mm = tokens_by_columns(pe, n, 512 if name == 2 else 288, bank)
                        else:
                            mm = columns_by_tokens(pe, n, bank)
                        mm.then_inc(sm("slab_used"), 1)

                @block.vector
                def _(dve):
                    V.link(dve, dve.memset(zc[:, :, 0:3], 0.0))
                    for name in range(7):
                        n = N_IN + name
                        bank = 2 * (n % 4)
                        dve.wait_ge(sm("slab_used"), n + 1)
                        tiles = bank2(bank).rearrange("p (j t) -> p j t", j=4)
                        if name < 2:
                            V.done(dve, dve.tensor_copy(zc[:, :, 3:], tiles), sm("z_copied"))
                            if name == 1:
                                dve.wait_ge(sm("qk_ready"), 1)
                            for j in range(4):
                                V.link(dve, dve.tensor_scalar(cv[:, j, :], zc[:, j, 0:SEQ], col("conv_qk", 4 * name + j),
                                                              None, ALU.mult))
                                for tap in range(1, 4):
                                    ins = dve.scalar_tensor_tensor(cv[:, j, :], zc[:, j, tap:tap + SEQ],
                                                                   col("conv_qk", 8 * tap + 4 * name + j), cv[:, j, :],
                                                                   ALU.mult, ALU.add)
                                    if j == 3 and tap == 3:
                                        V.done(dve, ins, sm("conv_ready"))
                                    else:
                                        V.link(dve, ins)
                        elif name == 5:
                            V.done(dve, dve.tensor_copy(tokz[:], ps[:, bank:bank + 2, 0:288]), sm("z_copied"))
                        else:
                            dst = {2: vm[:].rearrange("p t n -> p (t n)").rearrange("p (j t) -> p j t", j=4),
                                   3: oT[:], 4: qaT[:], 6: kc4[:]}[name]
                            V.done(dve, dve.tensor_copy(dst, tiles), sm("z_copied"))

        mix = hT
        with ExitStack() as pc:
            gt = sb("gt", [P, TT, 8], at=pc)
            lf = sb("lf", [P, TT, MH], at=pc)
            nab = sb("nab", [P, TT, MH], at=pc)
            F = sb("F", [P, TT, MH], at=pc)
            aa = sb("aa", [P, TT, MH], at=pc)
            nM = sb("nM", [P, TT, MH], at=pc)
            em = sb("em", [P, TT, MH], at=pc)
            den = sb("den", [P, TT, MH], at=pc)
            L1 = sb("L1", [P, AH, SEQ], at=pc)[:]
            LM1 = L1[:, 0:MH, :]
            LM0 = sb("LM0", [P, MH, P], at=pc)
            WT0 = L1[:, MH:, :]
            WT1 = sb("WT1", [P, MH, P], at=pc)
            kin = sb("kin", [P, 2, CMP_BLOCK, NCMP], at=pc)
            kcm = sb("kcm", [P, 2, NCMP], at=pc)
            vcm = sb("vcm", [NCMP, 2, AD], at=pc)
            ksw = sb("ksw", [P, 2, SEQ], at=pc)
            Lc = sb("Lc", [P, TT, AH, NCMP], at=pc)
            nmax = sb("nmax", [P, 5, TT, AH], at=pc)
            esum = sb("esum", [P, 5, TT, AH], at=pc)
            L0 = vm[:].rearrange("p t n -> p (t n)").rearrange("p (s n) -> p s n", s=AH)
            PT0 = wck[:].rearrange("p l e -> p (l e)").rearrange("p (b s t) -> p b s t", b=2, s=AH)
            PT1 = wcv[:].rearrange("p l e -> p (l e)").rearrange("p (b s t) -> p b s t", b=2, s=AH)
            PcT = qkT[0:NCMP]
            SLOTLIST = [(par, hh) for par in range(2) for hh in range(4)]
            UNITS = [(b, t) for b in range(2) for t in (1, 0)]
            ROUNDS = [("c", 0, t, 0, q) for t in range(TT) for q in range(2)]
            UNIT_ROUNDS = {(b, t): [("p", b, t, s, q) for s in range(t + 1) for q in range(2)] for b, t in UNITS}
            for u in UNITS:
                ROUNDS += UNIT_ROUNDS[u]
            MODS = list(range(N_MOD, N_OUT))

            def gate_of(c, t):
                return tokz[:, t, 264:288].rearrange("p (hh par c) -> p c par hh", hh=4, par=2)[:, c]

            with nc.Block() as block:
                @block.sync
                def _(sp):
                    sp.wait_ge(sm("z_copied"), 7)
                    for b in range(2):
                        for half in range(2):
                            sp.dma_start(ksw[64 * half:64 * half + 64, b, :],
                                         kc4[64 - 64 * half:128 - 64 * half, 2 + b, :]).then_inc(sm("ksw_in"), 16)
                    for m in range(4, 18):
                        n = SLOTS + N_MOD + m - 4
                        if n < len(SLABS1):
                            load_slab(sp, n, SLABS1[n])
                        mod_row_send(sp, m, 4 * (m - 4))

                @block.scalar
                def _(act):
                    copied = [4]

                    def mod_copies(k):
                        for _ in range(k):
                            mod_row_copy(act, N_MOD + copied[0] - 4, copied[0], 3)
                            copied[0] += 1

                    act.wait_ge(sm("nab_ready"), 1)
                    S.link(act, act.activation(nab[:], nab[:], ACT.Exp))
                    S.done(act, act.activation(nab[:], nab[:], ACT.Ln, bias=1.0), sm("ln_ready"))
                    act.wait_ge(sm("running_max"), 1)
                    for h in range(MH):
                        act.activation(LM1[:, h, :], LM1[:, h, :], ACT.Exp, bias=nM[:, 1, h:h + 1])
                        ins = act.activation(LM0[:, h, :], LM0[:, h, :], ACT.Exp, bias=nM[:, 0, h:h + 1])
                    S.done(act, ins, sm("decay_ready"))
                    act.wait_ge(sm("em_in"), 1)
                    S.done(act, act.activation(em[:], em[:], ACT.Exp, scale=-1.0), sm("em_ready"))
                    mod_copies(3)
                    act.wait_ge(sm("w_turned"), 1)
                    S.link(act, act.activation(WT0.rearrange("p h t -> p (h t)"), bank2(4), ACT.Copy))
                    S.done(act, act.activation(WT1[:].rearrange("p h t -> p (h t)"), ps[:, 2, :], ACT.Copy), sm("wt_ready"))
                    act.wait_ge(sm("lc_ready"), 1)
                    S.done(act, act.activation(Lc[:], Lc[:], ACT.Exp), sm("ec_ready"))
                    mod_copies(1)
                    nround = 0

                    def copy_rounds(rounds):
                        nonlocal nround
                        for what, b, t, s, q in rounds:
                            nround += 1
                            act.wait_ge(sm("p_turned"), nround)
                            sl, tk = slice(4 * q, 4 * q + 4), slice(t * P, (t + 1) * P)
                            if what == "c":
                                dst, src = PcT[:, sl, tk], ps[0:NCMP, 2, :]
                            else:
                                dst = PT0[:, b, sl, tk] if s == 0 else PT1[:, b, sl, :]
                                src = ps[:, 2, :]
                            S.done(act, act.activation(dst, src.rearrange("p (q t) -> p q t", q=4), ACT.Copy),
                                   sm("pt_ready"))

                    copy_rounds(ROUNDS[:4])
                    for u, (b, t) in enumerate(UNITS):
                        act.wait_ge(sm("logits_ready"), u + 1)
                        L = L1 if t else L0
                        for sl in range(AH):
                            ins = act.activation(L[:, sl, :], L[:, sl, :], ACT.Exp, bias=nmax[:, b, t, sl:sl + 1],
                                                 accum_out=esum[:, b, t, sl:sl + 1])
                        S.done(act, ins, sm("exp_ready"))
                        if u >= 1:
                            copy_rounds(UNIT_ROUNDS[UNITS[u - 1]])
                        mod_copies(2)
                    copy_rounds(UNIT_ROUNDS[UNITS[-1]])
                    mod_copies(2)

                @block.tensor
                def _(pe):
                    def mods(k):
                        for _ in range(k):
                            n = MODS.pop(0)
                            pe.wait_ge(sm(f"slab_ready{n % SLOTS}"), slab_count(SLABS1, n))
                            m = n - N_MOD + 4
                            if m >= 8:
                                pe.wait_ge(sm("mod_row_ready"), m - 3)
                            mod_row(pe, n, 0 if m < 12 else 1, m, 3)

                    for t in (1, 0):
                        w = (t + 1) * P
                        for h in range(MH):
                            dst = ps[:, h // 2, (h % 2) * w:(h % 2) * w + w] if t else ps[:, 2, h * w:h * w + w]
                            mm = pe.matmul(dst, qkT[:, h, t * P:(t + 1) * P], qkT[:, MH + h, 0:w], start=True, stop=True)
                    mm.then_inc(sm("qk_scored"), 1)
                    pe.wait_ge(sm("lf_ready"), 1)
                    tri = cst[:, C_TRI:C_TRI + P]
                    pe.matmul(ps[:, 3, 0:MH], tri, lf[:, 0, :], start=True, stop=True)
                    pe.matmul(ps[:, 3, MH:2 * MH], ones, lf[:, 0, :], start=True, stop=False)
                    pe.matmul(ps[:, 3, MH:2 * MH], tri, lf[:, 1, :], start=False, stop=True).then_inc(sm("f_summed"), 1)
                    pe.wait_ge(sm("kin_ready"), 2)
                    for g in range(2):
                        half = slice(64 * g, 64 * g + 64)
                        for l in range(CMP_BLOCK):
                            pe.matmul(ps[:, 6 + g, 0:NCMP], wck[half, l, :], kin[half, 0, l, :],
                                      start=(l == 0), stop=(l == CMP_BLOCK - 1))
                        for l in range(CMP_BLOCK):
                            mm = pe.matmul(ps[0:NCMP, 6 + g, 64:64 + AD], kin[half, 1, l, :], wcv[half, l, :],
                                           start=(l == 0), stop=(l == CMP_BLOCK - 1))
                    mm.then_inc(sm("compressed"), 1)
                    pe.wait_ge(sm("a_ready"), 1)
                    for h in range(MH):
                        for t in range(TT):
                            mm = pe.matmul(ps[:, 4 + h // 2, (h % 2) * SEQ + t * P:(h % 2) * SEQ + (t + 1) * P],
                                           aa[:, t, h:h + 1].to_broadcast([P, P]), idn, start=True, stop=True)
                    mm.then_inc(sm("a_spread"), 1)
                    pe.wait_ge(sm("kcm_ready"), 1)
                    for par, hh in SLOTLIST:
                        half = slice(64 * par, 64 * par + 64)
                        for t in range(TT):
                            at = (t * 4 + hh) * NCMP
                            mm = pe.matmul(ps[:, 6 + par, at:at + NCMP], qaT[half, hh, t * P:(t + 1) * P],
                                           kcm[half, hh // 2, :], start=True, stop=True)
                    mm.then_inc(sm("c_scored"), 1)
                    mods(3)
                    pe.wait_ge(sm("w_ready"), 2)
                    for h in range(MH):
                        at = (h % 2) * SEQ
                        pe.transpose(ps[:, 4 + h // 2, at:at + P], LM0[:, h, :], idn)
                        pe.transpose(ps[:, 4 + h // 2, at + P:at + SEQ], LM1[:, h, 0:P], idn)
                        mm = pe.transpose(ps[:, 2, h * P:(h + 1) * P], LM1[:, h, P:SEQ], idn)
                    mm.then_inc(sm("w_turned"), 1)
                    mods(1)
                    pe.wait_ge(sm("wt_ready"), 1)
                    for h in range(MH):
                        out_h = ps[:, h // 2, (h % 2) * SEQ:(h % 2 + 1) * SEQ]
                        pe.matmul(out_h, vm[:, 0, h * MD:(h + 1) * MD], WT0[:, h, :], start=True, stop=False)
                        mm = pe.matmul(out_h[:, P:SEQ], vm[:, 1, h * MD:(h + 1) * MD], WT1[:, h, :], start=False, stop=True)
                    mm.then_inc(sm("m_out"), 1)

                    nround = 0

                    def turn(rounds):
                        nonlocal nround
                        for what, b, t, s, q in rounds:
                            if nround:
                                pe.wait_ge(sm("pt_ready"), nround)
                            nround += 1
                            for i in range(4):
                                sl = 4 * q + i
                                if what == "c":
                                    mm = pe.transpose(ps[0:NCMP, 2, i * P:(i + 1) * P], Lc[:, t, sl, :], idn)
                                else:
                                    L = L1 if t else L0
                                    mm = pe.transpose(ps[:, 2, i * P:(i + 1) * P], L[:, sl, s * P:(s + 1) * P], idn)
                            mm.then_inc(sm("p_turned"), 1)

                    def scores(u):
                        b, t = UNITS[u]
                        w = (t + 1) * P
                        if u == 0:
                            pe.wait_ge(sm("ksw_in"), 64)
                            pe.wait_ge(sm("wt_ready"), 1)
                            pe.wait_ge(sm("c_copied"), 1)
                        if u == 1:
                            pe.wait_ge(sm("m_done"), 1)
                        if u >= 2:
                            pe.wait_ge(sm("logits_ready"), u - 1)
                        for sl, (par, hh) in enumerate(SLOTLIST):
                            half = slice(64 * par, 64 * par + 64)
                            k = kc4[half, 2 + b, 0:w] if hh // 2 == par else ksw[half, b, 0:w]
                            at = sl * w
                            dst = ps[:, (4 if t else 0) + at // 512, at % 512:at % 512 + w]
                            mm = pe.matmul(dst, qaT[half, hh, t * P:(t + 1) * P], k, start=True, stop=True)
                        mm.then_inc(sm("scored"), 1)

                    scores(0)
                    scores(1)
                    pe.wait_ge(sm("pc_ready"), 1)
                    turn(ROUNDS[:4])
                    for u in range(4):
                        mods(2)
                        if u + 2 < 4:
                            scores(u + 2)
                        pe.wait_ge(sm("probs_ready"), u + 1)
                        turn(UNIT_ROUNDS[UNITS[u]])
                    mods(2)
                    for q in range(4):
                        pe.wait_ge(sm(f"mod_rows_in{q}"), 16 * len(range(q, 18, 4)))
                    pe.transpose(ps[:, 6, 0:56], mrows[:], cst[0:56, C_ID:C_ID + 56]).then_inc(sm("mod_turned"), 1)
                    pe.wait_ge(sm("pt_ready"), len(ROUNDS))
                    for sl, (par, hh) in enumerate(SLOTLIST):
                        half = slice(64 * par, 64 * par + 64)
                        out_h = ps[half, hh // 2, (hh % 2) * SEQ:(hh % 2 + 1) * SEQ]
                        g = hh // 2
                        for b in range(2):
                            v0 = 8 + 128 * b + AD * g
                            pe.matmul(out_h, tokz[:, 0, v0:v0 + AD], PT0[:, b, sl, :], start=(b == 0), stop=False)
                            pe.matmul(out_h[:, P:SEQ], tokz[:, 1, v0:v0 + AD], PT1[:, b, sl, :], start=False, stop=False)
                        mm = pe.matmul(out_h, vcm[:, g, :], PcT[:, sl, :], start=False, stop=True)
                    mm.then_inc(sm("a_out"), 1)

                @block.vector
                def _(dve):
                    f = gt[:, :, MH:8]
                    V.link(dve, dve.tensor_tensor(gt[:], tokz[:, :, 0:8], bgate[:].unsqueeze(1).to_broadcast([P, TT, 8]),
                                                  ALU.add))
                    V.done(dve, dve.scalar_tensor_tensor(nab[:], f, -1.0, f, ALU.mult, ALU.min), sm("nab_ready"))
                    for kind in range(2):
                        src = kc4[:, kind, :]
                        windows = bass.AP(src.tensor, src.offset, [list(src.ap[0]), [1, CMP_BLOCK], [CMP_STRIDE, NCMP]])
                        V.done(dve, dve.tensor_tensor(kin[:, kind], windows, posT[:, kind, :].unsqueeze(2)
                                                      .to_broadcast([P, CMP_BLOCK, NCMP]), ALU.add), sm("kin_ready"))
                    dve.wait_ge(sm("ln_ready"), 1)
                    V.done(dve, dve.scalar_tensor_tensor(lf[:], f, 0.0, nab[:], ALU.min, ALU.subtract), sm("lf_ready"))
                    dve.wait_ge(sm("f_summed"), 1)
                    Ff = F[:].rearrange("p t h -> p (t h)")
                    V.link(dve, dve.tensor_copy(Ff, ps[:, 3, 0:2 * MH]))
                    V.done(dve, dve.tensor_tensor(aa[:], gt[:, :, 0:MH], F[:], ALU.subtract), sm("a_ready"))
                    dve.wait_ge(sm("compressed"), 1)
                    for g in range(2):
                        V.link(dve, dve.tensor_copy(kcm[:, g, :], ps[:, 6 + g, 0:NCMP]))
                        ins = dve.tensor_copy(vcm[:, g, :], ps[0:NCMP, 6 + g, 64:64 + AD])
                        (V.done(dve, ins, sm("kcm_ready")) if g else V.link(dve, ins))
                    dve.wait_ge(sm("a_spread"), 1)
                    spread = bank2(4).rearrange("p (h s) -> p h s", h=MH)
                    V.link(dve, dve.tensor_tensor(LM1, spread, cst[:, C_ZERO:C_ZERO + SEQ].unsqueeze(1)
                                                  .to_broadcast([P, MH, SEQ]), ALU.add))
                    V.link(dve, dve.tensor_tensor(LM0[:], spread[:, :, 0:P], cst[:, C_CM:C_CM + P].unsqueeze(1)
                                                  .to_broadcast([P, MH, P]), ALU.add))
                    V.link(dve, dve.tensor_reduce(nM[:, 1, :], LM1, AX.X, ALU.max, negate=True))
                    V.done(dve, dve.tensor_reduce(nM[:, 0, :], LM0[:], AX.X, ALU.max, negate=True), sm("running_max"))
                    V.done(dve, dve.tensor_tensor(em[:], F[:], nM[:], ALU.subtract), sm("em_in"))
                    dve.wait_ge(sm("c_scored"), 1)
                    for par in range(2):
                        sc = ps[:, 6 + par, 0:TT * 4 * NCMP].rearrange("p (t n) -> p t n", t=TT)
                        out_l = Lc[:, :, 4 * par:4 * par + 4, :].rearrange("p t s i -> p t (s i)")
                        in_b = cbias[:, :, 4 * par:4 * par + 4, :].rearrange("p t s i -> p t (s i)")
                        ins = dve.scalar_tensor_tensor(out_l, sc, AD ** -0.5, in_b, ALU.mult, ALU.add)
                        (V.done(dve, ins, sm("c_copied")) if par else V.link(dve, ins))
                    flat = Lc[:].rearrange("p t s i -> p (t s) i")
                    V.link(dve, dve.tensor_reduce(nmax[:, 2].rearrange("p t s -> p (t s)"), flat, AX.X, ALU.max))
                    V.done(dve, dve.tensor_tensor(flat, flat, nmax[:, 2].rearrange("p t s -> p (t s)").unsqueeze(2)
                                                  .to_broadcast([P, TT * AH, NCMP]), ALU.subtract), sm("lc_ready"))
                    dve.wait_ge(sm("decay_ready"), 1)
                    dve.wait_ge(sm("em_ready"), 1)
                    for t in (1, 0):
                        LM = LM1 if t else LM0[:]
                        sc = bank2(0).rearrange("p (h s) -> p h s", h=MH) if t else ps[:, 2, :].rearrange("p (h s) -> p h s", h=MH)
                        V.link(dve, dve.scalar_tensor_tensor(LM, sc, MD ** -0.5, LM, ALU.mult, ALU.mult))
                        V.link(dve, dve.tensor_reduce(den[:, t, :], LM, AX.X, ALU.add))
                        V.link(dve, dve.scalar_tensor_tensor(den[:, t, :], den[:, t, :], -1.0, den[:, t, :], ALU.mult, ALU.max))
                        V.link(dve, dve.tensor_tensor(den[:, t, :], den[:, t, :], em[:, t, :], ALU.max))
                        V.link(dve, dve.reciprocal(den[:, t, :], den[:, t, :]))
                        V.done(dve, dve.tensor_tensor(LM, LM, den[:, t, :].unsqueeze(2)
                                                      .to_broadcast([P, MH, (t + 1) * P]), ALU.mult), sm("w_ready"))
                    dve.wait_ge(sm("ec_ready"), 1)
                    for t in range(TT):
                        ok = cst[:, C_VALC + t * NCMP:C_VALC + (t + 1) * NCMP].unsqueeze(1).to_broadcast([P, AH, NCMP])
                        V.link(dve, dve.tensor_tensor(Lc[:, t], Lc[:, t], ok, ALU.mult))
                        V.link(dve, dve.tensor_reduce(esum[:, 2, t, :], Lc[:, t], AX.X, ALU.add))
                        V.link(dve, dve.tensor_scalar(esum[:, 2, t, :], esum[:, 2, t, :], 1e-30, None, ALU.max))
                        V.link(dve, dve.reciprocal(esum[:, 2, t, :], esum[:, 2, t, :]))
                        coef = esum[:, 2, t, :].rearrange("p (par hh) -> p par hh", par=2)
                        V.link(dve, dve.tensor_tensor(coef, coef, gate_of(0, t), ALU.mult))
                        ins = dve.tensor_tensor(Lc[:, t], Lc[:, t], esum[:, 2, t, :].unsqueeze(2)
                                                .to_broadcast([P, AH, NCMP]), ALU.mult)
                        (V.done(dve, ins, sm("pc_ready")) if t == TT - 1 else V.link(dve, ins))
                    dve.wait_ge(sm("m_out"), 1)
                    V.done(dve, dve.tensor_tensor(mix[:, 0:MH, :].rearrange("p k t -> p (k t)"), bank2(0),
                                                  oT[:].rearrange("p k t -> p (k t)"), ALU.mult), sm("m_done"))

                    def logits(u):
                        b, t = UNITS[u]
                        w = (t + 1) * P
                        dve.wait_ge(sm("scored"), u + 1)
                        if u >= 2:
                            need = sum(len(UNIT_ROUNDS[UNITS[v]]) for v in range(u - 1)) + 4
                            dve.wait_ge(sm("p_turned"), need)
                        L = L1 if t else L0
                        sc = (ps[:, 4:8, :] if t else ps[:, 0:2, :]).rearrange("p b n -> p (b n)")\
                            .rearrange("p (s n) -> p s n", s=AH)
                        V.link(dve, dve.scalar_tensor_tensor(L, sc, AD ** -0.5, TB[:, :, SEQ - w:SEQ], ALU.mult, ALU.add))
                        V.done(dve, dve.tensor_reduce(nmax[:, b, t, :], L, AX.X, ALU.max, negate=True),
                               sm("logits_ready"))

                    def probs(u):
                        b, t = UNITS[u]
                        L = L1 if t else L0
                        dve.wait_ge(sm("exp_ready"), u + 1)
                        es = esum[:, b, t, :]
                        V.link(dve, dve.reciprocal(es, es))
                        coef = es.rearrange("p (par hh) -> p par hh", par=2)
                        V.link(dve, dve.tensor_tensor(coef, coef, gate_of(1 + b, t), ALU.mult))
                        V.done(dve, dve.tensor_tensor(L, L, es.unsqueeze(2).to_broadcast([P, AH, (t + 1) * P]),
                                                      ALU.mult), sm("probs_ready"))

                    logits(0)
                    logits(1)
                    probs(0)
                    probs(1)
                    logits(2)
                    logits(3)
                    probs(2)
                    probs(3)
                    dve.wait_ge(sm("mod_turned"), 2)
                    V.link(dve, dve.tensor_tensor(mod[:, 16:48], ps[:, 6, 0:32], colv("b_ada")[:, 16:48], ALU.add))
                    V.link(dve, dve.tensor_tensor(mod2[:], ps[:, 6, 32:56], colv("ada_b_2"), ALU.add))
                    dve.wait_ge(sm("a_out"), 1)
                    V.done(dve, dve.tensor_copy(mix[:, MH:KT, :].rearrange("p k t -> p (k t)"), bank2(0)), sm("mix_ready"))

        att.close()
        with ExitStack() as pd:
            yT = sb("yT", [P, KT, SEQ], at=pd)
            sq = sb("sqd", [P, KT, SEQ], at=pd)
            flatten = lambda a: a[:].rearrange("p k t -> p (k t)")
            with nc.Block() as block:
                @block.tensor
                def _(pe):
                    for n in range(N_OUT, N_OUT + 2):
                        pe.wait_ge(sm(f"slab_ready{n % SLOTS}"), slab_count(SLABS1, n))
                        columns_by_tokens(pe, n, 2 * (n - N_OUT), src=mix).then_inc(sm("slab_used"), 1)
                    norm_sums(pe, sq, 4, "x_summed", (sm("sq_ready"), 3))
                    norm_sums(pe, sq, 5, "x_summed", (sm("sq_ready"), 4))

                @block.scalar
                def _(act):
                    for h in range(2):
                        act.wait_ge(sm("y_copied"), h + 1)
                        norm_squares(act, yT[:, 4 * h:4 * h + 4, :], sq[:, 4 * h:4 * h + 4, :], "sq_ready")
                    norm_root(act, 2)
                    act.wait_ge(sm("x1_ready"), 1)
                    norm_squares(act, xT[:], sq[:], "sq_ready")
                    norm_root(act, 3)
                    for k in range(KT):
                        act.wait_ge(sm("h_scaled"), KT + k + 1)
                        act.activation(hT[:, k, :], hT[:, k, :], ACT.Identity, bias=mod[:, 24 + k:25 + k])\
                            .then_inc(sm("h_ready"), 1)

                @block.vector
                def _(dve):
                    for h in range(2):
                        dve.wait_ge(sm("slab_used"), N_OUT + h + 1)
                        V.done(dve, dve.tensor_copy(yT[:, 4 * h:4 * h + 4, :].rearrange("p k t -> p (k t)"), bank2(2 * h)),
                               sm("y_copied"))
                    V.link(dve, dve.tensor_tensor(gain[:], mod[:, 16:24], colv("g_post_mix"), ALU.mult))
                    norm_rstd(dve, 4, (sm("x_summed"), 2))
                    for k in range(KT):
                        V.link(dve, dve.scalar_tensor_tensor(yT[:, k, :], yT[:, k, :], gain[:, k:k + 1], rstd[:],
                                                             ALU.mult, ALU.mult))
                    V.done(dve, dve.tensor_tensor(xT[:], xT[:], yT[:], ALU.add), sm("x1_ready"))
                    V.link(dve, dve.scalar_tensor_tensor(gain[:], mod[:, 32:40], 1.0, colv("g_pre_ffn"), ALU.add, ALU.mult))
                    norm_rstd(dve, 5, (sm("x_summed"), 3))
                    for k in range(KT):
                        dve.scalar_tensor_tensor(hT[:, k, :], xT[:, k, :], gain[:, k:k + 1], rstd[:], ALU.mult, ALU.mult)\
                            .then_inc(sm("h_scaled"), 1)
        first_ring.close()

        retire("""a_out a_ready a_spread c_copied c_scored compressed decay_ready ec_ready em_in em_ready exp_ready
                  f_summed kcm_ready kin_ready ksw_in lc_ready lf_ready ln_ready logits_ready m_done m_out mix_ready
                  nab_ready p_turned pc_ready probs_ready pt_ready qk_scored running_max w_ready w_turned wt_ready
                  conv_ready qk_ready small_in z_copied c_exp silc_ready rows_in rows_turned rv_ready rv_stored
                  rv_summed""")
        STAGES = 4
        SLABS = 12
        raw = ring_low[:].rearrange("p s k n -> p (s k n)").rearrange("p (s n) -> p s n", s=STAGES)
        EXPERT_SEMS = ("b3_in router_in h2_turned h2t_ready routed sel_ready places_summed gate_ready gate_turned gt_ready "
                       "bias_summed h2l_ready router_logits router_exp gate_high pm_ready gathered xg_ready act_ready act_turned "
                       "pm_turned pmT_ready gr_ready ye_high ye_low added aT_high aT_low scattered glu_ready sig_ready "
                       "steps slab_done w_high w_low w_low_pool filled "
                       "raw_in0 raw_in1 raw_in2 raw_in3").split()
        yacc = hT
        moe = ctx.enter_context(ExitStack())
        h2h = sb("h2h", [P, TT, D], F32R, at=moe)
        h2l = sb("h2l", [P, TT, D], F32R, at=moe)
        place = sb("place", [P, TT, NE], at=moe)
        gate = sb("gate", [P, TT, NE], at=moe)
        gate2 = sb("gate2", [P, TT, NE, 2], F32R, at=moe)
        idr = sb("idr", [P, P], F32R, at=moe)
        bup = sb("bup", [96, 2 * DE], BF16, at=moe)
        sel3 = sb("sel3", [96, NE], BF16, at=moe)
        flag = sb("flag", [1, 1], I32, at=moe)

        def load_expert(sp, e, j, sem):
            dst = raw[:, j % STAGES, :]
            if j < 8:
                h, kp = j // 4, j % 4
                for q in range(2):
                    src = A["w_up"][bass.ds(e, 1), (2 * kp + q) * P:(2 * kp + q + 1) * P, :]\
                        .rearrange("a p (c n) -> p (a c) n", c=2)[:, :, 512 * h:512 * h + 512]
                    sp.dma_start(dst[:, q * D:(q + 1) * D].rearrange("p (c n) -> p c n", c=2), src).then_inc(sem, 16)
            else:
                src = A["w_down"][bass.ds(e, 1), 2 * (j - 8) * P:2 * (j - 7) * P, :].rearrange("a (f p) n -> p (a f) n", p=P)
                sp.dma_start(dst.rearrange("p (f n) -> p f n", f=2), src).then_inc(sem, 16)

        def loads_counted(e, j):
            q, r = divmod(j, SLABS)
            return (e + q) * 80 + (32, 64, 80)[r // STAGES]

        with ExitStack() as pe_:
            wr = sb("wr", [P, KT, NE], at=pe_)
            br = sb("br", [1, NE], at=pe_)
            bdn = sb("bdn", [NE, D], at=pe_)
            b3 = sb("b3", [96, 2 * DE], at=pe_)
            lg = sb("lg", [P, TT, NE + 4], at=pe_)
            rep = sb("rep", [P, TT, NE + 4], at=pe_)
            top = sb("top", [P, TT, 8], at=pe_)
            sel = sb("sel", [P, TT, NE], at=pe_)
            gsum = sb("gsum", [P, TT], at=pe_)
            gT = sb("gT", [NE, SEQ], at=pe_)
            cnt = sb("cnt", [1, NE], at=pe_)
            fl = sb("fl", [1, 1], at=pe_)
            with nc.Block() as block:
                @block.sync
                def _(sp):
                    for part in range(3):
                        sp.dma_start(b3[32 * part:32 * part + 32, :], A["b_up"]).then_inc(sm("b3_in"), 16)
                    sp.dma_start(wr[:], A["w_router"].rearrange("(k p) e -> p k e", p=P)).then_inc(sm("router_in"), 16)
                    sp.dma_start(br[:], A["b_router"]).then_inc(sm("router_in"), 16)
                    sp.dma_start(bdn[:], A["b_down"]).then_inc(sm("router_in"), 16)
                    for j in range(STAGES):
                        load_expert(sp, 0, j, sm(f"raw_in{j}"))

                @block.tensor
                def _(pe):
                    for t in range(TT):
                        for k in range(KT):
                            mm = pe.transpose(ps[:, 2 * t + k // 4, (k % 4) * P:(k % 4 + 1) * P],
                                              hT[:, k, t * P:(t + 1) * P], idn)
                        mm.then_inc(sm("h2_turned"), 1)
                    pe.wait_ge(sm("router_in"), 48)
                    for t in range(TT):
                        dst = ps[:, 4, t * NE:(t + 1) * NE]
                        for k in range(KT):
                            pe.matmul(dst, hT[:, k, t * P:(t + 1) * P], wr[:, k, :], start=(k == 0), stop=False)
                        mm = pe.matmul(dst, cst[0:1, C_ONES:C_ONES + P], br[:], start=False, stop=True)
                    mm.then_inc(sm("routed"), 1)
                    pe.wait_ge(sm("sel_ready"), 1)
                    tris = cst[:, C_TRIS:C_TRIS + P]
                    pe.matmul(ps[:, 5, 0:NE], tris, sel[:, 0, :], start=True, stop=True)
                    pe.matmul(ps[:, 5, NE:2 * NE], ones, sel[:, 0, :], start=True, stop=False)
                    pe.matmul(ps[:, 5, NE:2 * NE], tris, sel[:, 1, :], start=False, stop=True)
                    pe.matmul(ps[0:1, 5, 2 * NE:3 * NE], cst[:, C_ONES:C_ONES + 1], sel[:, 0, :], start=True, stop=False)
                    pe.matmul(ps[0:1, 5, 2 * NE:3 * NE], cst[:, C_ONES:C_ONES + 1], sel[:, 1, :], start=False, stop=True)\
                        .then_inc(sm("places_summed"), 1)
                    pe.wait_ge(sm("gate_ready"), 1)
                    for t in range(TT):
                        mm = pe.transpose(ps[0:NE, 6, t * P:(t + 1) * P], gate[:, t, :], idn)
                    mm.then_inc(sm("gate_turned"), 1)
                    pe.wait_ge(sm("h2l_ready"), TT)
                    pe.wait_ge(sm("gt_ready"), 1)
                    for k in range(KT):
                        mm = pe.matmul(ps[:, k // 2, (k % 2) * SEQ:(k % 2 + 1) * SEQ], bdn[:, k * P:(k + 1) * P], gT[:],
                                       start=True, stop=True)
                    mm.then_inc(sm("bias_summed"), 1)

                @block.scalar
                def _(act):
                    for t in range(TT):
                        act.wait_ge(sm("h2_turned"), t + 1)
                        S.done(act, act.activation(h2h[:, t, :], bank2(2 * t), ACT.Copy), sm("h2t_ready"))
                    act.wait_ge(sm("router_logits"), 1)
                    S.done(act, act.activation(rep[:], rep[:], ACT.Exp), sm("router_exp"))
                    act.wait_ge(sm("gate_ready"), 1)
                    S.done(act, act.activation(gate2[:, :, :, 0], gate[:], ACT.Copy), sm("gate_high"))

                @block.vector
                def _(dve):
                    dve.wait_ge(sm("b3_in"), 48)
                    V.link(dve, dve.tensor_copy(bup[:], b3[:]))
                    V.link(dve, dve.tensor_tensor(b3[:], b3[:], bup[:], ALU.subtract))
                    V.link(dve, dve.tensor_copy(bup[32:64, :], b3[32:64, :]))
                    V.link(dve, dve.tensor_copy(bup[64:96, :], b3[64:96, :]))
                    V.link(dve, dve.tensor_tensor(b3[64:96, :], b3[64:96, :], bup[64:96, :], ALU.subtract))
                    V.link(dve, dve.tensor_copy(bup[64:96, :], b3[64:96, :]))
                    V.link(dve, dve.tensor_copy(sel3[:], cst[0:96, C_SEL3:C_SEL3 + NE]))
                    V.link(dve, dve.memset(lg[:, :, NE:], -2e38))
                    V.link(dve, dve.tensor_copy(idr[:], idn))
                    for t in range(TT):
                        dve.wait_ge(sm("h2t_ready"), t + 1)
                        V.done(dve, dve.tensor_tensor(h2l[:, t, :], bank2(2 * t), h2h[:, t, :].bitcast(F32), ALU.subtract),
                               sm("h2l_ready"))
                    dve.wait_ge(sm("routed"), 1)
                    V.link(dve, dve.tensor_copy(lg[:, :, 0:NE], ps[:, 4, 0:TT * NE].rearrange("p (t e) -> p t e", t=TT)))
                    for t in range(TT):
                        V.link(dve, dve.max(top[:, t, :], lg[:, t, 0:NE]))
                        V.link(dve, dve.memset(top[:, t, TOPK:], -2e38))
                        V.link(dve, dve.match_replace(rep[:, t, :], top[:, t, :], lg[:, t, :], -3e38))
                    V.done(dve, dve.tensor_single_scalar(sel[:], rep[:, :, 0:NE], -3e38, ALU.is_equal), sm("sel_ready"))
                    V.done(dve, dve.tensor_tensor(rep[:], lg[:], top[:, :, 0:1].to_broadcast([P, TT, NE + 4]),
                                                  ALU.subtract), sm("router_logits"))
                    dve.wait_ge(sm("router_exp"), 1)
                    V.link(dve, dve.tensor_tensor(rep[:, :, 0:NE], rep[:, :, 0:NE], sel[:], ALU.mult))
                    V.link(dve, dve.tensor_reduce(gsum[:], rep[:, :, 0:NE], AX.X, ALU.add))
                    V.link(dve, dve.reciprocal(gsum[:], gsum[:]))
                    V.done(dve, dve.tensor_tensor(gate[:], rep[:, :, 0:NE], gsum[:].unsqueeze(2)
                                                  .to_broadcast([P, TT, NE]), ALU.mult), sm("gate_ready"))
                    dve.wait_ge(sm("places_summed"), 1)
                    pv = place[:]
                    V.link(dve, dve.scalar_tensor_tensor(pv, ps[:, 5, 0:TT * NE].rearrange("p (t e) -> p t e", t=TT), 1.0,
                                                         sel[:], ALU.add, ALU.mult))
                    V.link(dve, dve.tensor_scalar(pv, pv, 1.0, None, ALU.subtract))
                    V.link(dve, dve.tensor_reduce(fl[:], ps[0:1, 5, 2 * NE:3 * NE], AX.X, ALU.max))
                    V.link(dve, dve.tensor_single_scalar(flag[:], fl[:], float(P), ALU.is_gt))
                    dve.wait_ge(sm("gate_high"), 1)
                    V.link(dve, dve.tensor_tensor(gate2[:, :, :, 1], gate[:], gate2[:, :, :, 0].bitcast(F32), ALU.subtract))
                    dve.wait_ge(sm("gate_turned"), 1)
                    V.done(dve, dve.tensor_copy(gT[:], ps[0:NE, 6, 0:SEQ]), sm("gt_ready"))
                    dve.wait_ge(sm("bias_summed"), 1)
                    V.link(dve, dve.tensor_copy(yacc[:].rearrange("p k t -> p (k t)"),
                                                ps[:, 0:4, :].rearrange("p b n -> p (b n)")))

        high = sb("high", [P, STAGES, 2 * DE], F32R, at=moe)
        low = sb("low", [P, STAGES, 2 * DE], F32R, at=moe)
        pm = sb("pm", [P, TT, P], F32R, at=moe)
        pmT = sb("pmT", [P, SEQ], F32R, at=moe)
        gr = sb("gr", [P, 1], at=moe)
        xh = sb("xh", [P, KT, P], F32R, at=moe)
        xl = sb("xl", [P, KT, P], F32R, at=moe)
        gl = sb("gl", [P, DE], at=moe)
        li = sb("li", [P, DE], at=moe)
        sg = sb("sg", [P, DE], at=moe)
        ah = sb("ah", [P, KT, P], F32R, at=moe)
        al = sb("al", [P, KT, P], F32R, at=moe)
        yh = sb("yh", [P, D], F32R, at=moe)
        yl = sb("yl", [P, D], F32R, at=moe)
        iota = cst[:, C_IOTA:C_IOTA + P]
        LEAD = STAGES - 1
        POOL_SLABS = (3, 7, 11)
        DVE_SLABS = tuple(j for j in range(SLABS) if j not in POOL_SLABS)

        def experts_block(block, tag, base, first_loaded, condition):
            s = lambda name: sm(tag + name)
            LINKS = 4

            def slabs_done(e, n):
                return e * SLABS + n + 1

            def wait_low(eng, e, j):
                q, r = divmod(j, SLABS)
                if r in POOL_SLABS:
                    eng.wait_ge(s("w_low_pool"), (e + q) * len(POOL_SLABS) + POOL_SLABS.index(r) + 1)
                else:
                    eng.wait_ge(s("w_low"), (e + q) * len(DVE_SLABS) + DVE_SLABS.index(r) + 1)

            def wait_place(eng, e, j):
                if isinstance(e, int) and e == 0 and j < STAGES:
                    return
                eng.wait_ge(s("slab_done"), slabs_done(e, j - STAGES + 1))

            def low_part(eng, e, j, ready):
                eng.wait_ge(s("w_high"), e * SLABS + j + 1)
                wait_place(eng, e, j)
                sl = j % STAGES
                eng.tensor_tensor(low[:, sl, :], raw[:, sl, :], high[:, sl, :].bitcast(F32), ALU.subtract)\
                    .then_inc(s(ready), 1)

            @block.sync
            def _(sp):
                with condition(sp):
                    if not first_loaded:
                        for j in range(STAGES):
                            load_expert(sp, 0, j, s(f"raw_in{j}"))

                    def follow(e, j):
                        wait_low(sp, e, j)
                        n = j + STAGES
                        load_expert(sp, e + n // SLABS, n % SLABS, s(f"raw_in{n % STAGES}"))

                    with sp.Fori(0, NE - 1) as e:
                        for j in range(SLABS):
                            follow(e, j)
                    for j in range(SLABS - STAGES):
                        follow(NE - 1, j)

            @block.gpsimd
            def _(pool):
                with condition(pool):
                    with pool.Fori(0, NE) as e:
                        for j in POOL_SLABS:
                            low_part(pool, e, j, "w_low_pool")

            @block.tensor
            def _(pe):
                def gather(n, rounds):
                    if rounds[0] == 0:
                        pe.wait_ge(s("pm_ready"), n + 1)
                    for r in rounds:
                        half, part = r // 2, (h2h, h2l)[r % 2]
                        if r >= 2:
                            pe.wait_ge(s("xg_ready"), n * 4 + r - 1)
                        for q in range(4):
                            k = 4 * half + q
                            for t in range(TT):
                                mm = pe.matmul(ps[:, r % 2, q * P:(q + 1) * P], part[:, t, k * P:(k + 1) * P], pm[:, t, :],
                                               start=(t == 0), stop=(t == TT - 1))
                                if isinstance(n, int) and n == 0 and (r, q, t) == (0, 0, 0):
                                    mm.then_inc(s("slab_done"), 1)
                        mm.then_inc(s("gathered"), 1)

                def scatter(e, rounds):
                    for r in rounds:
                        if r == 0:
                            pe.wait_ge(s("ye_low"), e * 2 + 3)
                        if r >= 2:
                            pe.wait_ge(s("added"), e * 4 + r - 1)
                        for q in range(2):
                            d = 2 * r + q
                            for part in (yh, yl):
                                mm = pe.matmul(ps[:, 6 + r % 2, q * SEQ:(q + 1) * SEQ], part[:, d * P:(d + 1) * P], pmT[:],
                                               start=(part is yh), stop=(part is yl))
                        mm.then_inc(s("scattered"), 1)

                def turn_act(e, h):
                    pe.wait_ge(s("act_ready"), e * 2 + h + 1)
                    pe.wait_ge(s("gr_ready" if h else "pmT_ready"), e + 1)
                    for q in range(4):
                        f = 4 * h + q
                        mm = pe.transpose(ps[:, 6 + h, q * P:(q + 1) * P], gl[:, f * P:(f + 1) * P], idn)
                    mm.then_inc(s("act_turned"), 1)

                def slab(e, j, first):
                    hi_w, lo_w = high[:, j % STAGES, :], low[:, j % STAGES, :]
                    kp = j % 4
                    hi_x, lo_x, bank = (xh, xl, 2 * (j // 4)) if j < 8 else (ah, al, 4)
                    pe.wait_ge(s("w_high"), e * SLABS + j + 1)
                    for i, (x, w) in enumerate(((hi_x, hi_w), (lo_x, hi_w), (hi_x, lo_w))):
                        if i == 2:
                            wait_low(pe, e, j)
                        for q in range(2):
                            for c in range(2):
                                mm = pe.matmul(ps[:, bank + c, :], x[:, 2 * kp + q, :], w[:, q * D + c * 512:q * D + (c + 1) * 512],
                                               start=(first and i == 0 and q == 0), stop=(kp == 3 and i == 2 and q == 1))
                    mm.then_inc(s("slab_done"), 1)

                def expert(e, last):
                    for h in range(2):
                        if h == 0:
                            pe.wait_ge(s("xg_ready"), e * 4 + 4)
                        for c in range(2):
                            at = c * DE + h * 512
                            pe.matmul(ps[:, 2 * h + c, :], sel3[:, bass.ds(e, 1)].to_broadcast([96, P]), bup[:, at:at + 512],
                                      start=True, stop=False)
                        for kp in range(4):
                            slab(e, 4 * h + kp, False)
                            if h == 0 and kp == 1:
                                scatter(e, (0, 1))
                            if h == 0 and kp == 2:
                                scatter(e, (2, 3))
                            if h == 1 and kp == 0:
                                pe.wait_ge(s("added"), e * 4 + 4)
                                for t in range(TT):
                                    pe.matmul(ps[:, 6, t * P:(t + 1) * P], pm[:, t, :], idr[:], start=True, stop=True)
                                for t in range(TT):
                                    mm = pe.matmul(ps[:, 7, 0:2], pm[:, t, :],
                                                   gate2[:, t, bass.ds(e, 1), :].rearrange("p a c -> p (a c)"),
                                                   start=(t == 0), stop=(t == TT - 1))
                                mm.then_inc(s("pm_turned"), 1)
                            if h == 1 and kp == 1:
                                turn_act(e, 0)
                    pe.wait_ge(s("aT_high"), e * 2 + 1)
                    pe.wait_ge(s("aT_low"), e * 2 + 1)
                    slab(e, 8, True)
                    if not last:
                        gather(e + 1, (0, 1))
                    turn_act(e, 1)
                    slab(e, 9, False)
                    if not last:
                        gather(e + 1, (2, 3))
                    pe.wait_ge(s("aT_high"), e * 2 + 2)
                    pe.wait_ge(s("aT_low"), e * 2 + 2)
                    slab(e, 10, False)
                    slab(e, 11, False)

                with condition(pe):
                    gather(0, (0, 1, 2, 3))
                    with pe.Fori(0, NE - 1) as e:
                        expert(e, False)
                    expert(NE - 1, True)
                    scatter(NE, (0, 1, 2, 3))

            @block.scalar
            def _(act):
                def high_part(e, j):
                    act.wait_ge(s(f"raw_in{j % STAGES}"), loads_counted(e, j))
                    wait_place(act, e, j)
                    sl = j % STAGES
                    act.activation(high[:, sl, :], raw[:, sl, :], ACT.Copy).then_inc(s("w_high"), 1)

                def copy_rows(n, r):
                    act.wait_ge(s("gathered"), n * 4 + r + 1)
                    dst = (xh, xl)[r % 2][:, 4 * (r // 2):4 * (r // 2) + 4, :].rearrange("p k r -> p (k r)")
                    act.activation(dst, ps[:, r % 2, :], ACT.Copy).then_inc(s("xg_ready"), 1)

                def sigmoid(e, h):
                    act.wait_ge(s("glu_ready"), e * 2 + h + 1)
                    act.activation(sg[:, h * 512:(h + 1) * 512], gl[:, h * 512:(h + 1) * 512], ACT.Sigmoid, scale=ALPHA)\
                        .then_inc(s("sig_ready"), 1)

                def turned_act(e, h):
                    act.wait_ge(s("act_turned"), e * 2 + h + 1)
                    act.activation(ah[:, 4 * h:4 * h + 4, :].rearrange("p k r -> p (k r)"), ps[:, 6 + h, :], ACT.Copy)\
                        .then_inc(s("aT_high"), 1)

                def expert(e, last):
                    for j in range(SLABS):
                        if j == 4:
                            sigmoid(e, 0)
                        if j == 5:
                            act.wait_ge(s("pm_turned"), e + 1)
                            act.activation(pmT[:], ps[:, 6, 0:SEQ], ACT.Copy).then_inc(s("pmT_ready"), 1)
                        if j == 6:
                            turned_act(e, 0)
                        if j == 8:
                            sigmoid(e, 1)
                        if j == 9:
                            if not last:
                                copy_rows(e + 1, 0)
                                copy_rows(e + 1, 1)
                            turned_act(e, 1)
                        if j == 10 and not last:
                            copy_rows(e + 1, 2)
                            copy_rows(e + 1, 3)
                        if not (last and j + LEAD >= SLABS):
                            high_part(e, j + LEAD)
                    act.wait_ge(s("slab_done"), slabs_done(e, SLABS))
                    act.wait_ge(s("gr_ready"), e + 1)
                    for h in range(2):
                        act.activation(yh[:, h * 512:(h + 1) * 512], ps[:, 4 + h, :], ACT.Copy, scale=gr[:, 0:1])\
                            .then_inc(s("ye_high"), 1)

                with condition(act):
                    for j in range(LEAD):
                        high_part(0, j)
                    for r in range(4):
                        copy_rows(0, r)
                    with act.Fori(0, NE - 1) as e:
                        expert(e, False)
                    expert(NE - 1, True)

            @block.vector
            def _(dve):
                def one_hot(n):
                    for t in range(TT):
                        ins = dve.tensor_scalar(pm[:, t, :], iota, place[:, t, bass.ds(n, 1)], None, ALU.is_equal)
                    ins.then_inc(s("pm_ready"), 1)

                def add(e, r):
                    dve.wait_ge(s("scattered"), e * 4 + r + 1)
                    acc = yacc[:, 2 * r:2 * r + 2, :].rearrange("p k t -> p (k t)")
                    dve.tensor_tensor(acc, acc, ps[:, 6 + r % 2, :], ALU.add).then_inc(s("added"), 1)

                def expert(e, last):
                    n = [0]

                    def link(ins):
                        n[0] += 1
                        ins.then_inc(s("steps"), 1)
                        dve.wait_ge(s("steps"), e * LINKS + n[0])

                    def swiglu(h):
                        a = slice(h * 512, (h + 1) * 512)
                        dve.wait_ge(s("slab_done"), slabs_done(e, 4 * h + 4))
                        dve.tensor_scalar(gl[:, a], ps[:, 2 * h, :], LIMIT, None, ALU.min).then_inc(s("glu_ready"), 1)
                        link(dve.tensor_scalar(li[:, a], ps[:, 2 * h + 1, :], LIMIT, -LIMIT, ALU.min, ALU.max))
                        dve.wait_ge(s("glu_ready"), e * 2 + h + 1)
                        link(dve.scalar_tensor_tensor(li[:, a], li[:, a], 1.0, gl[:, a], ALU.add, ALU.mult))
                        dve.wait_ge(s("sig_ready"), e * 2 + h + 1)
                        dve.tensor_tensor(gl[:, a], li[:, a], sg[:, a], ALU.mult).then_inc(s("act_ready"), 1)

                    def turned_low(h):
                        dve.wait_ge(s("aT_high"), e * 2 + h + 1)
                        at = slice(4 * h, 4 * h + 4)
                        dve.tensor_tensor(al[:, at, :].rearrange("p k r -> p (k r)"), ps[:, 6 + h, :],
                                          ah[:, at, :].rearrange("p k r -> p (k r)").bitcast(F32), ALU.subtract)\
                            .then_inc(s("aT_low"), 1)

                    for j in range(SLABS):
                        if j in (2, 3):
                            add(e, 2 * j - 4)
                            add(e, 2 * j - 3)
                        if j in (4, 8):
                            swiglu(j // 4 - 1)
                        if j == 5:
                            dve.wait_ge(s("pm_turned"), e + 1)
                            dve.tensor_reduce(gr[:], ps[:, 7, 0:2], AX.X, ALU.add).then_inc(s("gr_ready"), 1)
                            if not last:
                                one_hot(e + 1)
                        if j == 6:
                            turned_low(0)
                        if j == 9:
                            turned_low(1)
                        if (j + LEAD) % SLABS not in POOL_SLABS and not (last and j + LEAD >= SLABS):
                            low_part(dve, e, j + LEAD, "w_low")
                    for h in range(2):
                        a = slice(h * 512, (h + 1) * 512)
                        dve.wait_ge(s("ye_high"), e * 2 + h + 1)
                        dve.scalar_tensor_tensor(yl[:, a], ps[:, 4 + h, :], gr[:, 0:1], yh[:, a].bitcast(F32), ALU.mult,
                                                 ALU.subtract).then_inc(s("ye_low"), 1)
                    assert n[0] == LINKS, n

                with condition(dve):
                    if base:
                        dve.tensor_scalar(place[:], place[:], float(base), None, ALU.subtract).then_inc(s("filled"), 1)
                        dve.wait_ge(s("filled"), 1)
                    one_hot(0)
                    for unset in (pmT, yh, yl):
                        dve.memset(unset[:].bitcast(F32), 0.0).then_inc(s("ye_low"), 1)
                    for j in range(LEAD):
                        low_part(dve, 0, j, "w_low")
                    with dve.Fori(0, NE - 1) as e:
                        expert(e, False)
                    expert(NE - 1, True)
                    for r in range(4):
                        add(NE, r)

        with nc.Block() as block:
            experts_block(block, "", 0, True, lambda eng: nullcontext())
        with nc.Block() as block:
            experts_block(block, "more_", P, False, lambda eng: eng.If(eng.value_load(flag[0:1, 0:1], min_val=0, max_val=1)))
        moe.close()
        more_slots("second_ring")

        retire(" ".join(n for n in list(sems) if n in EXPERT_SEMS or n.startswith(("more_", "up_", "down_"))))
        with ExitStack() as pg_:
            sq = sb("sqg", [P, KT, SEQ], at=pg_)
            with nc.Block() as block:
                @block.sync
                def _(sp):
                    for n in range(SLOTS):
                        load_slab(sp, n, SLABS2[n], "b_")

                @block.tensor
                def _(pe):
                    norm_sums(pe, sq, 4, "x_summed", (sm("sq_ready"), 5))
                    norm_sums(pe, sq, 5, "x_summed", (sm("sq_ready"), 6))

                @block.scalar
                def _(act):
                    norm_squares(act, yacc[:], sq[:], "sq_ready")
                    norm_root(act, 4)
                    act.wait_ge(sm("x2_ready"), 1)
                    norm_squares(act, xT[:], sq[:], "sq_ready")
                    norm_root(act, 5)
                    for k in range(KT):
                        act.wait_ge(sm("h_scaled"), 2 * KT + k + 1)
                        act.activation(hT[:, k, :], hT[:, k, :], ACT.Identity, bias=mod2[:, k:k + 1])\
                            .then_inc(sm("h_ready"), 1)

                @block.vector
                def _(dve):
                    V.link(dve, dve.tensor_tensor(gain[:], mod[:, 40:48], colv("g_post_ffn"), ALU.mult))
                    norm_rstd(dve, 4, (sm("x_summed"), 4))
                    for k in range(KT):
                        V.link(dve, dve.scalar_tensor_tensor(yacc[:, k, :], yacc[:, k, :], gain[:, k:k + 1], rstd[:],
                                                             ALU.mult, ALU.mult))
                    V.done(dve, dve.tensor_tensor(xT[:], xT[:], yacc[:], ALU.add), sm("x2_ready"))
                    V.link(dve, dve.scalar_tensor_tensor(gain[:], mod2[:, 8:16], 1.0, colv("norm_g_2"), ALU.add, ALU.mult))
                    norm_rstd(dve, 5, (sm("x_summed"), 5))
                    for k in range(KT):
                        dve.scalar_tensor_tensor(hT[:, k, :], xT[:, k, :], gain[:, k:k + 1], rstd[:], ALU.mult, ALU.mult)\
                            .then_inc(sm("h_scaled"), 1)

        NH = QH + KVH
        xbc = sb("xbc", [P, XBC // P, SEQ])
        azT = sb("azT", [P, KT, SEQ])
        idt = sb("idt", [P, TT, 356])
        bc = sb("bc", [P, 2 * HD + 2 * ID + 3 * SH])
        att2 = ctx.enter_context(ExitStack())
        qkv = sb("qkv", [P, TT, (NH + KVH) * HD], at=att2)
        ang = sb("ang", [P, TT, ROT // 2 + IROT // 2], at=att2)
        turns = sb("turns", [P, TT, ROT // 2 + IROT // 2], at=att2)
        sin = sb("sin", [P, TT, ROT // 2 + IROT // 2], at=att2)
        cos = sb("cos", [P, TT, ROT // 2 + IROT // 2], at=att2)
        pos = sb("pos", [P, TT], I32, at=att2)
        posf = sb("posf", [P, TT], at=att2)
        with ExitStack() as ph:
            zc = sb("zc2", [P, 2, SEQ + 3], at=ph)
            cv = sb("cv2", [P, 2, 2, SEQ], at=ph)
            NHALF = XBC // 256
            with nc.Block() as block:
                @block.sync
                def _(sp):
                    for n in range(SLOTS, SLOTS + M_ZS):
                        load_slab(sp, n, SLABS2[n], "b_")

                @block.scalar
                def _(act):
                    for name, (at, w) in BC.items():
                        act.dma_start(bc[:, at:at + w], bass.AP(A[name].tensor, 0, [[0, P], [1, w]]))\
                            .then_inc(sm("bc_in"), 16)
                    with nc.allow_non_contiguous_dma("256 positions"):
                        act.dma_start(pos[:], A["positions_2"].rearrange("(t p) a -> p (t a)", p=P)).then_inc(sm("pos_in"), 16)
                    act.wait_ge(sm("angle_ready"), 1)
                    S.link(act, act.activation(sin[:], ang[:], ACT.Sin))
                    S.done(act, act.activation(cos[:], ang[:], ACT.Sin, scale=0.5), sm("half_sin_ready"))
                    for i in range(2):
                        act.wait_ge(sm("b_z_copied"), M_ZA + i + 1)
                        S.link(act, act.activation(azT[:, 4 * i:4 * i + 4, :], azT[:, 4 * i:4 * i + 4, :], ACT.Silu))
                    for i in range(NHALF):
                        act.wait_ge(sm("b_conv_ready"), i + 1)
                        for j in range(2):
                            ins = act.activation(xbc[:, 2 * i + j, :], cv[:, i % 2, j, :], ACT.Silu,
                                                 bias=col("conv_b_2", 2 * i + j))
                        S.done(act, ins, sm("b_silu_ready"))
                    act.wait_ge(sm("bc_in"), 16 * len(BC))

                @block.tensor
                def _(pe):
                    for n in range(M_ZS):
                        pe.wait_ge(sm(f"b_slab_ready{n % SLOTS}"), slab_count(SLABS2, n))
                        bank = 2 * (n % 4)
                        if n >= 4:
                            pe.wait_ge(sm("b_z_copied"), n - 3)
                        if n < 4:
                            mm = tokens_by_columns(pe, n, 356 if n == 3 else 512, bank)
                        else:
                            mm = columns_by_tokens(pe, n, bank)
                        mm.then_inc(sm("b_slab_used"), 1)

                @block.vector
                def _(dve):
                    V.link(dve, dve.memset(zc[:, :, 0:3], 0.0))
                    dve.wait_ge(sm("pos_in"), 16)
                    V.link(dve, dve.tensor_copy(posf[:], pos[:]))
                    nf = ROT // 2 + IROT // 2
                    V.link(dve, dve.tensor_tensor(ang[:], posf[:].unsqueeze(2).to_broadcast([P, TT, nf]),
                                                  cst[:, C_FREQ:C_FREQ + nf].unsqueeze(1).to_broadcast([P, TT, nf]), ALU.mult))
                    V.link(dve, dve.tensor_scalar(turns[:], ang[:], 1 / (2 * math.pi), ROUNDER, ALU.mult, ALU.add))
                    V.link(dve, dve.tensor_scalar(turns[:], turns[:], ROUNDER, None, ALU.subtract))
                    for part in (TWO_PI_HIGH, TWO_PI_LOW):
                        V.link(dve, dve.scalar_tensor_tensor(ang[:], turns[:], -part, ang[:], ALU.mult, ALU.add))
                    V.done(dve, dve.tensor_scalar(ang[:], ang[:], 3.1415925, -3.1415925, ALU.min, ALU.max), sm("angle_ready"))
                    dve.wait_ge(sm("half_sin_ready"), 1)
                    V.link(dve, dve.tensor_tensor(cos[:], cos[:], cos[:], ALU.mult))
                    V.link(dve, dve.tensor_scalar(cos[:], cos[:], -2.0, 1.0, ALU.mult, ALU.add))
                    for n in range(M_ZS):
                        bank = 2 * (n % 4)
                        dve.wait_ge(sm("b_slab_used"), n + 1)
                        tiles = bank2(bank).rearrange("p (j t) -> p j t", j=4)
                        if n < 3:
                            V.done(dve, dve.tensor_copy(qkv[:, :, 512 * n:512 * n + 512], ps[:, bank:bank + 2, :]),
                                   sm("b_z_copied"))
                        elif n == 3:
                            V.done(dve, dve.tensor_copy(idt[:], ps[:, bank:bank + 2, 0:356]), sm("b_z_copied"))
                        elif n < M_XBC:
                            V.done(dve, dve.tensor_copy(azT[:, 4 * (n - M_ZA):4 * (n - M_ZA) + 4, :], tiles), sm("b_z_copied"))
                        else:
                            for half in range(2):
                                i = 2 * (n - M_XBC) + half
                                ins = dve.tensor_copy(zc[:, :, 3:], tiles[:, 2 * half:2 * half + 2, :])
                                (V.done(dve, ins, sm("b_z_copied")) if half else V.link(dve, ins))
                                if i >= 2:
                                    dve.wait_ge(sm("b_silu_ready"), i - 1)
                                for j in range(2):
                                    c = cv[:, i % 2, j, :]
                                    V.link(dve, dve.tensor_scalar(c, zc[:, j, 0:SEQ], col("conv_w_2", 2 * i + j), None,
                                                                  ALU.mult))
                                    for tap in range(1, 4):
                                        ins = dve.scalar_tensor_tensor(c, zc[:, j, tap:tap + SEQ],
                                                                       col("conv_w_2", 24 * tap + 2 * i + j), c,
                                                                       ALU.mult, ALU.add)
                                        if j == 1 and tap == 3:
                                            V.done(dve, ins, sm("b_conv_ready"))
                                        else:
                                            V.link(dve, ins)

        with ExitStack() as pi:
            sq2 = sb("sq2", [P, NH * HD], at=pi)
            ssum = sb("ssum", [P, TT, NH], at=pi)
            rt = sb("rt", [P, 4, NH, ROT // 2], at=pi)
            kd = sb("kd", [P, TT, 2 * ID], at=pi)
            mean = sb("mean", [P, TT], at=pi)
            var = sb("var", [P, TT], at=pi)
            wix = sb("wix", [P, TT, IH], at=pi)
            qT = sb("qT", [P, QH, SEQ], at=pi)
            kT = sb("kT", [P, KVH, SEQ], at=pi)
            iqT = sb("iqT", [P, IH // 2, SEQ], at=pi)
            ikT = sb("ikT", [P, SEQ], at=pi)
            sc = sb("sc", [P, TT, SEQ], at=pi)
            tmp = sb("tmp", [P, SEQ], at=pi)
            top2 = sb("top2", [P, 8], at=pi)
            A1 = sb("A1", [P, QH, SEQ], at=pi)
            A0 = sq2[:, 0:QH * P].rearrange("p (h t) -> p h t", h=QH)
            nm2 = sb("nm2", [P, TT, QH], at=pi)
            es2 = sb("es2", [P, TT, QH], at=pi)
            P0 = qT
            P1 = A0

            def rotate(dve, x, c, s_, half, heads):
                x1, x2 = x[:, :, 0:half], x[:, :, half:2 * half]
                cb = c.unsqueeze(1).to_broadcast([P, heads, half])
                sb_ = s_.unsqueeze(1).to_broadcast([P, heads, half])
                r = [rt[:, i, 0:heads, 0:half] for i in range(4)]
                V.link(dve, dve.tensor_tensor(r[0], x1, cb, ALU.mult))
                V.link(dve, dve.tensor_tensor(r[1], x2, sb_, ALU.mult))
                V.link(dve, dve.tensor_tensor(r[2], x2, cb, ALU.mult))
                V.link(dve, dve.tensor_tensor(r[3], x1, sb_, ALU.mult))
                V.link(dve, dve.tensor_tensor(x1, r[0], r[1], ALU.subtract))
                return dve.tensor_tensor(x2, r[2], r[3], ALU.add)

            def bcv(name):
                at, w = BC[name]
                return bc[:, at:at + w]

            with nc.Block() as block:
                @block.scalar
                def _(act):
                    act.wait_ge(sm("var_ready"), 1)
                    S.done(act, act.activation(var[:], var[:], ACT.Sqrt), sm("dev_ready"))
                    for t in range(TT):
                        S.done(act, act.activation(sq2[:], qkv[:, t, 0:NH * HD], ACT.Square), sm("head_sq"))
                        act.wait_ge(sm("head_sums"), t + 1)
                    S.done(act, act.activation(ssum[:], ssum[:], ACT.Sqrt), sm("head_rms"))
                    act.wait_ge(sm("i_turned"), 1)
                    S.link(act, act.activation(iqT[:].rearrange("p j t -> p (j t)"), ps[:, 0, :], ACT.Copy))
                    S.done(act, act.activation(ikT[:], ps[:, 1, 0:SEQ], ACT.Copy), sm("i_ready"))
                    act.wait_ge(sm("q_turned"), 1)
                    S.link(act, act.activation(qT[:].rearrange("p h t -> p (h t)"),
                                               ps[:, 2:6, :].rearrange("p b n -> p (b n)"), ACT.Copy))
                    S.done(act, act.activation(kT[:].rearrange("p h t -> p (h t)"), ps[:, 6, :], ACT.Copy), sm("q_ready"))
                    for u, t in enumerate((0, 1)):
                        act.wait_ge(sm("b_logits"), u + 1)
                        L = A1[:] if t else A0
                        for h in range(QH):
                            ins = act.activation(L[:, h, :], L[:, h, :], ACT.Exp, bias=nm2[:, t, h:h + 1],
                                                 accum_out=es2[:, t, h:h + 1])
                        S.done(act, ins, sm("b_exp"))
                        for s_ in range(t + 1):
                            act.wait_ge(sm("b_p_turned"), 2 * u + s_ if u else 1)
                            dst = P0[:, :, t * P:(t + 1) * P] if s_ == 0 else P1
                            S.done(act, act.activation(dst, bank2(6).rearrange("p (h t) -> p h t", h=QH), ACT.Copy),
                                   sm("b_pt_ready"))

                @block.tensor
                def _(pe):
                    pe.wait_ge(sm("i_rotated"), TT)
                    for t in range(TT):
                        for j in range(2):
                            pe.transpose(ps[:, 0, j * SEQ + t * P:j * SEQ + (t + 1) * P], idt[:, t, j * P:(j + 1) * P], idn)
                        mm = pe.transpose(ps[:, 1, t * P:(t + 1) * P], kd[:, t, :], idn)
                    mm.then_inc(sm("i_turned"), 1)
                    pe.wait_ge(sm("q_rotated"), TT)
                    for h in range(NH):
                        for t in range(TT):
                            dst = ps[:, 2 + h // 2, (h % 2) * SEQ + t * P:(h % 2) * SEQ + (t + 1) * P]
                            mm = pe.transpose(dst, qkv[:, t, h * HD:(h + 1) * HD], idn)
                    mm.then_inc(sm("q_turned"), 1)
                    pe.wait_ge(sm("i_ready"), 1)
                    for t in range(TT):
                        w = (t + 1) * P
                        if t:
                            pe.wait_ge(sm("i_scored"), 1)
                        for h in range(IH):
                            half = slice(64 * (h % 2), 64 * (h % 2) + 64)
                            mm = pe.matmul(ps[:, h % 2, (h // 2) * w:(h // 2) * w + w], iqT[half, h // 2, t * P:(t + 1) * P],
                                           ikT[half, 0:w], start=True, stop=True)
                        mm.then_inc(sm("i_logits"), 1)
                    pe.wait_ge(sm("q_ready"), 1)
                    for t in range(TT):
                        w = (t + 1) * P
                        for h in range(QH):
                            at = h * w
                            mm = pe.matmul(ps[:, (2 if t else 6) + at // 512, at % 512:at % 512 + w],
                                           qT[:, h, t * P:(t + 1) * P], kT[:, h // (QH // KVH), 0:w], start=True, stop=True)
                        mm.then_inc(sm("b_scored"), 1)
                    nturn = 0
                    for t in range(TT):
                        pe.wait_ge(sm("b_probs"), t + 1)
                        for s_ in range(t + 1):
                            if nturn:
                                pe.wait_ge(sm("b_pt_ready"), nturn)
                            for h in range(QH):
                                L = A1[:] if t else A0
                                mm = pe.transpose(ps[:, 6 + h // 4, (h % 4) * P:(h % 4 + 1) * P],
                                                  L[:, h, s_ * P:(s_ + 1) * P], idn)
                            mm.then_inc(sm("b_p_turned"), 1)
                            nturn += 1
                    pe.wait_ge(sm("b_pt_ready"), 3)
                    for h in range(QH):
                        out_h = ps[:, 2 + h // 2, (h % 2) * SEQ:(h % 2 + 1) * SEQ]
                        v0 = (NH + h // (QH // KVH)) * HD
                        pe.matmul(out_h, qkv[:, 0, v0:v0 + HD], P0[:, h, :], start=True, stop=False)
                        mm = pe.matmul(out_h[:, P:SEQ], qkv[:, 1, v0:v0 + HD], P1[:, h, :], start=False, stop=True)
                    mm.then_inc(sm("b_att"), 1)

                @block.vector
                def _(dve):
                    for t in range(TT):
                        ki = idt[:, t, 256:320]
                        V.link(dve, dve.tensor_reduce(mean[:, t:t + 1], ki, AX.X, ALU.add))
                        V.link(dve, dve.tensor_scalar(mean[:, t:t + 1], mean[:, t:t + 1], 1.0 / ID, None, ALU.mult))
                        V.link(dve, dve.tensor_scalar(ki, ki, mean[:, t:t + 1], None, ALU.subtract))
                        V.link(dve, dve.tensor_tensor(tmp[:, 0:ID], ki, ki, ALU.mult))
                        V.link(dve, dve.tensor_reduce(var[:, t:t + 1], tmp[:, 0:ID], AX.X, ALU.add))
                    V.done(dve, dve.tensor_scalar(var[:], var[:], 1.0 / ID, EPS, ALU.mult, ALU.add), sm("var_ready"))
                    V.link(dve, dve.tensor_scalar(wix[:], idt[:, :, 320:324], IH ** -0.5 * ID ** -0.5, None, ALU.mult))
                    dve.wait_ge(sm("dev_ready"), 1)
                    V.link(dve, dve.reciprocal(var[:], var[:]))
                    for t in range(TT):
                        ki = idt[:, t, 256:320]
                        V.link(dve, dve.tensor_scalar(ki, ki, var[:, t:t + 1], None, ALU.mult))
                        V.link(dve, dve.tensor_tensor(ki, ki, bcv("idx_k_ln_g_2"), ALU.mult))
                        V.link(dve, dve.tensor_tensor(ki, ki, bcv("idx_k_ln_b_2"), ALU.add))
                        x = idt[:, t, 0:320].rearrange("p (h d) -> p h d", h=IH + 1)
                        f0 = ROT // 2
                        V.link(dve, rotate(dve, x, cos[:, t, f0:f0 + IROT // 2], sin[:, t, f0:f0 + IROT // 2],
                                           IROT // 2, IH + 1))
                        V.link(dve, dve.tensor_copy(kd[:, t, 0:ID], ki))
                        V.done(dve, dve.tensor_copy(kd[:, t, ID:], ki), sm("i_rotated"))
                    for t in range(TT):
                        dve.wait_ge(sm("head_sq"), t + 1)
                        V.link(dve, dve.tensor_reduce(ssum[:, t, :], sq2[:].rearrange("p (h d) -> p h d", h=NH), AX.X,
                                                      ALU.add))
                        V.done(dve, dve.tensor_scalar(ssum[:, t, :], ssum[:, t, :], 1.0 / HD, EPS, ALU.mult, ALU.add),
                               sm("head_sums"))
                    dve.wait_ge(sm("head_rms"), 1)
                    V.link(dve, dve.reciprocal(ssum[:], ssum[:]))
                    for t in range(TT):
                        x = qkv[:, t, 0:NH * HD].rearrange("p (h d) -> p h d", h=NH)
                        V.link(dve, dve.tensor_tensor(x, x, ssum[:, t, :].unsqueeze(2).to_broadcast([P, NH, HD]), ALU.mult))
                        V.link(dve, dve.tensor_tensor(x[:, 0:QH], x[:, 0:QH], bcv("q_norm_g_2").unsqueeze(1)
                                                      .to_broadcast([P, QH, HD]), ALU.mult))
                        V.link(dve, dve.tensor_tensor(x[:, QH:], x[:, QH:], bcv("k_norm_g_2").unsqueeze(1)
                                                      .to_broadcast([P, KVH, HD]), ALU.mult))
                        V.done(dve, rotate(dve, x, cos[:, t, 0:ROT // 2], sin[:, t, 0:ROT // 2], ROT // 2, NH),
                               sm("q_rotated"))
                    for t in range(TT):
                        w = (t + 1) * P
                        s_ = sc[:, t, 0:w]
                        dve.wait_ge(sm("i_logits"), t + 1)
                        for h in range(IH):
                            src = ps[:, h % 2, (h // 2) * w:(h // 2) * w + w]
                            dst = s_ if h == 0 else tmp[:, 0:w]
                            ins = dve.tensor_scalar(dst, src, 0.0, wix[:, t, h:h + 1], ALU.max, ALU.mult)
                            if h == IH - 1:
                                V.done(dve, ins, sm("i_scored"))
                            else:
                                V.link(dve, ins)
                            if h:
                                V.link(dve, dve.tensor_tensor(s_, s_, tmp[:, 0:w], ALU.add))
                        cm = cst[:, C_ZERO:C_ZERO + SEQ] if t else cst[:, C_CM:C_CM + P]
                        V.link(dve, dve.tensor_tensor(s_, s_, cm, ALU.add))
                        for r in range(KEEP // 8):
                            V.link(dve, dve.max(top2[:], s_))
                            V.link(dve, dve.match_replace(s_, top2[:], s_, -3e38))
                        V.link(dve, dve.tensor_single_scalar(s_, s_, -3e38, ALU.is_equal))
                        V.link(dve, dve.tensor_scalar(s_, s_, 1.0, -NEG, ALU.subtract, ALU.mult))
                        V.link(dve, dve.tensor_tensor(s_, s_, cm, ALU.add))
                        dve.wait_ge(sm("b_scored"), t + 1)
                        L = A1[:] if t else A0
                        src = (ps[:, 2:6, :] if t else ps[:, 6:8, :]).rearrange("p b n -> p (b n)")\
                            .rearrange("p (h n) -> p h n", h=QH)
                        V.link(dve, dve.scalar_tensor_tensor(L, src, HD ** -0.5, s_.unsqueeze(1).to_broadcast([P, QH, w]),
                                                             ALU.mult, ALU.add))
                        V.done(dve, dve.tensor_reduce(nm2[:, t, :], L, AX.X, ALU.max, negate=True), sm("b_logits"))
                    for t in range(TT):
                        L = A1[:] if t else A0
                        dve.wait_ge(sm("b_exp"), t + 1)
                        V.link(dve, dve.reciprocal(es2[:, t, :], es2[:, t, :]))
                        V.done(dve, dve.tensor_tensor(L, L, es2[:, t, :].unsqueeze(2).to_broadcast([P, QH, (t + 1) * P]),
                                                      ALU.mult), sm("b_probs"))
                    dve.wait_ge(sm("b_att"), 1)
                    V.link(dve, dve.tensor_tensor(azT[:].rearrange("p k t -> p (k t)"), azT[:].rearrange("p k t -> p (k t)"),
                                                  ps[:, 2:6, :].rearrange("p b n -> p (b n)"), ALU.mult))
        att2.close()

        GH = SH // SG
        GW = GH * SP
        ssm = ctx.enter_context(ExitStack())
        y = sb("y", [P, TT, DI], at=ssm)
        with ExitStack() as pj:
            xs = sb("xs", [P, TT, DI], at=pj)
            bt = sb("bt", [P, SG * SN], at=pj)
            xd = sb("xd", [P, GW], at=pj)
            st = sb("st", [P, GW], at=pj)
            dts = sb("dts", [P, TT, SH], at=pj)
            u_ = sb("u_", [P, TT, SH], at=pj)
            z_ = sb("z_", [P, TT, SH], at=pj)
            z2 = sb("z2", [P, TT, SH], at=pj)
            adt = sb("adt", [P, TT, SH], at=pj)
            aexp = sb("aexp", [P, SH], at=pj)
            cum = sb("cum", [P, TT, SH], at=pj)
            dec = sb("dec", [P, SH], at=pj)
            ecum = sb("ecum", [P, SH], at=pj)
            M = xbc[:, 0:8, :].rearrange("p (u k) t -> p u (k t)", u=2).rearrange("p u (h l) -> p u h l", h=GH)
            L_ = xbc[:, 8:16, :].rearrange("p (u k) t -> p u (k t)", u=2).rearrange("p u (h l) -> p u h l", h=GH)
            cb = sb("cb", [P, 2, P], at=pj)
            zs = sb("zs", [P, 2, 512], at=pj)
            t5 = sb("t5", [P, GW], at=pj)
            gs = sb("gs", [P, TT, SG], at=pj)

            def bcv(name):
                at, w = BC[name]
                return bc[:, at:at + w]

            PAIRS = [(c, g) for g in range(SG) for c in range(TT)]
            with nc.Block() as block:
                @block.gpsimd
                def _(pool):
                    pool.wait_ge(sm("adt_ready"), 1)
                    pool.wait_ge(sm("xs_ready"), 9)
                    for i, (c, g) in enumerate(PAIRS):
                        if i >= 2:
                            pool.wait_ge(sm("seg_summed"), i - 1)
                        gh = slice(g * GH, (g + 1) * GH)
                        pool.tensor_tensor(L_[:, i % 2], cst[:, C_LATER:C_LATER + P].unsqueeze(1).to_broadcast([P, GH, P]),
                                           adt[:, c, gh].unsqueeze(2).to_broadcast([P, GH, P]), ALU.mult)\
                            .then_inc(sm("later_ready"), 1)

                @block.sync
                def _(sp):
                    for n in range(SLOTS + M_ZS, SLOTS + M_SSM):
                        load_slab(sp, n, SLABS2[n], "b_")

                @block.scalar
                def _(act):
                    S.done(act, act.activation(aexp[:], bcv("a_log_2"), ACT.Exp), sm("a_exp"))
                    act.wait_ge(sm("dt_abs"), 1)
                    S.done(act, act.activation(u_[:], u_[:], ACT.Exp), sm("dt_exp"))
                    for i in range(9):
                        act.wait_ge(sm("xs_turned"), i + 1)
                        bank = 2 * (i % 2)
                        if i < 8:
                            t, q = i // 4, i % 4
                            S.done(act, act.activation(xs[:, t, q * 512:(q + 1) * 512], ps[:, bank, :], ACT.Copy),
                                   sm("xs_ready"))
                        else:
                            S.done(act, act.activation(bt[:], ps[:, bank, :], ACT.Copy), sm("xs_ready"))
                    act.wait_ge(sm("dec_in"), 1)
                    S.link(act, act.activation(dec[:], dec[:], ACT.Exp))
                    S.done(act, act.activation(ecum[:], cum[:, 1, :], ACT.Exp), sm("dec_ready"))
                    for i in range(len(PAIRS)):
                        act.wait_ge(sm("seg_ready"), i + 1)
                        S.done(act, act.activation(M[:, i % 2], M[:, i % 2], ACT.Exp), sm("seg_exp"))
                    for n in range(4):
                        for t in range(TT):
                            i = 2 * n + t
                            act.wait_ge(sm("b_slab_used"), M_ZS + n + 1)
                            if i >= 2:
                                act.wait_ge(sm("zs_used"), i - 1)
                            S.done(act, act.activation(zs[:, i % 2, :], ps[:, 2 * (n % 2) + t, :], ACT.Silu), sm("zs_ready"))
                    act.wait_ge(sm("gs_ready"), 1)
                    S.done(act, act.activation(gs[:], gs[:], ACT.Sqrt), sm("gs_rms"))

                @block.tensor
                def _(pe):
                    for i in range(9):
                        bank = 2 * (i % 2)
                        if i >= 2:
                            pe.wait_ge(sm("xs_ready"), i - 1)
                        for j in range(4):
                            t = i // 4 if i < 8 else 0
                            tile = 4 * (i % 4) + j if i < 8 else 16 + j
                            mm = pe.transpose(ps[:, bank, j * P:(j + 1) * P], xbc[:, tile, t * P:(t + 1) * P], idn)
                        mm.then_inc(sm("xs_turned"), 1)
                    tri = cst[:, C_TRI:C_TRI + P]
                    pe.wait_ge(sm("adt_ready"), 1)
                    for t in range(TT):
                        pe.matmul(ps[:, 1, t * SH:(t + 1) * SH], tri, adt[:, t, :], start=True, stop=True)
                    pe.matmul(ps[:, 1, 2 * SH:3 * SH], cst[:, C_LATER:C_LATER + P], adt[:, 0, :], start=True, stop=True)\
                        .then_inc(sm("cum_summed"), 1)
                    pe.wait_ge(sm("cum_ready"), 1)
                    for i, (c, g) in enumerate(PAIRS):
                        tk = slice(c * P, (c + 1) * P)
                        if i >= 2:
                            pe.wait_ge(sm("seg_ready"), i - 1)
                            pe.wait_ge(sm("y_out"), i - 1)
                        pe.wait_ge(sm("xs_ready"), 9)
                        pe.matmul(ps[:, 6 + i % 2, 0:P], xbc[:, 16 + g, tk], xbc[:, 20 + g, tk], start=True, stop=True)
                        pe.wait_ge(sm("later_ready"), i + 1)
                        for h in range(GH):
                            mm = pe.matmul(ps[:, 2 + 2 * (i % 2) + h // 4, (h % 4) * P:(h % 4 + 1) * P],
                                           L_[:, i % 2, h, :], tri, start=True, stop=True)
                        mm.then_inc(sm("seg_summed"), 1)
                        if c == 0:
                            pe.wait_ge(sm("xd_ready"), g + 1)
                            pe.matmul(ps[:, 0, :], bt[:, g * SN:(g + 1) * SN], xd[:], start=True, stop=True)\
                                .then_inc(sm("st_made"), 1)
                            pe.wait_ge(sm("st_ready"), g + 1)
                            if i:
                                pe.wait_ge(sm("y_out"), i)
                            pe.matmul(ps[:, 1, :], xbc[:, 20 + g, P:SEQ], st[:], start=True, stop=True)\
                                .then_inc(sm("off_made"), 1)
                        pe.wait_ge(sm("m_ready"), i + 1)
                        for h in range(GH):
                            mm = pe.matmul(ps[:, 6 + i % 2, h * SP:(h + 1) * SP], M[:, i % 2, h, :],
                                           y[:, c, g * GW + h * SP:g * GW + (h + 1) * SP], start=True, stop=True)
                        mm.then_inc(sm("y_made"), 1)
                    for n in range(4):
                        m = M_ZS + n
                        pe.wait_ge(sm(f"b_slab_ready{m % SLOTS}"), slab_count(SLABS2, m))
                        if n >= 2:
                            pe.wait_ge(sm("zs_ready"), 2 * n - 2)
                        elif n == 0:
                            pe.wait_ge(sm("y_out"), 2 * SG)
                        tokens_by_columns(pe, m, 512, 2 * (n % 2)).then_inc(sm("b_slab_used"), 1)

                @block.vector
                def _(dve):
                    dtr = idt[:, :, 324:356]
                    V.link(dve, dve.tensor_tensor(dts[:], dtr, bcv("dt_bias_2").unsqueeze(1).to_broadcast([P, TT, SH]), ALU.add))
                    V.done(dve, dve.scalar_tensor_tensor(u_[:], dts[:], -1.0, dts[:], ALU.mult, ALU.min), sm("dt_abs"))
                    dve.wait_ge(sm("dt_exp"), 1)
                    V.link(dve, dve.tensor_scalar(z_[:], u_[:], 2.0, None, ALU.add))
                    V.link(dve, dve.reciprocal(z_[:], z_[:]))
                    V.link(dve, dve.tensor_tensor(z_[:], z_[:], u_[:], ALU.mult))
                    V.link(dve, dve.tensor_tensor(z2[:], z_[:], z_[:], ALU.mult))
                    V.link(dve, dve.tensor_scalar(u_[:], z2[:], 2.0 / 17, 2.0 / 15, ALU.mult, ALU.add))
                    for odd in (13, 11, 9, 7, 5, 3, 1):
                        V.link(dve, dve.tensor_tensor(u_[:], u_[:], z2[:], ALU.mult))
                        V.link(dve, dve.tensor_scalar(u_[:], u_[:], 2.0 / odd, None, ALU.add))
                    V.link(dve, dve.tensor_tensor(u_[:], u_[:], z_[:], ALU.mult))
                    V.link(dve, dve.scalar_tensor_tensor(dts[:], dts[:], 0.0, u_[:], ALU.max, ALU.add))
                    dve.wait_ge(sm("a_exp"), 1)
                    V.link(dve, dve.scalar_tensor_tensor(adt[:], dts[:], -1.0, aexp[:].unsqueeze(1).to_broadcast([P, TT, SH]),
                                                         ALU.mult, ALU.mult))
                    V.done(dve, dve.tensor_scalar(adt[:], adt[:], -120.0, None, ALU.max), sm("adt_ready"))
                    dve.wait_ge(sm("cum_summed"), 1)
                    V.link(dve, dve.tensor_copy(cum[:].rearrange("p t h -> p (t h)"), ps[:, 1, 0:2 * SH]))
                    V.done(dve, dve.tensor_copy(dec[:], ps[:, 1, 2 * SH:3 * SH]), sm("dec_in"))
                    dve.wait_ge(sm("xs_ready"), 8)
                    for t in range(TT):
                        yv = y[:, t, :].rearrange("p (h q) -> p h q", h=SH)
                        ins = dve.tensor_tensor(yv, xs[:, t, :].rearrange("p (h q) -> p h q", h=SH),
                                                dts[:, t, :].unsqueeze(2).to_broadcast([P, SH, SP]), ALU.mult)
                        (V.done(dve, ins, sm("cum_ready")) if t else V.link(dve, ins))
                    dve.wait_ge(sm("dec_ready"), 1)
                    for i, (c, g) in enumerate(PAIRS):
                        gw = slice(g * GW, (g + 1) * GW)
                        heads = lambda a: a.rearrange("p (h q) -> p h q", h=GH)
                        gh = slice(g * GH, (g + 1) * GH)
                        if c == 0:
                            if g:
                                dve.wait_ge(sm("st_made"), g)
                            V.done(dve, dve.tensor_tensor(heads(xd[:]), heads(y[:, 0, gw]),
                                                          dec[:, gh].unsqueeze(2).to_broadcast([P, GH, SP]), ALU.mult),
                                   sm("xd_ready"))
                        dve.wait_ge(sm("seg_summed"), i + 1)
                        seg = bank2(2 + 2 * (i % 2)).rearrange("p (h l) -> p h l", h=GH)
                        if i >= 2:
                            dve.wait_ge(sm("y_made"), i - 1)
                        Mi = M[:, i % 2]
                        V.link(dve, dve.tensor_copy(cb[:, i % 2, :], ps[:, 6 + i % 2, 0:P]))
                        V.done(dve, dve.tensor_tensor(Mi, seg, cst[:, C_CMT:C_CMT + P].unsqueeze(1).to_broadcast([P, GH, P]),
                                                      ALU.min), sm("seg_ready"))
                        if c == 0:
                            dve.wait_ge(sm("st_made"), g + 1)
                            if g:
                                dve.wait_ge(sm("off_made"), g)
                            V.done(dve, dve.tensor_copy(st[:], ps[:, 0, :]), sm("st_ready"))
                        dve.wait_ge(sm("seg_exp"), i + 1)
                        V.done(dve, dve.tensor_tensor(Mi, Mi, cb[:, i % 2, :].unsqueeze(1).to_broadcast([P, GH, P]), ALU.mult),
                               sm("m_ready"))
                        if c == 1:
                            dve.wait_ge(sm("off_made"), g + 1)
                            V.link(dve, dve.tensor_tensor(heads(t5[:]), heads(ps[:, 1, :]),
                                                          ecum[:, gh].unsqueeze(2).to_broadcast([P, GH, SP]), ALU.mult))
                        dve.wait_ge(sm("y_made"), i + 1)
                        if c == 1:
                            V.link(dve, dve.tensor_tensor(y[:, c, gw], t5[:], ps[:, 6 + i % 2, :], ALU.add))
                        else:
                            V.link(dve, dve.tensor_copy(y[:, c, gw], ps[:, 6 + i % 2, :]))
                        V.link(dve, dve.tensor_tensor(heads(t5[:]), heads(xs[:, c, gw]), bcv("d_skip_2")[:, gh].unsqueeze(2)
                                                      .to_broadcast([P, GH, SP]), ALU.mult))
                        V.done(dve, dve.tensor_tensor(y[:, c, gw], y[:, c, gw], t5[:], ALU.add), sm("y_out"))
                    for n in range(4):
                        for t in range(TT):
                            i = 2 * n + t
                            dve.wait_ge(sm("zs_ready"), i + 1)
                            yv = y[:, t, 512 * n:512 * n + 512]
                            V.done(dve, dve.tensor_tensor(yv, yv, zs[:, i % 2, :], ALU.mult), sm("zs_used"))
                            V.link(dve, dve.tensor_tensor(t5[:], yv, yv, ALU.mult))
                            V.link(dve, dve.tensor_reduce(gs[:, t, n:n + 1], t5[:], AX.X, ALU.add))
                    V.done(dve, dve.tensor_scalar(gs[:], gs[:], 1.0 / GW, EPS, ALU.mult, ALU.add), sm("gs_ready"))
                    dve.wait_ge(sm("gs_rms"), 1)
                    V.link(dve, dve.reciprocal(gs[:], gs[:]))
                    for t in range(TT):
                        yv = y[:, t, :].rearrange("p (g q) -> p g q", g=SG)
                        V.link(dve, dve.tensor_tensor(yv, yv, gs[:, t, :].unsqueeze(2).to_broadcast([P, SG, GW]), ALU.mult))

        with ExitStack() as pk:
            yT, mer = xbc[:, 0:2 * KT, :], xbc[:, 2 * KT:, :]
            sig = sb("sig2", [P, KT, SEQ], at=pk)
            otok = sb("otok", [P, TT, D], at=pk)
            with nc.Block() as block:
                @block.sync
                def _(sp):
                    for n in range(SLOTS + M_SSM, len(SLABS2)):
                        load_slab(sp, n, SLABS2[n], "b_")
                    for t in range(TT):
                        sp.wait_ge(sm(f"o_ready{t}"), 1)
                        sp.dma_start(out[t * P:(t + 1) * P, :], otok[:, t, :]).then_inc(sm("out_stored"), 16)
                    sp.wait_ge(sm("out_stored"), 16 * TT)

                @block.tensor
                def _(pe):
                    for i in range(8):
                        bank = i % 4
                        if i >= 4:
                            pe.wait_ge(sm("yT_ready"), 2 * (i - 3))
                        for j in range(2):
                            for t in range(TT):
                                k = 2 * i + j
                                mm = pe.transpose(ps[:, bank, j * SEQ + t * P:j * SEQ + (t + 1) * P],
                                                  y[:, t, k * P:(k + 1) * P], idn)
                        mm.then_inc(sm("y_turned"), 1)
                    def slab(n):
                        pe.wait_ge(sm(f"b_slab_ready{n % SLOTS}"), slab_count(SLABS2, n))
                    pe.wait_ge(sm("yT_ready"), 16)
                    for i in range(2):
                        n = M_SSM + 2 * i
                        slab(n)
                        slab(n + 1)
                        for j in range(4):
                            for k in range(2 * KT):
                                mm = pe.matmul(ps[:, 2 * i + j // 2, (j % 2) * SEQ:(j % 2 + 1) * SEQ],
                                               slots[(n + k // KT) % SLOTS][:, k % KT, j * P:(j + 1) * P], yT[:, k, :],
                                               start=(k == 0), stop=(k == 2 * KT - 1))
                        mm.then_inc(sm("b_slab_used"), 2)
                    for i in range(2):
                        slab(M_GS + i)
                        columns_by_tokens(pe, M_GS + i, 4 + 2 * i).then_inc(sm("b_slab_used"), 1)
                    for i in range(2):
                        pe.wait_ge(sm("mer_first"), 1)
                        slab(M_ATT + i)
                        columns_by_tokens(pe, M_ATT + i, 2 * i, src=azT).then_inc(sm("b_slab_used"), 1)
                    for i in range(2):
                        pe.wait_ge(sm("sig_copied"), 2)
                        slab(M_GA + i)
                        columns_by_tokens(pe, M_GA + i, 4 + 2 * i).then_inc(sm("b_slab_used"), 1)
                    pe.wait_ge(sm("mer_ready"), 1)
                    for i in range(2):
                        slab(M_OUT + i)
                        columns_by_tokens(pe, M_OUT + i, 2 * i, src=mer).then_inc(sm("b_slab_used"), 1)
                    for t in range(TT):
                        pe.wait_ge(sm("x3_ready"), 8)
                        for k in range(KT):
                            mm = pe.transpose(ps[:, 4 + 2 * t + k // 4, (k % 4) * P:(k % 4 + 1) * P],
                                              xT[:, k, t * P:(t + 1) * P], idn)
                        mm.then_inc(sm("o_turned"), 1)

                @block.scalar
                def _(act):
                    for i in range(8):
                        act.wait_ge(sm("y_turned"), i + 1)
                        for j in range(2):
                            kk = 2 * i + j
                            ins = act.activation(yT[:, kk, :], ps[:, i % 4, j * SEQ:(j + 1) * SEQ], ACT.Copy,
                                                 scale=col("ssm_norm_g_2", kk))
                            S.done(act, ins, sm("yT_ready"))
                    for r in range(2):
                        act.wait_ge(sm("b_slab_used"), (M_GS if r == 0 else M_GA) + 2)
                        if r == 1:
                            act.wait_ge(sm("mer_first"), 1)
                        for i in range(2):
                            S.done(act, act.activation(sig[:, 4 * i:4 * i + 4, :].rearrange("p k t -> p (k t)"),
                                                       bank2(4 + 2 * i), ACT.Sigmoid), sm("sig_copied"))
                    act.wait_ge(sm("o_turned"), 2)
                    S.done(act, act.activation(otok[:, 1, :], bank2(6), ACT.Copy), sm("o_ready1"))

                @block.vector
                def _(dve):
                    flat = lambda a: a[:].rearrange("p k t -> p (k t)")
                    acc = ps[:, 0:4, :].rearrange("p b n -> p (b n)")
                    dve.wait_ge(sm("b_slab_used"), M_GS)
                    dve.wait_ge(sm("sig_copied"), 2)
                    V.done(dve, dve.tensor_tensor(flat(mer), acc, flat(sig), ALU.mult), sm("mer_first"))
                    dve.wait_ge(sm("b_slab_used"), M_GA)
                    dve.wait_ge(sm("sig_copied"), 4)
                    V.link(dve, dve.tensor_tensor(flat(sig), acc, flat(sig), ALU.mult))
                    V.done(dve, dve.tensor_tensor(flat(mer), flat(mer), flat(sig), ALU.add), sm("mer_ready"))
                    for k in range(KT):
                        dve.wait_ge(sm("b_slab_used"), M_OUT + 1 + k // 4)
                        V.done(dve, dve.scalar_tensor_tensor(xT[:, k, :], ps[:, k // 2, (k % 2) * SEQ:(k % 2 + 1) * SEQ],
                                                             mod2[:, 16 + k:17 + k], xT[:, k, :], ALU.mult, ALU.add),
                               sm("x3_ready"))
                    dve.wait_ge(sm("o_turned"), 1)
                    V.done(dve, dve.tensor_copy(otok[:, 0, :], bank2(4)), sm("o_ready0"))

def flat_inputs(inputs, ascontiguous):
    shapes = {
        "x": (SEQ, D), "c": (8, P), "c_2": (8, P), "w_ada": (D, 6 * D), "b_ada": (48, P), "g_pre_mix": (8, P),
        "g_post_mix": (8, P), "g_pre_ffn": (8, P), "g_post_ffn": (8, P), "w_in": (D, -1), "b_gates": (1, 8),
        "conv_qk": (32, P), "w_cmp_k": (CMP_BLOCK, AD, AD), "w_cmp_v": (CMP_BLOCK, AD, AD),
        "pos_cmp_k": (CMP_BLOCK, AD), "pos_cmp_v": (CMP_BLOCK, AD), "rel_bias": (NBUCKET, AH), "w_out": (D, D),
        "w_router": (D, NE), "b_router": (1, NE), "w_up": (NE, D, 2 * DE), "b_up": (NE, 2 * DE),
        "w_down": (NE, DE, D), "b_down": (NE, D), "positions_2": (SEQ, 1), "ada_w_2": (D, 3 * D), "ada_b_2": (24, P),
        "norm_g_2": (8, P), "w_in_2": (D, -1), "q_norm_g_2": (1, HD), "k_norm_g_2": (1, HD),
        "idx_k_ln_g_2": (1, ID), "idx_k_ln_b_2": (1, ID), "conv_w_2": (96, P), "conv_b_2": (24, P),
        "dt_bias_2": (1, SH), "a_log_2": (1, SH), "d_skip_2": (1, SH), "ssm_norm_g_2": (16, P),
        "w_branch_att_2": (D, D), "w_branch_ssm_2": (DI, D), "w_out_2": (D, D),
    }
    return {n: ascontiguous(inputs[n]).reshape(s) for n, s in shapes.items()}


def kernel(**inputs):
    import numpy as _np
    import concourse.bacc as _bacc
    from concourse import mybir as _mybir
    from concourse.bass_utils import run_bass_kernel_spmd as _run

    nc = _bacc.Bacc("TRN2", target_bir_lowering=False, num_devices=1)
    given = flat_inputs(inputs, _np.ascontiguousarray)
    arrays, aps = {}, {}
    constants, onehots = shape_constants()
    for name, a in list(given.items()) + [("constants", constants), ("onehots", onehots)]:
        arrays[f"in_{name}_dram"] = a
        aps[name] = nc.dram_tensor(f"in_{name}_dram", a.shape, _mybir.dt.from_np(a.dtype), kind="ExternalInput").ap()
    out = nc.dram_tensor("out_0_dram", (SEQ, D), _mybir.dt.float32, kind="ExternalOutput").ap()
    two_layers(nc, aps, aps["constants"], aps["onehots"], out)
    r = _run(nc, [arrays], core_ids=[0])
    return r.results[0]["out_0_dram"].reshape(1, SEQ, D)
```

```python
import math
from contextlib import ExitStack, nullcontext

import numpy as np
import concourse.bass as bass
from concourse import mybir

F32 = mybir.dt.float32
F32R = mybir.dt.float32r
BF16 = mybir.dt.bfloat16
I32 = mybir.dt.int32
ALU = mybir.AluOpType
ACT = mybir.ActivationFunctionType
AX = mybir.AxisListType

P = 128
SEQ = 256
TT = SEQ // P
D = 1024
KT = D // P
EPS = 1e-6
NEG = -1e30

MH, MD = 4, 128
AH, AD = 8, 64
CMP_BLOCK, CMP_STRIDE = 32, 16
NCMP = (SEQ - CMP_BLOCK) // CMP_STRIDE + 1
NBUCKET, MAXDIST = 32, 128
NE, TOPK = 32, 4
DE = D
LIMIT, ALPHA = 7.0, 1.702

QH, KVH, HD = 8, 2, 128
IH, ID = 4, 64
KEEP = min(256, SEQ // 4)
ROT, IROT = HD // 4, ID // 4
THETA = 500000.0
SH, SP, SG, SN = 32, 64, 4, 128
DI = SH * SP
XBC = DI + 2 * SG * SN

SLOTS, SLOTS2 = 6, 5
RV = 3 * P - 1


def t5_bucket(dist):
    n = np.maximum(dist, 0)
    max_exact = NBUCKET // 2
    nf = np.maximum(n, 1).astype(np.float32)
    large = max_exact + (np.log(nf / np.float32(max_exact)) / np.float32(math.log(MAXDIST / max_exact))
                         * np.float32(NBUCKET - max_exact)).astype(np.int32)
    return np.where(n < max_exact, n, np.minimum(large, NBUCKET - 1))


C_ID, C_ONES, C_TRI, C_TRIS, C_ZERO, C_CM, C_CMT, C_IOTA = (i * P for i in range(8))
C_FREQ = 8 * P
C_NEGC = C_FREQ + ROT // 2 + IROT // 2
C_VALC = C_NEGC + TT * NCMP
C_SEL3 = C_VALC + TT * NCMP
C_LATER = C_SEL3 + NE
C_FLIP = C_LATER + P
C_W = C_FLIP + P
K_RV = 0
K_NEG = RV
K_CMP = 2 * RV
K_W = K_CMP + NCMP * SEQ


def shape_constants():
    c = np.zeros((P, C_W), np.float32)
    i, j = np.arange(P)[:, None], np.arange(P)[None, :]
    c[:, C_ID:C_ID + P] = i == j
    c[:, C_ONES:C_ONES + P] = 1
    c[:, C_TRI:C_TRI + P] = i <= j
    c[:, C_TRIS:C_TRIS + P] = i < j
    c[:, C_LATER:C_LATER + P] = i > j
    c[:, C_FLIP:C_FLIP + P] = i + j == P - 1
    c[:, C_CM:C_CM + P] = np.where(j <= i, 0, NEG)
    c[:, C_CMT:C_CMT + P] = np.where(i <= j, 0, NEG)
    c[:, C_IOTA:C_IOTA + P] = j
    for at, rot in ((C_FREQ, ROT), (C_FREQ + ROT // 2, IROT)):
        c[:, at:at + rot // 2] = np.power(np.float32(THETA), -(np.arange(0, rot, 2, dtype=np.float32) / np.float32(rot)))
    for t in range(TT):
        ok = CMP_STRIDE * np.arange(NCMP)[None, :] + CMP_BLOCK - 1 <= t * P + i
        c[:, C_NEGC + t * NCMP:C_NEGC + (t + 1) * NCMP] = np.where(ok, 0, NEG)
        c[:, C_VALC + t * NCMP:C_VALC + (t + 1) * NCMP] = ok
    c[:96, C_SEL3:C_SEL3 + NE] = np.arange(96)[:, None] % 32 == np.arange(NE)[None, :]
    k = np.zeros((NBUCKET, K_W), np.float32)
    dist = 2 * P - 1 - np.arange(RV)
    b = np.arange(NBUCKET)[:, None]
    k[:, K_RV:K_RV + RV] = (t5_bucket(dist)[None, :] == b) & (dist >= 0)[None, :]
    k[:, K_NEG:K_NEG + RV] = np.where(dist >= 0, 0, NEG)
    end = CMP_STRIDE * np.arange(NCMP) + CMP_BLOCK - 1
    d = np.arange(SEQ)[None, :] - end[:, None]
    k[:, K_CMP:] = (t5_bucket(d).reshape(-1)[None, :] == b)
    return c, k


R1 = {"c": (0, 8), "c_2": (8, 8), "g_pre_mix": (16, 8), "g_post_mix": (24, 8), "g_pre_ffn": (32, 8),
      "g_post_ffn": (40, 8), "norm_g_2": (48, 8), "ssm_norm_g_2": (56, 16), "conv_b_2": (72, 24)}
R2 = {"b_ada": (0, 48), "ada_b_2": (48, 24)}
R3 = {"conv_qk": (0, 32), "conv_w_2": (32, 96)}
COLS = {}
for base, rows in ((0, R1), (96, R2), (168, R3)):
    for name, (at, n) in rows.items():
        COLS[name] = (base + at, n)
NCOLS = 168 + 128

Z_Q, Z_K, Z_V, Z_O, Z_IF, Z_QA, Z_KC, Z_VC, Z_KS, Z_VS, Z_KW, Z_VW, Z_GA = (
    0, 512, 1024, 1536, 2048, 2056, 2568, 2696, 2824, 2952, 3080, 3208, 3336)
SLABS1 = [("w_ada", 0, [(0, 512 * n, 512)]) for n in range(4)]
SLABS1 += [("w_in", 0, [(0, z, 512)]) for z in (Z_Q, Z_K, Z_V, Z_O, Z_QA)]
SLABS1 += [("w_in", 0, [(0, Z_IF, 8), (8, Z_VS, 128), (136, Z_VW, 128), (264, Z_GA, 24)]),
           ("w_in", 0, [(0, Z_KC, 384), (384, Z_KW, 128)])]
SLABS1 += [("w_ada", 0, [(0, 512 * n, 512)]) for n in range(4, 12)]
SLABS1 += [("ada_w_2", 0, [(0, 512 * n, 512)]) for n in range(6)]
SLABS1 += [("w_out", 0, [(0, 512 * n, 512)]) for n in range(2)]
N_ADA, N_IN, N_MOD, N_OUT = 0, 4, 11, 25

P_Q, P_K, P_V, P_ZA, P_QI, P_KI, P_WI, P_ZS, P_XBC, P_DT, P_G = (
    0, 1024, 1280, 1536, 2560, 2816, 2880, 2884, 4932, 8004, 8036)
SLABS2 = [("w_in_2", 0, [(0, c, 512)]) for c in (P_Q, P_Q + 512, P_K)]
SLABS2 += [("w_in_2", 0, [(0, P_QI, 324), (324, P_DT, 32)])]
SLABS2 += [("w_in_2", 0, [(0, P_ZA + 512 * n, 512)]) for n in range(2)]
SLABS2 += [("w_in_2", 0, [(0, P_XBC + 512 * n, 512)]) for n in range(6)]
Z_G = [(P_ZS, P_G + D), (P_ZS + 512, P_G + D + 512), (P_ZS + 1024, P_G), (P_ZS + 1536, P_G + 512)]
for z, gate_at in Z_G:
    SLABS2 += [("w_in_2", 0, [(0, z, 512)]), ("w_in_2", 0, [(0, gate_at, 512)])]
SLABS2 += [("w_branch_att_2", 0, [(0, 512 * n, 512)]) for n in range(2)]
SLABS2 += [("w_branch_ssm_2", D * k, [(0, 512 * n, 512)]) for n in range(2) for k in range(2)]
SLABS2 += [("w_out_2", 0, [(0, 512 * n, 512)]) for n in range(2)]
M_ZA, M_XBC, M_ZS, M_ATT, M_SSM, M_OUT = 4, 6, 12, 20, 22, 26
BC = {"q_norm_g_2": (0, HD), "k_norm_g_2": (HD, HD), "idx_k_ln_g_2": (2 * HD, ID), "idx_k_ln_b_2": (2 * HD + ID, ID),
      "dt_bias_2": (2 * HD + 2 * ID, SH), "a_log_2": (2 * HD + 2 * ID + SH, SH), "d_skip_2": (2 * HD + 2 * ID + 2 * SH, SH)}
TWO_PI_HIGH = 6.28125
TWO_PI_LOW = 2 * math.pi - TWO_PI_HIGH
ROUNDER = 1.5 * 2 ** 23


class Steps:

    def __init__(self, order):
        self.order = order
        self.n = 0
        self.counts = {}

    def link(self, eng, ins):
        self.n += 1
        ins.then_inc(self.order, 1)
        eng.wait_ge(self.order, self.n)

    def done(self, eng, ins, sem):
        n = self.counts.get(sem.name, 0) + 1
        self.counts[sem.name] = n
        ins.then_inc(sem, 1)
        eng.wait_ge(sem, n)


def two_layers(nc, A, cst_in, c32_in, out):
    with ExitStack() as ctx:
        sems = {}

        def sb(name, shape, dt=F32, at=ctx):
            return at.enter_context(nc.sbuf_tensor(name, shape, dt))

        def sm(name):
            if name not in sems:
                sems[name] = nc.alloc_semaphore(name)
            return sems[name]

        def retire(names):
            nc.clear_and_free_semaphores([sems.pop(name) for name in names.split()])
            nc.all_engine_barrier()

        ps = ctx.enter_context(nc.psum_tensor("ps", [P, 8, 512], F32))
        cst = sb("cst", [P, C_W])
        cols = sb("cols", [P, NCOLS])
        ring_low = sb("ring_low", [P, 2, KT, 512])
        xT = sb("xT", [P, KT, SEQ])
        hT = sb("hT", [P, KT, SEQ])
        rstd = sb("rstd", [P, SEQ])
        mod = sb("mod", [P, 48])
        mod2 = sb("mod2", [P, 24])
        silc = sb("silc", [P, 2, KT])
        gain = sb("gain", [P, KT])
        mrow = sb("mrow", [P, 512])
        mrows = sb("mrows", [56, P])
        idn = cst[:, C_ID:C_ID + P]
        ones = cst[:, C_ONES:C_ONES + P]
        slots = [ring_low[:, i] for i in range(2)]

        def more_slots(name, n):
            stack = ctx.enter_context(ExitStack())
            ring_high = sb(name, [P, n - 2, KT, 512], at=stack)
            slots[2:] = [ring_high[:, i] for i in range(n - 2)]
            return stack

        first_ring = more_slots("first_ring", SLOTS)
        rv_dram = nc.dram_tensor("rv_dram", (AH, RV), F32).ap()

        V = Steps(sm("dve_order"))
        S = Steps(sm("act_order"))
        G = Steps(sm("pool_order"))

        def col(name, k):
            at, _ = COLS[name]
            return cols[:, at + k:at + k + 1]

        def colv(name):
            at, n = COLS[name]
            return cols[:, at:at + n]

        def load_slab(sp, n, spec, stream=""):
            slot = n % len(slots)
            if n >= len(slots):
                sp.wait_ge(sm(f"{stream}slab_used"), n - len(slots) + 1)
            name, row, parts = spec
            for at, c0, w in parts:
                src = A[name][row:row + D, c0:c0 + w].rearrange("(k p) n -> p k n", p=P)
                sp.dma_start(slots[slot][:, :, at:at + w], src).then_inc(sm(f"{stream}slab_ready{slot}"), 16)

        def slab_count(specs, n):
            return 16 * sum(len(specs[m][2]) for m in range(n % len(slots), n + 1, len(slots)))

        def tokens_by_columns(pe, n, w, bank):
            for t in range(TT):
                for k in range(KT):
                    mm = pe.matmul(ps[:, bank + t, 0:w], hT[:, k, t * P:(t + 1) * P], slots[n % len(slots)][:, k, 0:w],
                                   start=(k == 0), stop=(k == KT - 1))
            return mm

        def columns_by_tokens(pe, n, bank, src=None):
            src = hT if src is None else src
            for j in range(4):
                for k in range(KT):
                    mm = pe.matmul(ps[:, bank + j // 2, (j % 2) * SEQ:(j % 2 + 1) * SEQ],
                                   slots[n % len(slots)][:, k, j * P:(j + 1) * P], src[:, k, :],
                                   start=(k == 0), stop=(k == KT - 1))
            return mm

        def half_slab(pe, n, j2, bank, src):
            for j in (2 * j2, 2 * j2 + 1):
                for k in range(KT):
                    mm = pe.matmul(ps[:, bank, (j % 2) * SEQ:(j % 2 + 1) * SEQ], slots[n % len(slots)][:, k, j * P:(j + 1) * P],
                                   src[:, k, :], start=(k == 0), stop=(k == KT - 1))
            return mm

        def mod_row(pe, n, which, m, bank):
            q = 32 * (m % 4)
            for k in range(KT):
                mm = pe.matmul(ps[q:q + 1, bank, :], silc[:, which, k:k + 1], slots[n % len(slots)][:, k, :],
                               start=(k == 0), stop=(k == KT - 1))
            mm.then_inc(sm("slab_used"), 1)

        def mod_row_copy(act, n, m, bank):
            q = 32 * (m % 4)
            act.wait_ge(sm("slab_used"), n + 1)
            if m >= 8:
                act.wait_ge(sm(f"mod_rows_in{m % 4}"), 16 * (m // 4 - 1))
            S.done(act, act.activation(mrow[q:q + 1, :], ps[q:q + 1, bank, :], ACT.Copy), sm("mod_row_ready"))

        def mod_row_send(sp, m, at):
            sp.wait_ge(sm("mod_row_ready"), m + 1)
            q = 32 * (m % 4)
            sp.dma_start(mrows[at:at + 4, :], mrow[q:q + 1, :].rearrange("a (j p) -> a j p", p=P))\
                .then_inc(sm(f"mod_rows_in{m % 4}"), 16)

        def bank2(b):
            return ps[:, b:b + 2, :].rearrange("p b n -> p (b n)")

        def norm_squares(act, src, sq, tiles, after=None):
            for i, k in enumerate(tiles):
                if after:
                    act.wait_ge(sm(after[0]), after[1] + i + 1)
                S.done(act, act.activation(sq[:, k, :], src[:, k, :], ACT.Square), sm("sq_ready"))

        def norm_sums(pe, sq, bank, signal, nth):
            for k in range(KT):
                pe.wait_ge(sm("sq_ready"), (nth - 1) * KT + k + 1)
                mm = pe.matmul(ps[:, bank, 0:SEQ], ones, sq[:, k, :], start=(k == 0), stop=(k == KT - 1))
            mm.then_inc(sm(signal), 1)

        def norm_rstd(dve, bank, after):
            dve.wait_ge(*after)
            V.done(dve, dve.tensor_scalar(rstd[:], ps[:, bank, 0:SEQ], 1.0 / D, EPS, ALU.mult, ALU.add), sm("mean_square"))
            dve.wait_ge(sm("rms_ready"), V.counts["mean_square"])
            V.link(dve, dve.reciprocal(rstd[:], rstd[:]))

        def norm_root(act, nth):
            act.wait_ge(sm("mean_square"), nth)
            S.done(act, act.activation(rstd[:], rstd[:], ACT.Sqrt), sm("rms_ready"))

        with ExitStack() as pa:
            att = ctx.enter_context(ExitStack())
            TB = sb("TB", [P, AH, SEQ], at=att)
            cbias = sb("cbias", [P, TT, AH, NCMP], at=att)
            room0 = sb("room0", [P, 2 * AH * SEQ], at=att)
            tbr = room0[:, AH * SEQ:].rearrange("p (s n) -> p s n", s=AH)
            rows1 = sb("rows1", [96, P], at=pa)
            rows2 = sb("rows2", [72, P], at=pa)
            rows3 = sb("rows3", [128, P], at=pa)
            xtok = sb("xtok", [P, TT, D], at=pa)
            first_rows = sb("first_rows", [1, 4 * 512], at=pa)
            c32 = sb("c32", [NBUCKET, K_W], at=pa)
            relb = sb("relb", [NBUCKET, AH], at=pa)
            rv = sb("rv", [AH, RV], at=pa)
            sq = sb("sq", [P, KT, SEQ], at=pa)

            with nc.Block() as block:
                @block.sync
                def _(sp):
                    for rows, where, name in ((rows1, R1, "rows1_in"), (rows2, R2, "rows2_in"), (rows3, R3, "rows3_in")):
                        for vec, (at, n) in where.items():
                            sp.dma_start(rows[at:at + n, :], A[vec]).then_inc(sm("rows_in"), 16)
                    sp.dma_start(xtok[:], A["x"].rearrange("(t p) d -> p t d", p=P)).then_inc(sm("x_in"), 16)
                    for n in range(SLOTS):
                        load_slab(sp, n, SLABS1[n])
                    sp.wait_ge(sm("rv_ready"), 1)
                    sp.dma_start(rv_dram, rv[:]).then_inc(sm("rv_stored"), 16)
                    sp.wait_ge(sm("rv_stored"), 16)
                    for par in range(2):
                        src = bass.AP(rv_dram.tensor, rv_dram.offset + par * RV, [[1, P], [2 * RV, AH // 2], [1, SEQ]])
                        sp.dma_start(tbr[:, par * 4:par * 4 + 4, :], src).then_inc(sm("tb_in"), 16)
                    for n in range(4):
                        load_slab(sp, SLOTS + n, SLABS1[SLOTS + n])

                @block.scalar
                def _(act):
                    act.dma_start(cst[:], cst_in).then_inc(sm("cst_in"), 16)
                    act.dma_start(relb[:], A["rel_bias"]).then_inc(sm("c32_in"), 16)
                    act.dma_start(c32[:], c32_in).then_inc(sm("c32_in"), 16)
                    act.wait_ge(sm("cols_ready"), 1)
                    S.done(act, act.activation(silc[:].rearrange("p a k -> p (a k)"), cols[:, 0:16], ACT.Exp, scale=-1.0),
                           sm("c_exp"))
                    act.wait_ge(sm("x_ready"), 2)
                    norm_squares(act, xT, sq, range(KT))
                    norm_root(act, 1)
                    for n in range(4):
                        act.wait_ge(sm("slab_used"), n + 1)
                        S.done(act, act.activation(first_rows[:, n * 512:(n + 1) * 512], ps[32 * n:32 * n + 1, 5, :], ACT.Copy),
                               sm("mod_row_ready"))
                    for k in range(KT):
                        act.wait_ge(sm("h_scaled"), k + 1)
                        ins = act.activation(hT[:, k, :], hT[:, k, :], ACT.Identity, bias=mod[:, k:k + 1])
                        ins.then_inc(sm("h_ready"), 1)

                @block.tensor
                def _(pe):
                    pe.wait_ge(sm("cst_in"), 16)
                    pe.wait_ge(sm("rows_in"), 16 * (len(R1) + len(R2) + len(R3)))
                    for rows, n, at in ((rows1, 96, 0), (rows2, 72, 96), (rows3, 128, 168)):
                        mm = pe.transpose(ps[:, 4, at:at + n], rows[:, :], cst[0:n, C_ID:C_ID + n])
                    mm.then_inc(sm("rows_turned"), 1)
                    pe.wait_ge(sm("x_in"), 16)
                    for k in range(KT):
                        for t in range(TT):
                            mm = pe.transpose(ps[:, k // 2, (k % 2) * SEQ + t * P:(k % 2) * SEQ + (t + 1) * P],
                                              xtok[:, t, k * P:(k + 1) * P], idn)
                        if k % 4 == 3:
                            mm.then_inc(sm("x_turned"), 1)
                    pe.wait_ge(sm("c32_in"), 32)
                    pe.matmul(ps[0:AH, 6, 0:RV], relb[:], c32[:, K_RV:K_RV + RV], start=True, stop=True)\
                        .then_inc(sm("rv_summed"), 1)
                    for t in range(TT):
                        for i in range(NCMP):
                            at = (t * NCMP + i) * AH
                            mm = pe.matmul(ps[:, 7, at:at + AH], c32[:, K_CMP + i * SEQ + t * P:K_CMP + i * SEQ + (t + 1) * P],
                                           relb[:], start=True, stop=True)
                    mm.then_inc(sm("cbias_summed"), 1)
                    pe.wait_ge(sm("rv_ready"), 1)
                    norm_sums(pe, sq, 6, "x_summed", 1)
                    pe.wait_ge(sm("silc_ready"), 1)
                    for n in range(4):
                        pe.wait_ge(sm(f"slab_ready{n % len(slots)}"), slab_count(SLABS1, n))
                        mod_row(pe, n, 0, n, 5)
                    for n in range(4):
                        pe.wait_ge(sm("mod_row_ready"), n + 1)
                        for k in range(4 * n, 4 * n + 4):
                            mm = pe.matmul(ps[:, 4, k:k + 1], first_rows[:, k * P:(k + 1) * P], cst[0:1, C_ONES:C_ONES + 1],
                                           start=True, stop=True)
                    mm.then_inc(sm("mod_turned"), 1)

                @block.vector
                def _(dve):
                    dve.wait_ge(sm("rows_turned"), 1)
                    V.done(dve, dve.tensor_copy(cols[:], ps[:, 4, 0:NCOLS]), sm("cols_ready"))
                    for h in range(2):
                        dve.wait_ge(sm("x_turned"), h + 1)
                        V.done(dve, dve.tensor_copy(xT[:, 4 * h:4 * h + 4, :].rearrange("p k t -> p (k t)"),
                                                    bank2(2 * h)), sm("x_ready"))
                    flat = silc[:].rearrange("p a k -> p (a k)")
                    dve.wait_ge(sm("c_exp"), 1)
                    V.link(dve, dve.tensor_scalar(flat, flat, 1.0, None, ALU.add))
                    V.link(dve, dve.reciprocal(flat, flat))
                    V.done(dve, dve.tensor_tensor(flat, flat, cols[:, 0:16], ALU.mult), sm("silc_ready"))
                    dve.wait_ge(sm("rv_summed"), 1)
                    V.done(dve, dve.tensor_tensor(rv[:], ps[0:AH, 6, 0:RV], c32[0:AH, K_NEG:K_NEG + RV], ALU.add),
                           sm("rv_ready"))
                    dve.wait_ge(sm("cbias_summed"), 1)
                    for t in range(TT):
                        src = ps[:, 7, t * NCMP * AH:(t + 1) * NCMP * AH].rearrange("p (i hh par) -> p par hh i", hh=4, par=2)
                        neg = cst[:, C_NEGC + t * NCMP:C_NEGC + (t + 1) * NCMP]
                        for par in range(2):
                            V.link(dve, dve.tensor_tensor(cbias[:, t, 4 * par:4 * par + 4, :], src[:, par],
                                                          neg.unsqueeze(1).to_broadcast([P, 4, NCMP]), ALU.add))
                    norm_rstd(dve, 6, (sm("x_summed"), 1))
                    dve.wait_ge(sm("mod_turned"), 1)
                    V.link(dve, dve.tensor_tensor(mod[:, 0:16], ps[:, 4, 0:16], colv("b_ada")[:, 0:16], ALU.add))
                    V.link(dve, dve.scalar_tensor_tensor(gain[:], mod[:, 8:16], 1.0, colv("g_pre_mix"), ALU.add, ALU.mult))
                    for k in range(KT):
                        dve.scalar_tensor_tensor(hT[:, k, :], xT[:, k, :], gain[:, k:k + 1], rstd[:], ALU.mult, ALU.mult)\
                            .then_inc(sm("h_scaled"), 1)

        qkT = sb("qkT", [P, 2 * MH, SEQ], at=att)
        vm = sb("vm", [P, TT, MH * MD], at=att)
        oT = sb("oT", [P, MH, SEQ], at=att)
        qaT = sb("qaT", [P, AH // 2, SEQ], at=att)
        tokz = sb("tokz", [P, TT, 288], at=att)
        kc4 = sb("kc4", [P, 4, SEQ], at=att)
        room1 = sb("room1", [P, 2 * AH * P], at=att)
        wck = room0[:, 0:CMP_BLOCK * AD].rearrange("p (l e) -> p l e", l=CMP_BLOCK // 2)
        wcv = room1[:, 0:CMP_BLOCK // 2 * AD].rearrange("p (l e) -> p l e", l=CMP_BLOCK // 2)
        posT = sb("posT", [P, 2, CMP_BLOCK // 2], at=att)
        bgate = sb("bgate", [P, 8], at=att)
        with ExitStack() as pb:
            zc = sb("zc", [P, 4, SEQ + 3], at=pb)
            cv = sb("cv", [P, 4, SEQ], at=pb)

            with nc.Block() as block:
                @block.sync
                def _(sp):
                    for n in range(SLOTS + 4, SLOTS + N_MOD):
                        load_slab(sp, n, SLABS1[n])

                @block.scalar
                def _(act):
                    act.dma_start(bgate[:], bass.AP(A["b_gates"].tensor, 0, [[0, P], [1, 8]])).then_inc(sm("small_in"), 16)
                    for par in range(2):
                        at = slice(64 * par, 64 * par + 64)
                        every = bass.ds(par, CMP_BLOCK // 2, step=2)
                        for twice in range(2):
                            act.dma_start(wck[at, :, 64 * twice:64 * twice + 64],
                                          A["w_cmp_k"][every].rearrange("l d e -> d l e")).then_inc(sm("small_in"), 16)
                        act.dma_start(wcv[at, :, :], A["w_cmp_v"][every].rearrange("l d e -> d l e"))\
                            .then_inc(sm("small_in"), 16)
                        with nc.allow_non_contiguous_dma("64 x 32 position embedding"):
                            for kind, name in enumerate(("pos_cmp_k", "pos_cmp_v")):
                                act.dma_start(posT[at, kind, :], A[name][every].rearrange("l d -> d l"))\
                                    .then_inc(sm("small_in"), 16)
                    for m in range(2):
                        act.wait_ge(sm("conv_ready"), m + 1)
                        ins = act.activation(qkT[:, 4 * m:4 * m + 4, :], cv[:], ACT.Silu)
                        S.done(act, ins, sm("qk_ready"))
                    for half in range(2):
                        act.wait_ge(sm("tb_flipped"), half + 1)
                        S.done(act, act.activation(TB[:, 4 * half:4 * half + 4, :].rearrange("p s n -> p (s n)"),
                                                   bank2(6 - 6 * half), ACT.Copy), sm("tb_ready"))
                    act.wait_ge(sm("z_copied"), 7)
                    S.link(act, act.activation(oT[:], oT[:], ACT.Sigmoid))
                    S.link(act, act.activation(tokz[:, :, 264:288], tokz[:, :, 264:288], ACT.Sigmoid))
                    act.wait_ge(sm("small_in"), 16 * 11)

                @block.tensor
                def _(pe):
                    for n in range(N_IN, N_MOD):
                        pe.wait_ge(sm(f"slab_ready{n % len(slots)}"), slab_count(SLABS1, n))
                        bank = 2 * (n % 4)
                        if n >= N_IN + 4:
                            pe.wait_ge(sm("z_copied"), n - N_IN - 3)
                        name = n - N_IN
                        if name in (2, 5):
                            mm = tokens_by_columns(pe, n, 512 if name == 2 else 288, bank)
                        else:
                            mm = columns_by_tokens(pe, n, bank)
                        mm.then_inc(sm("slab_used"), 1)
                        if name == 5:
                            pe.wait_ge(sm("tb_in"), 32)
                            for sl in range(AH):
                                if sl % 4 == 0:
                                    pe.wait_ge(sm("z_copied"), 4 + sl // 4)
                                bank = (6 if sl < 4 else 0) + sl % 4 // 2
                                mm = pe.matmul(ps[:, bank, (sl % 2) * SEQ:(sl % 2 + 1) * SEQ], cst[:, C_FLIP:C_FLIP + P],
                                               tbr[:, sl, :], start=True, stop=True)
                                if sl % 4 == 3:
                                    mm.then_inc(sm("tb_flipped"), 1)

                @block.vector
                def _(dve):
                    V.link(dve, dve.memset(zc[:, :, 0:3], 0.0))
                    for name in range(7):
                        n = N_IN + name
                        bank = 2 * (n % 4)
                        dve.wait_ge(sm("slab_used"), n + 1)
                        tiles = bank2(bank).rearrange("p (j t) -> p j t", j=4)
                        if name < 2:
                            V.done(dve, dve.tensor_copy(zc[:, :, 3:], tiles), sm("z_copied"))
                            if name == 1:
                                dve.wait_ge(sm("qk_ready"), 1)
                            for j in range(4):
                                V.link(dve, dve.tensor_scalar(cv[:, j, :], zc[:, j, 0:SEQ], col("conv_qk", 4 * name + j),
                                                              None, ALU.mult))
                                for tap in range(1, 4):
                                    ins = dve.scalar_tensor_tensor(cv[:, j, :], zc[:, j, tap:tap + SEQ],
                                                                   col("conv_qk", 8 * tap + 4 * name + j), cv[:, j, :],
                                                                   ALU.mult, ALU.add)
                                    if j == 3 and tap == 3:
                                        V.done(dve, ins, sm("conv_ready"))
                                    else:
                                        V.link(dve, ins)
                        elif name == 5:
                            V.done(dve, dve.tensor_copy(tokz[:], ps[:, bank:bank + 2, 0:288]), sm("z_copied"))
                        else:
                            dst = {2: vm[:].rearrange("p t n -> p (t n)").rearrange("p (j t) -> p j t", j=4),
                                   3: oT[:], 4: qaT[:], 6: kc4[:]}[name]
                            V.done(dve, dve.tensor_copy(dst, tiles), sm("z_copied"))

        mix = hT
        with ExitStack() as pc:
            gt = sb("gt", [P, TT, 8], at=pc)
            lf = sb("lf", [P, TT, MH], at=pc)
            nab = sb("nab", [P, TT, MH], at=pc)
            F = sb("F", [P, TT, MH], at=pc)
            aa = sb("aa", [P, TT, MH], at=pc)
            nM = sb("nM", [P, TT, MH], at=pc)
            em = sb("em", [P, TT, MH], at=pc)
            den = sb("den", [P, TT, MH], at=pc)
            L1 = sb("L1", [P, AH, SEQ], at=pc)[:]
            LM1 = L1[:, 0:MH, :]
            LM0 = sb("LM0", [P, MH, P], at=pc)
            WT0 = L1[:, MH:, :]
            WT1 = sb("WT1", [P, MH, P], at=pc)
            kin = sb("kin", [P, 2, CMP_BLOCK // 2, 2, NCMP], at=pc)
            kvx = sb("kvx", [P, 2, SEQ], at=pc)
            kcm = sb("kcm", [P, 2, NCMP], at=pc)
            vcm = sb("vcm", [NCMP, 2, AD], at=pc)
            ksw = sb("ksw", [P, 2, SEQ], at=pc)
            Lc = sb("Lc", [P, TT, AH, NCMP], at=pc)
            nmax = sb("nmax", [P, 5, TT, AH], at=pc)
            esum = sb("esum", [P, 5, TT, AH], at=pc)
            L0 = vm[:].rearrange("p t n -> p (t n)").rearrange("p (s n) -> p s n", s=AH)
            PT0 = room0[:].rearrange("p (b s t) -> p b s t", b=2, s=AH)
            PT1 = room1[:].rearrange("p (b s t) -> p b s t", b=2, s=AH)
            PcT = qkT[0:NCMP]
            SLOTLIST = [(par, hh) for par in range(2) for hh in range(4)]
            UNITS = [(b, t) for b in range(2) for t in (1, 0)]
            ROUNDS = [("c", 0, t, 0, q) for t in range(TT) for q in range(2)]
            UNIT_ROUNDS = {(b, t): [("p", b, t, s, q) for s in range(t + 1) for q in range(2)] for b, t in UNITS}
            for u in UNITS:
                ROUNDS += UNIT_ROUNDS[u]
            MODS = list(range(N_MOD, N_OUT))

            def turn_bank(what, t, s, q):
                return 2 if what == "c" else 4 + 2 * s + q if t else q

            def rounds_before(u):
                return 4 + sum(len(UNIT_ROUNDS[UNITS[v]]) for v in range(u))

            def gate_of(c, t):
                return tokz[:, t, 264:288].rearrange("p (hh par c) -> p c par hh", hh=4, par=2)[:, c]

            with nc.Block() as block:
                @block.sync
                def _(sp):
                    sp.wait_ge(sm("z_copied"), 7)
                    for kind in range(2):
                        for half in range(2):
                            sp.dma_start(kvx[64 * half:64 * half + 64, kind, :],
                                         kc4[64 - 64 * half:128 - 64 * half, kind, :]).then_inc(sm("kvx_in"), 16)
                    for b in range(2):
                        for half in range(2):
                            sp.dma_start(ksw[64 * half:64 * half + 64, b, :],
                                         kc4[64 - 64 * half:128 - 64 * half, 2 + b, :]).then_inc(sm("ksw_in"), 16)
                    for m in range(4, 18):
                        n = SLOTS + N_MOD + m - 4
                        if n < len(SLABS1):
                            load_slab(sp, n, SLABS1[n])
                        mod_row_send(sp, m, 4 * (m - 4))

                @block.scalar
                def _(act):
                    copied = [4]

                    def mod_copies(k):
                        for _ in range(k):
                            mod_row_copy(act, N_MOD + copied[0] - 4, copied[0], 3)
                            copied[0] += 1

                    act.wait_ge(sm("nab_ready"), 1)
                    S.link(act, act.activation(nab[:], nab[:], ACT.Exp))
                    S.done(act, act.activation(nab[:], nab[:], ACT.Ln, bias=1.0), sm("ln_ready"))
                    act.wait_ge(sm("running_max"), 1)
                    for h in range(MH):
                        act.activation(LM1[:, h, :], LM1[:, h, :], ACT.Exp, bias=nM[:, 1, h:h + 1])
                        ins = act.activation(LM0[:, h, :], LM0[:, h, :], ACT.Exp, bias=nM[:, 0, h:h + 1])
                    S.done(act, ins, sm("decay_ready"))
                    act.wait_ge(sm("em_in"), 1)
                    S.done(act, act.activation(em[:], em[:], ACT.Exp, scale=-1.0), sm("em_ready"))
                    mod_copies(3)
                    act.wait_ge(sm("w_turned"), 1)
                    S.link(act, act.activation(WT0.rearrange("p h t -> p (h t)"), bank2(4), ACT.Copy))
                    S.done(act, act.activation(WT1[:].rearrange("p h t -> p (h t)"), ps[:, 2, :], ACT.Copy), sm("wt_ready"))
                    act.wait_ge(sm("lc_ready"), 1)
                    S.done(act, act.activation(Lc[:], Lc[:], ACT.Exp), sm("ec_ready"))
                    mod_copies(1)
                    nround = 0

                    def copy_rounds(rounds):
                        nonlocal nround
                        for what, b, t, s, q in rounds:
                            nround += 1
                            act.wait_ge(sm("p_turned"), nround)
                            sl, tk = slice(4 * q, 4 * q + 4), slice(t * P, (t + 1) * P)
                            src = ps[:, turn_bank(what, t, s, q), :]
                            if what == "c":
                                dst, src = PcT[:, sl, tk], src[0:NCMP]
                            else:
                                dst = PT0[:, b, sl, tk] if s == 0 else PT1[:, b, sl, :]
                            S.done(act, act.activation(dst, src.rearrange("p (q t) -> p q t", q=4), ACT.Copy),
                                   sm("pt_ready"))

                    def exps(u):
                        b, t = UNITS[u]
                        act.wait_ge(sm("logits_ready"), u + 1)
                        L = L1 if t else L0
                        for sl in range(AH):
                            ins = act.activation(L[:, sl, :], L[:, sl, :], ACT.Exp, bias=nmax[:, b, t, sl:sl + 1],
                                                 accum_out=esum[:, b, t, sl:sl + 1])
                        S.done(act, ins, sm("exp_ready"))

                    copy_rounds(ROUNDS[:4])
                    for u, counts in ((0, (2, 1)), (2, (3, 4))):
                        exps(u)
                        exps(u + 1)
                        mod_copies(counts[0])
                        copy_rounds(UNIT_ROUNDS[UNITS[u]])
                        copy_rounds(UNIT_ROUNDS[UNITS[u + 1]])
                        mod_copies(counts[1])

                @block.tensor
                def _(pe):
                    def mods(k):
                        for _ in range(k):
                            n = MODS.pop(0)
                            pe.wait_ge(sm(f"slab_ready{n % len(slots)}"), slab_count(SLABS1, n))
                            m = n - N_MOD + 4
                            if m >= 8:
                                pe.wait_ge(sm("mod_row_ready"), m - 3)
                            mod_row(pe, n, 0 if m < 12 else 1, m, 3)

                    for t in (1, 0):
                        w = (t + 1) * P
                        for h in range(MH):
                            dst = ps[:, h // 2, (h % 2) * w:(h % 2) * w + w] if t else ps[:, 2, h * w:h * w + w]
                            mm = pe.matmul(dst, qkT[:, h, t * P:(t + 1) * P], qkT[:, MH + h, 0:w], start=True, stop=True)
                    mm.then_inc(sm("qk_scored"), 1)
                    pe.wait_ge(sm("lf_ready"), 1)
                    tri = cst[:, C_TRI:C_TRI + P]
                    pe.matmul(ps[:, 3, 0:MH], tri, lf[:, 0, :], start=True, stop=True)
                    pe.matmul(ps[:, 3, MH:2 * MH], ones, lf[:, 0, :], start=True, stop=False)
                    pe.matmul(ps[:, 3, MH:2 * MH], tri, lf[:, 1, :], start=False, stop=True).then_inc(sm("f_summed"), 1)
                    pe.wait_ge(sm("kin_ready"), 8)
                    for l in range(CMP_BLOCK // 2):
                        mm = pe.matmul(ps[:, 6, 0:2 * NCMP], wck[:, l, :], kin[:, 0, l].rearrange("p g i -> p (g i)"),
                                       start=(l == 0), stop=(l == CMP_BLOCK // 2 - 1))
                    for g in range(2):
                        for l in range(CMP_BLOCK // 2):
                            mm = pe.matmul(ps[0:NCMP, 7, g * AD:(g + 1) * AD], kin[:, 1, l, g, :], wcv[:, l, :],
                                           start=(l == 0), stop=(l == CMP_BLOCK // 2 - 1))
                    mm.then_inc(sm("compressed"), 1)
                    pe.wait_ge(sm("a_ready"), 1)
                    for h in range(MH):
                        for t in range(TT):
                            mm = pe.matmul(ps[:, 4 + h // 2, (h % 2) * SEQ + t * P:(h % 2) * SEQ + (t + 1) * P],
                                           aa[:, t, h:h + 1].to_broadcast([P, P]), idn, start=True, stop=True)
                    mm.then_inc(sm("a_spread"), 1)
                    pe.wait_ge(sm("kcm_ready"), 1)
                    for par, hh in SLOTLIST:
                        half = slice(64 * par, 64 * par + 64)
                        for t in range(TT):
                            at = (t * 4 + hh) * NCMP
                            mm = pe.matmul(ps[:, 6 + par, at:at + NCMP], qaT[half, hh, t * P:(t + 1) * P],
                                           kcm[half, hh // 2, :], start=True, stop=True)
                    mm.then_inc(sm("c_scored"), 1)
                    mods(3)
                    pe.wait_ge(sm("w_ready"), 2)
                    for h in range(MH):
                        at = (h % 2) * SEQ
                        pe.transpose(ps[:, 4 + h // 2, at:at + P], LM0[:, h, :], idn)
                        pe.transpose(ps[:, 4 + h // 2, at + P:at + SEQ], LM1[:, h, 0:P], idn)
                        mm = pe.transpose(ps[:, 2, h * P:(h + 1) * P], LM1[:, h, P:SEQ], idn)
                    mm.then_inc(sm("w_turned"), 1)
                    mods(1)
                    pe.wait_ge(sm("wt_ready"), 1)
                    for h in range(MH):
                        out_h = ps[:, h // 2, (h % 2) * SEQ:(h % 2 + 1) * SEQ]
                        pe.matmul(out_h, vm[:, 0, h * MD:(h + 1) * MD], WT0[:, h, :], start=True, stop=False)
                        mm = pe.matmul(out_h[:, P:SEQ], vm[:, 1, h * MD:(h + 1) * MD], WT1[:, h, :], start=False, stop=True)
                    mm.then_inc(sm("m_out"), 1)

                    nround = 0

                    def turn(rounds):
                        nonlocal nround
                        for what, b, t, s, q in rounds:
                            if what == "c" and nround:
                                pe.wait_ge(sm("pt_ready"), nround)
                            nround += 1
                            dst = ps[:, turn_bank(what, t, s, q), :]
                            for i in range(4):
                                sl = 4 * q + i
                                if what == "c":
                                    mm = pe.transpose(dst[0:NCMP, i * P:(i + 1) * P], Lc[:, t, sl, :], idn)
                                else:
                                    L = L1 if t else L0
                                    mm = pe.transpose(dst[:, i * P:(i + 1) * P], L[:, sl, s * P:(s + 1) * P], idn)
                            mm.then_inc(sm("p_turned"), 1)

                    def scores(u):
                        b, t = UNITS[u]
                        w = (t + 1) * P
                        if u == 0:
                            pe.wait_ge(sm("ksw_in"), 64)
                            pe.wait_ge(sm("wt_ready"), 1)
                            pe.wait_ge(sm("c_copied"), 1)
                        if u == 1:
                            pe.wait_ge(sm("m_done"), 1)
                        if u >= 2:
                            pe.wait_ge(sm("pt_ready"), rounds_before(u - 1))
                        for sl, (par, hh) in enumerate(SLOTLIST):
                            half = slice(64 * par, 64 * par + 64)
                            k = kc4[half, 2 + b, 0:w] if hh // 2 == par else ksw[half, b, 0:w]
                            at = sl * w
                            dst = ps[:, (4 if t else 0) + at // 512, at % 512:at % 512 + w]
                            mm = pe.matmul(dst, qaT[half, hh, t * P:(t + 1) * P], k, start=True, stop=True)
                        mm.then_inc(sm("scored"), 1)

                    scores(0)
                    scores(1)
                    pe.wait_ge(sm("pc_ready"), 1)
                    turn(ROUNDS[:4])
                    def turn_unit(u):
                        pe.wait_ge(sm("probs_ready"), u + 1)
                        turn(UNIT_ROUNDS[UNITS[u]])

                    mods(2)
                    turn_unit(0)
                    turn_unit(1)
                    mods(1)
                    scores(2)
                    scores(3)
                    mods(3)
                    turn_unit(2)
                    turn_unit(3)
                    mods(4)
                    for q in range(4):
                        pe.wait_ge(sm(f"mod_rows_in{q}"), 16 * len(range(4 + q, 18, 4)))
                    pe.wait_ge(sm("pt_ready"), len(ROUNDS))
                    pe.transpose(ps[:, 6, 0:56], mrows[:], cst[0:56, C_ID:C_ID + 56]).then_inc(sm("mod_turned"), 1)
                    for sl, (par, hh) in enumerate(SLOTLIST):
                        half = slice(64 * par, 64 * par + 64)
                        out_h = ps[half, hh // 2, (hh % 2) * SEQ:(hh % 2 + 1) * SEQ]
                        g = hh // 2
                        for b in range(2):
                            v0 = 8 + 128 * b + AD * g
                            pe.matmul(out_h, tokz[:, 0, v0:v0 + AD], PT0[:, b, sl, :], start=(b == 0), stop=False)
                            pe.matmul(out_h[:, P:SEQ], tokz[:, 1, v0:v0 + AD], PT1[:, b, sl, :], start=False, stop=False)
                        mm = pe.matmul(out_h, vcm[:, g, :], PcT[:, sl, :], start=False, stop=True)
                    mm.then_inc(sm("a_out"), 1)

                @block.vector
                def _(dve):
                    f = gt[:, :, MH:8]
                    V.link(dve, dve.tensor_tensor(gt[:], tokz[:, :, 0:8], bgate[:].unsqueeze(1).to_broadcast([P, TT, 8]),
                                                  ALU.add))
                    V.done(dve, dve.scalar_tensor_tensor(nab[:], f, -1.0, f, ALU.mult, ALU.min), sm("nab_ready"))
                    dve.wait_ge(sm("kvx_in"), 64)
                    for kind in range(2):
                        for par in range(2):
                            half = slice(64 * par, 64 * par + 64)
                            for g in range(2):
                                src = (kc4 if g == par else kvx)[half, kind, par:par + 1]
                                windows = bass.AP(src.tensor, src.offset,
                                                  [list(src.ap[0]), [2, CMP_BLOCK // 2], [CMP_STRIDE, NCMP]])
                                V.done(dve, dve.tensor_tensor(kin[half, kind, :, g, :], windows, posT[half, kind, :]
                                                              .unsqueeze(2).to_broadcast([64, CMP_BLOCK // 2, NCMP]),
                                                              ALU.add), sm("kin_ready"))
                    dve.wait_ge(sm("ln_ready"), 1)
                    V.done(dve, dve.scalar_tensor_tensor(lf[:], f, 0.0, nab[:], ALU.min, ALU.subtract), sm("lf_ready"))
                    dve.wait_ge(sm("f_summed"), 1)
                    Ff = F[:].rearrange("p t h -> p (t h)")
                    V.link(dve, dve.tensor_copy(Ff, ps[:, 3, 0:2 * MH]))
                    V.done(dve, dve.tensor_tensor(aa[:], gt[:, :, 0:MH], F[:], ALU.subtract), sm("a_ready"))
                    dve.wait_ge(sm("compressed"), 1)
                    for g in range(2):
                        V.link(dve, dve.tensor_copy(kcm[:, g, :], ps[:, 6, g * NCMP:(g + 1) * NCMP]))
                        ins = dve.tensor_copy(vcm[:, g, :], ps[0:NCMP, 7, g * AD:(g + 1) * AD])
                        (V.done(dve, ins, sm("kcm_ready")) if g else V.link(dve, ins))
                    dve.wait_ge(sm("a_spread"), 1)
                    spread = bank2(4).rearrange("p (h s) -> p h s", h=MH)
                    V.link(dve, dve.tensor_tensor(LM1, spread, cst[:, C_ZERO:C_ZERO + SEQ].unsqueeze(1)
                                                  .to_broadcast([P, MH, SEQ]), ALU.add))
                    V.link(dve, dve.tensor_tensor(LM0[:], spread[:, :, 0:P], cst[:, C_CM:C_CM + P].unsqueeze(1)
                                                  .to_broadcast([P, MH, P]), ALU.add))
                    V.link(dve, dve.tensor_reduce(nM[:, 1, :], LM1, AX.X, ALU.max, negate=True))
                    V.done(dve, dve.tensor_reduce(nM[:, 0, :], LM0[:], AX.X, ALU.max, negate=True), sm("running_max"))
                    V.done(dve, dve.tensor_tensor(em[:], F[:], nM[:], ALU.subtract), sm("em_in"))
                    dve.wait_ge(sm("c_scored"), 1)
                    for par in range(2):
                        sc = ps[:, 6 + par, 0:TT * 4 * NCMP].rearrange("p (t n) -> p t n", t=TT)
                        out_l = Lc[:, :, 4 * par:4 * par + 4, :].rearrange("p t s i -> p t (s i)")
                        in_b = cbias[:, :, 4 * par:4 * par + 4, :].rearrange("p t s i -> p t (s i)")
                        ins = dve.scalar_tensor_tensor(out_l, sc, AD ** -0.5, in_b, ALU.mult, ALU.add)
                        (V.done(dve, ins, sm("c_copied")) if par else V.link(dve, ins))
                    flat = Lc[:].rearrange("p t s i -> p (t s) i")
                    V.link(dve, dve.tensor_reduce(nmax[:, 2].rearrange("p t s -> p (t s)"), flat, AX.X, ALU.max))
                    V.done(dve, dve.tensor_tensor(flat, flat, nmax[:, 2].rearrange("p t s -> p (t s)").unsqueeze(2)
                                                  .to_broadcast([P, TT * AH, NCMP]), ALU.subtract), sm("lc_ready"))
                    dve.wait_ge(sm("decay_ready"), 1)
                    dve.wait_ge(sm("em_ready"), 1)
                    for t in (1, 0):
                        LM = LM1 if t else LM0[:]
                        sc = bank2(0).rearrange("p (h s) -> p h s", h=MH) if t else ps[:, 2, :].rearrange("p (h s) -> p h s", h=MH)
                        V.link(dve, dve.scalar_tensor_tensor(LM, sc, MD ** -0.5, LM, ALU.mult, ALU.mult))
                        V.link(dve, dve.tensor_reduce(den[:, t, :], LM, AX.X, ALU.add))
                        V.link(dve, dve.scalar_tensor_tensor(den[:, t, :], den[:, t, :], -1.0, den[:, t, :], ALU.mult, ALU.max))
                        V.link(dve, dve.tensor_tensor(den[:, t, :], den[:, t, :], em[:, t, :], ALU.max))
                        V.link(dve, dve.reciprocal(den[:, t, :], den[:, t, :]))
                        V.done(dve, dve.tensor_tensor(LM, LM, den[:, t, :].unsqueeze(2)
                                                      .to_broadcast([P, MH, (t + 1) * P]), ALU.mult), sm("w_ready"))
                    dve.wait_ge(sm("ec_ready"), 1)
                    for t in range(TT):
                        ok = cst[:, C_VALC + t * NCMP:C_VALC + (t + 1) * NCMP].unsqueeze(1).to_broadcast([P, AH, NCMP])
                        V.link(dve, dve.tensor_tensor(Lc[:, t], Lc[:, t], ok, ALU.mult))
                        V.link(dve, dve.tensor_reduce(esum[:, 2, t, :], Lc[:, t], AX.X, ALU.add))
                        V.link(dve, dve.tensor_scalar(esum[:, 2, t, :], esum[:, 2, t, :], 1e-30, None, ALU.max))
                        V.link(dve, dve.reciprocal(esum[:, 2, t, :], esum[:, 2, t, :]))
                        coef = esum[:, 2, t, :].rearrange("p (par hh) -> p par hh", par=2)
                        V.link(dve, dve.tensor_tensor(coef, coef, gate_of(0, t), ALU.mult))
                        ins = dve.tensor_tensor(Lc[:, t], Lc[:, t], esum[:, 2, t, :].unsqueeze(2)
                                                .to_broadcast([P, AH, NCMP]), ALU.mult)
                        (V.done(dve, ins, sm("pc_ready")) if t == TT - 1 else V.link(dve, ins))
                    dve.wait_ge(sm("m_out"), 1)
                    V.done(dve, dve.tensor_tensor(mix[:, 0:MH, :].rearrange("p k t -> p (k t)"), bank2(0),
                                                  oT[:].rearrange("p k t -> p (k t)"), ALU.mult), sm("m_done"))

                    def logits(u):
                        b, t = UNITS[u]
                        w = (t + 1) * P
                        dve.wait_ge(sm("scored"), u + 1)
                        if u >= 2:
                            need = sum(len(UNIT_ROUNDS[UNITS[v]]) for v in range(u - 1)) + 4
                            dve.wait_ge(sm("p_turned"), need)
                        L = L1 if t else L0
                        sc = (ps[:, 4:8, :] if t else ps[:, 0:2, :]).rearrange("p b n -> p (b n)")\
                            .rearrange("p (s n) -> p s n", s=AH)
                        V.link(dve, dve.scalar_tensor_tensor(L, sc, AD ** -0.5, TB[:, :, SEQ - w:SEQ], ALU.mult, ALU.add))
                        V.done(dve, dve.tensor_reduce(nmax[:, b, t, :], L, AX.X, ALU.max, negate=True),
                               sm("logits_ready"))

                    def probs(u):
                        b, t = UNITS[u]
                        L = L1 if t else L0
                        dve.wait_ge(sm("exp_ready"), u + 1)
                        es = esum[:, b, t, :]
                        V.link(dve, dve.reciprocal(es, es))
                        coef = es.rearrange("p (par hh) -> p par hh", par=2)
                        V.link(dve, dve.tensor_tensor(coef, coef, gate_of(1 + b, t), ALU.mult))
                        V.done(dve, dve.tensor_tensor(L, L, es.unsqueeze(2).to_broadcast([P, AH, (t + 1) * P]),
                                                      ALU.mult), sm("probs_ready"))

                    logits(0)
                    logits(1)
                    probs(0)
                    probs(1)
                    logits(2)
                    logits(3)
                    probs(2)
                    probs(3)
                    dve.wait_ge(sm("mod_turned"), 2)
                    V.link(dve, dve.tensor_tensor(mod[:, 16:48], ps[:, 6, 0:32], colv("b_ada")[:, 16:48], ALU.add))
                    V.link(dve, dve.tensor_tensor(mod2[:], ps[:, 6, 32:56], colv("ada_b_2"), ALU.add))
                    dve.wait_ge(sm("a_out"), 1)
                    V.done(dve, dve.tensor_copy(mix[:, MH:KT, :].rearrange("p k t -> p (k t)"), bank2(0)), sm("mix_ready"))

        att.close()
        with ExitStack() as pd:
            yT = sb("yT", [P, KT, SEQ], at=pd)
            sq = sb("sqd", [P, KT, SEQ], at=pd)
            flatten = lambda a: a[:].rearrange("p k t -> p (k t)")
            with nc.Block() as block:
                @block.tensor
                def _(pe):
                    for n in range(N_OUT, N_OUT + 2):
                        pe.wait_ge(sm(f"slab_ready{n % len(slots)}"), slab_count(SLABS1, n))
                        columns_by_tokens(pe, n, 2 * (n - N_OUT), src=mix).then_inc(sm("slab_used"), 1)
                    norm_sums(pe, sq, 4, "x_summed", 2)
                    norm_sums(pe, sq, 5, "x_summed", 3)

                @block.scalar
                def _(act):
                    for h in range(2):
                        act.wait_ge(sm("y_copied"), h + 1)
                        norm_squares(act, yT, sq, range(4 * h, 4 * h + 4))
                    norm_root(act, 2)
                    norm_squares(act, xT, sq, range(KT), ("x1_ready", 0))
                    norm_root(act, 3)
                    for k in range(KT):
                        act.wait_ge(sm("h_scaled"), KT + k + 1)
                        act.activation(hT[:, k, :], hT[:, k, :], ACT.Identity, bias=mod[:, 24 + k:25 + k])\
                            .then_inc(sm("h_ready"), 1)

                @block.vector
                def _(dve):
                    for h in range(2):
                        dve.wait_ge(sm("slab_used"), N_OUT + h + 1)
                        V.done(dve, dve.tensor_copy(yT[:, 4 * h:4 * h + 4, :].rearrange("p k t -> p (k t)"), bank2(2 * h)),
                               sm("y_copied"))
                    V.link(dve, dve.tensor_tensor(gain[:], mod[:, 16:24], colv("g_post_mix"), ALU.mult))
                    norm_rstd(dve, 4, (sm("x_summed"), 2))
                    for k in range(KT):
                        V.link(dve, dve.scalar_tensor_tensor(yT[:, k, :], yT[:, k, :], gain[:, k:k + 1], rstd[:],
                                                             ALU.mult, ALU.mult))
                        V.done(dve, dve.tensor_tensor(xT[:, k, :], xT[:, k, :], yT[:, k, :], ALU.add), sm("x1_ready"))
                    V.link(dve, dve.scalar_tensor_tensor(gain[:], mod[:, 32:40], 1.0, colv("g_pre_ffn"), ALU.add, ALU.mult))
                    norm_rstd(dve, 5, (sm("x_summed"), 3))
                    for k in range(KT):
                        dve.scalar_tensor_tensor(hT[:, k, :], xT[:, k, :], gain[:, k:k + 1], rstd[:], ALU.mult, ALU.mult)\
                            .then_inc(sm("h_scaled"), 1)
        first_ring.close()

        retire("""a_out a_ready a_spread c_copied c_scored compressed decay_ready ec_ready em_in em_ready exp_ready
                  f_summed kcm_ready kin_ready ksw_in kvx_in lc_ready lf_ready ln_ready logits_ready m_done m_out mix_ready
                  nab_ready p_turned pc_ready probs_ready pt_ready qk_scored running_max w_ready w_turned wt_ready
                  conv_ready qk_ready small_in z_copied c_exp silc_ready rows_in rows_turned rv_ready rv_stored
                  rv_summed""")
        STAGES = 4
        SLABS = 12
        raw = ring_low[:].rearrange("p s k n -> p (s k n)").rearrange("p (s n) -> p s n", s=STAGES)
        EXPERT_SEMS = ("b3_in router_in h2_turned h2t_ready routed sel_ready places_summed gate_ready gate_turned gt_ready "
                       "bias_summed b_part b_rest h2l_ready router_logits router_exp gate_high pm_ready gathered xg_ready act_ready act_turned "
                       "pm_turned pmT_ready gr_ready ye_high ye_low added aT_high aT_low scattered glu_ready sig_ready "
                       "steps slab_done w_high w_low w_low_pool filled "
                       "raw_in0 raw_in1 raw_in2 raw_in3").split()
        yacc = hT
        moe = ctx.enter_context(ExitStack())
        h2h = sb("h2h", [P, TT, D], F32R, at=moe)
        h2l = sb("h2l", [P, TT, D], F32R, at=moe)
        place = sb("place", [P, TT, NE], at=moe)
        gate = sb("gate", [P, TT, NE], at=moe)
        gate2 = sb("gate2", [P, TT, NE, 2], F32R, at=moe)
        idr = sb("idr", [P, P], F32R, at=moe)
        bup = sb("bup", [96, 2 * DE], BF16, at=moe)
        sel3 = sb("sel3", [96, NE], BF16, at=moe)
        flag = sb("flag", [1, 1], I32, at=moe)

        def load_expert(sp, e, j, sem):
            dst = raw[:, j % STAGES, :]
            if j < 8:
                h, kp = j // 4, j % 4
                for q in range(2):
                    src = A["w_up"][bass.ds(e, 1), (2 * kp + q) * P:(2 * kp + q + 1) * P, :]\
                        .rearrange("a p (c n) -> p (a c) n", c=2)[:, :, 512 * h:512 * h + 512]
                    sp.dma_start(dst[:, q * D:(q + 1) * D].rearrange("p (c n) -> p c n", c=2), src).then_inc(sem, 16)
            else:
                src = A["w_down"][bass.ds(e, 1), 2 * (j - 8) * P:2 * (j - 7) * P, :].rearrange("a (f p) n -> p (a f) n", p=P)
                sp.dma_start(dst.rearrange("p (f n) -> p f n", f=2), src).then_inc(sem, 16)

        def loads_counted(e, j):
            q, r = divmod(j, SLABS)
            return (e + q) * 80 + (32, 64, 80)[r // STAGES]

        with ExitStack() as pe_:
            wr = sb("wr", [P, KT, NE], at=pe_)
            br = sb("br", [1, NE], at=pe_)
            bdn = sb("bdn", [NE, D], at=pe_)
            b3 = sb("b3", [96, 2 * DE], at=pe_)
            lg = sb("lg", [P, TT, NE + 4], at=pe_)
            rep = sb("rep", [P, TT, NE + 4], at=pe_)
            top = sb("top", [P, TT, 8], at=pe_)
            sel = sb("sel", [P, TT, NE], at=pe_)
            gsum = sb("gsum", [P, TT], at=pe_)
            gT = sb("gT", [NE, SEQ], at=pe_)
            cnt = sb("cnt", [1, NE], at=pe_)
            fl = sb("fl", [1, 1], at=pe_)
            with nc.Block() as block:
                @block.sync
                def _(sp):
                    for part in range(3):
                        sp.dma_start(b3[32 * part:32 * part + 32, :], A["b_up"]).then_inc(sm("b3_in"), 16)
                    sp.dma_start(wr[:], A["w_router"].rearrange("(k p) e -> p k e", p=P)).then_inc(sm("router_in"), 16)
                    sp.dma_start(br[:], A["b_router"]).then_inc(sm("router_in"), 16)
                    sp.dma_start(bdn[:], A["b_down"]).then_inc(sm("router_in"), 16)
                    for j in range(STAGES):
                        load_expert(sp, 0, j, sm(f"raw_in{j}"))

                @block.tensor
                def _(pe):
                    for t in range(TT):
                        for k in range(KT):
                            mm = pe.transpose(ps[:, 2 * t + k // 4, (k % 4) * P:(k % 4 + 1) * P],
                                              hT[:, k, t * P:(t + 1) * P], idn)
                        mm.then_inc(sm("h2_turned"), 1)
                    pe.wait_ge(sm("router_in"), 48)
                    for t in range(TT):
                        dst = ps[:, 4, t * NE:(t + 1) * NE]
                        for k in range(KT):
                            pe.matmul(dst, hT[:, k, t * P:(t + 1) * P], wr[:, k, :], start=(k == 0), stop=False)
                        mm = pe.matmul(dst, cst[0:1, C_ONES:C_ONES + P], br[:], start=False, stop=True)
                    mm.then_inc(sm("routed"), 1)
                    pe.wait_ge(sm("sel_ready"), 1)
                    tris = cst[:, C_TRIS:C_TRIS + P]
                    pe.matmul(ps[:, 5, 0:NE], tris, sel[:, 0, :], start=True, stop=True)
                    pe.matmul(ps[:, 5, NE:2 * NE], ones, sel[:, 0, :], start=True, stop=False)
                    pe.matmul(ps[:, 5, NE:2 * NE], tris, sel[:, 1, :], start=False, stop=True)
                    pe.matmul(ps[0:1, 5, 2 * NE:3 * NE], cst[:, C_ONES:C_ONES + 1], sel[:, 0, :], start=True, stop=False)
                    pe.matmul(ps[0:1, 5, 2 * NE:3 * NE], cst[:, C_ONES:C_ONES + 1], sel[:, 1, :], start=False, stop=True)\
                        .then_inc(sm("places_summed"), 1)
                    pe.wait_ge(sm("gate_ready"), 1)
                    for t in range(TT):
                        mm = pe.transpose(ps[0:NE, 6, t * P:(t + 1) * P], gate[:, t, :], idn)
                    mm.then_inc(sm("gate_turned"), 1)
                    pe.wait_ge(sm("h2l_ready"), TT)
                    pe.wait_ge(sm("gt_ready"), 1)
                    for k in range(KT):
                        mm = pe.matmul(ps[:, k // 2, (k % 2) * SEQ:(k % 2 + 1) * SEQ], bdn[:, k * P:(k + 1) * P], gT[:],
                                       start=True, stop=True)
                    mm.then_inc(sm("bias_summed"), 1)

                @block.gpsimd
                def _(pool):
                    for r, at in ((1, slice(0, 96)), (2, slice(64, 96))):
                        pool.wait_ge(sm("b_part"), r)
                        G.done(pool, pool.tensor_tensor(b3[at], b3[at], bup[at], ALU.subtract), sm("b_rest"))

                @block.scalar
                def _(act):
                    for t in range(TT):
                        act.wait_ge(sm("h2_turned"), t + 1)
                        S.done(act, act.activation(h2h[:, t, :], bank2(2 * t), ACT.Copy), sm("h2t_ready"))
                    act.wait_ge(sm("b3_in"), 48)
                    S.done(act, act.activation(bup[:], b3[:], ACT.Copy), sm("b_part"))
                    act.wait_ge(sm("router_logits"), 1)
                    S.done(act, act.activation(rep[:], rep[:], ACT.Exp), sm("router_exp"))
                    act.wait_ge(sm("gate_ready"), 1)
                    S.done(act, act.activation(gate2[:, :, :, 0], gate[:], ACT.Copy), sm("gate_high"))
                    act.wait_ge(sm("b_rest"), 1)
                    S.link(act, act.activation(bup[32:64, :], b3[32:64, :], ACT.Copy))
                    S.done(act, act.activation(bup[64:96, :], b3[64:96, :], ACT.Copy), sm("b_part"))
                    act.wait_ge(sm("b_rest"), 2)
                    S.link(act, act.activation(bup[64:96, :], b3[64:96, :], ACT.Copy))

                @block.vector
                def _(dve):
                    V.link(dve, dve.tensor_copy(sel3[:], cst[0:96, C_SEL3:C_SEL3 + NE]))
                    V.link(dve, dve.memset(lg[:, :, NE:], -2e38))
                    V.link(dve, dve.tensor_copy(idr[:], idn))
                    for t in range(TT):
                        dve.wait_ge(sm("h2t_ready"), t + 1)
                        V.done(dve, dve.tensor_tensor(h2l[:, t, :], bank2(2 * t), h2h[:, t, :].bitcast(F32), ALU.subtract),
                               sm("h2l_ready"))
                    dve.wait_ge(sm("routed"), 1)
                    V.link(dve, dve.tensor_copy(lg[:, :, 0:NE], ps[:, 4, 0:TT * NE].rearrange("p (t e) -> p t e", t=TT)))
                    for t in range(TT):
                        V.link(dve, dve.max(top[:, t, :], lg[:, t, 0:NE]))
                        V.link(dve, dve.memset(top[:, t, TOPK:], -2e38))
                        V.link(dve, dve.match_replace(rep[:, t, :], top[:, t, :], lg[:, t, :], -3e38))
                    V.done(dve, dve.tensor_single_scalar(sel[:], rep[:, :, 0:NE], -3e38, ALU.is_equal), sm("sel_ready"))
                    V.done(dve, dve.tensor_tensor(rep[:], lg[:], top[:, :, 0:1].to_broadcast([P, TT, NE + 4]),
                                                  ALU.subtract), sm("router_logits"))
                    dve.wait_ge(sm("router_exp"), 1)
                    V.link(dve, dve.tensor_tensor(rep[:, :, 0:NE], rep[:, :, 0:NE], sel[:], ALU.mult))
                    V.link(dve, dve.tensor_reduce(gsum[:], rep[:, :, 0:NE], AX.X, ALU.add))
                    V.link(dve, dve.reciprocal(gsum[:], gsum[:]))
                    V.done(dve, dve.tensor_tensor(gate[:], rep[:, :, 0:NE], gsum[:].unsqueeze(2)
                                                  .to_broadcast([P, TT, NE]), ALU.mult), sm("gate_ready"))
                    dve.wait_ge(sm("places_summed"), 1)
                    pv = place[:]
                    V.link(dve, dve.scalar_tensor_tensor(pv, ps[:, 5, 0:TT * NE].rearrange("p (t e) -> p t e", t=TT), 1.0,
                                                         sel[:], ALU.add, ALU.mult))
                    V.link(dve, dve.tensor_scalar(pv, pv, 1.0, None, ALU.subtract))
                    V.link(dve, dve.tensor_reduce(fl[:], ps[0:1, 5, 2 * NE:3 * NE], AX.X, ALU.max))
                    V.link(dve, dve.tensor_single_scalar(flag[:], fl[:], float(P), ALU.is_gt))
                    dve.wait_ge(sm("gate_high"), 1)
                    V.link(dve, dve.tensor_tensor(gate2[:, :, :, 1], gate[:], gate2[:, :, :, 0].bitcast(F32), ALU.subtract))
                    dve.wait_ge(sm("gate_turned"), 1)
                    V.done(dve, dve.tensor_copy(gT[:], ps[0:NE, 6, 0:SEQ]), sm("gt_ready"))
                    dve.wait_ge(sm("bias_summed"), 1)
                    V.link(dve, dve.tensor_copy(yacc[:].rearrange("p k t -> p (k t)"),
                                                ps[:, 0:4, :].rearrange("p b n -> p (b n)")))

        high = sb("high", [P, STAGES, 2 * DE], F32R, at=moe)
        low = sb("low", [P, STAGES, 2 * DE], F32R, at=moe)
        pm = sb("pm", [P, TT, P], F32R, at=moe)
        pmT = sb("pmT", [P, SEQ], F32R, at=moe)
        gr = sb("gr", [P, 1], at=moe)
        xh = sb("xh", [P, KT, P], F32R, at=moe)
        xl = sb("xl", [P, KT, P], F32R, at=moe)
        gl = sb("gl", [P, DE], at=moe)
        li = sb("li", [P, DE], at=moe)
        sg = sb("sg", [P, DE], at=moe)
        ah = sb("ah", [P, KT, P], F32R, at=moe)
        al = sb("al", [P, KT, P], F32R, at=moe)
        yh = sb("yh", [P, D], F32R, at=moe)
        yl = sb("yl", [P, D], F32R, at=moe)
        iota = cst[:, C_IOTA:C_IOTA + P]
        LEAD = STAGES - 1
        POOL_SLABS = (3, 6, 10)
        DVE_SLABS = tuple(j for j in range(SLABS) if j not in POOL_SLABS)

        def experts_block(block, tag, base, first_loaded, condition):
            s = lambda name: sm(tag + name)
            LINKS = 4

            def slabs_done(e, n):
                return e * SLABS + n + 1

            def wait_low(eng, e, j):
                q, r = divmod(j, SLABS)
                if r in POOL_SLABS:
                    eng.wait_ge(s("w_low_pool"), (e + q) * len(POOL_SLABS) + POOL_SLABS.index(r) + 1)
                else:
                    eng.wait_ge(s("w_low"), (e + q) * len(DVE_SLABS) + DVE_SLABS.index(r) + 1)

            def wait_place(eng, e, j):
                if isinstance(e, int) and e == 0 and j < STAGES:
                    return
                eng.wait_ge(s("slab_done"), slabs_done(e, j - STAGES + 1))

            def low_part(eng, e, j, ready):
                eng.wait_ge(s("w_high"), e * SLABS + j + 1)
                wait_place(eng, e, j)
                sl = j % STAGES
                eng.tensor_tensor(low[:, sl, :], raw[:, sl, :], high[:, sl, :].bitcast(F32), ALU.subtract)\
                    .then_inc(s(ready), 1)

            @block.sync
            def _(sp):
                with condition(sp):
                    if not first_loaded:
                        for j in range(STAGES):
                            load_expert(sp, 0, j, s(f"raw_in{j}"))

                    def follow(e, j):
                        wait_low(sp, e, j)
                        n = j + STAGES
                        load_expert(sp, e + n // SLABS, n % SLABS, s(f"raw_in{n % STAGES}"))

                    with sp.Fori(0, NE - 1) as e:
                        for j in range(SLABS):
                            follow(e, j)
                    for j in range(SLABS - STAGES):
                        follow(NE - 1, j)

            @block.gpsimd
            def _(pool):
                with condition(pool):
                    with pool.Fori(0, NE) as e:
                        for j in POOL_SLABS:
                            low_part(pool, e, j, "w_low_pool")

            @block.tensor
            def _(pe):
                def gather(n, rounds):
                    if rounds[0] == 0:
                        pe.wait_ge(s("pm_ready"), n + 1)
                    for r in rounds:
                        half, part = r // 2, (h2h, h2l)[r % 2]
                        if r >= 2:
                            pe.wait_ge(s("xg_ready"), n * 4 + r - 1)
                        for q in range(4):
                            k = 4 * half + q
                            for t in range(TT):
                                mm = pe.matmul(ps[:, r % 2, q * P:(q + 1) * P], part[:, t, k * P:(k + 1) * P], pm[:, t, :],
                                               start=(t == 0), stop=(t == TT - 1))
                                if isinstance(n, int) and n == 0 and (r, q, t) == (0, 0, 0):
                                    mm.then_inc(s("slab_done"), 1)
                        mm.then_inc(s("gathered"), 1)

                def scatter(e, rounds):
                    for r in rounds:
                        if r == 0:
                            pe.wait_ge(s("ye_low"), e * 2 + 3)
                        if r >= 2:
                            pe.wait_ge(s("added"), e * 4 + r - 1)
                        for q in range(2):
                            d = 2 * r + q
                            for part in (yh, yl):
                                mm = pe.matmul(ps[:, 6 + r % 2, q * SEQ:(q + 1) * SEQ], part[:, d * P:(d + 1) * P], pmT[:],
                                               start=(part is yh), stop=(part is yl))
                        mm.then_inc(s("scattered"), 1)

                def turn_act(e, h):
                    pe.wait_ge(s("act_ready"), e * 2 + h + 1)
                    pe.wait_ge(s("gr_ready" if h else "pmT_ready"), e + 1)
                    for q in range(4):
                        f = 4 * h + q
                        mm = pe.transpose(ps[:, 6 + h, q * P:(q + 1) * P], gl[:, f * P:(f + 1) * P], idn)
                    mm.then_inc(s("act_turned"), 1)

                def slab(e, j, first, between=lambda: None, after=1):
                    hi_w, lo_w = high[:, j % STAGES, :], low[:, j % STAGES, :]
                    kp = j % 4
                    hi_x, lo_x, bank = (xh, xl, 2 * (j // 4)) if j < 8 else (ah, al, 4)
                    pe.wait_ge(s("w_high"), e * SLABS + j + 1)
                    for i, (x, w) in enumerate(((hi_x, hi_w), (lo_x, hi_w), (hi_x, lo_w))):
                        if i == after:
                            between()
                        if i == 2:
                            wait_low(pe, e, j)
                        for q in range(2):
                            for c in range(2):
                                mm = pe.matmul(ps[:, bank + c, :], x[:, 2 * kp + q, :], w[:, q * D + c * 512:q * D + (c + 1) * 512],
                                               start=(first and i == 0 and q == 0), stop=(kp == 3 and i == 2 and q == 1))
                    mm.then_inc(s("slab_done"), 1)

                def expert(e, last):
                    for h in range(2):
                        if h == 0:
                            pe.wait_ge(s("xg_ready"), e * 4 + 4)
                        for c in range(2):
                            at = c * DE + h * 512
                            pe.matmul(ps[:, 2 * h + c, :], sel3[:, bass.ds(e, 1)].to_broadcast([96, P]), bup[:, at:at + 512],
                                      start=True, stop=False)
                        for kp in range(4):
                            if h == 0 and kp == 3:
                                slab(e, kp, False, lambda: scatter(e, (2, 3)))
                            else:
                                slab(e, 4 * h + kp, False)
                            if h == 0 and kp == 1:
                                scatter(e, (0, 1))
                            if h == 1 and kp == 0:
                                pe.wait_ge(s("added"), e * 4 + 4)
                                for t in range(TT):
                                    pe.matmul(ps[:, 6, t * P:(t + 1) * P], pm[:, t, :], idr[:], start=True, stop=True)
                                for t in range(TT):
                                    mm = pe.matmul(ps[:, 7, 0:2], pm[:, t, :],
                                                   gate2[:, t, bass.ds(e, 1), :].rearrange("p a c -> p (a c)"),
                                                   start=(t == 0), stop=(t == TT - 1))
                                mm.then_inc(s("pm_turned"), 1)
                            if h == 1 and kp == 1:
                                turn_act(e, 0)
                    pe.wait_ge(s("aT_high"), e * 2 + 1)
                    pe.wait_ge(s("aT_low"), e * 2 + 1)
                    slab(e, 8, True)
                    if not last:
                        gather(e + 1, (0, 1))
                    slab(e, 9, False, lambda: turn_act(e, 1), 2)
                    if not last:
                        gather(e + 1, (2, 3))
                    pe.wait_ge(s("aT_high"), e * 2 + 2)
                    pe.wait_ge(s("aT_low"), e * 2 + 2)
                    slab(e, 10, False)
                    slab(e, 11, False)

                with condition(pe):
                    gather(0, (0, 1, 2, 3))
                    with pe.Fori(0, NE - 1) as e:
                        expert(e, False)
                    expert(NE - 1, True)
                    scatter(NE, (0, 1, 2, 3))

            @block.scalar
            def _(act):
                def high_part(e, j):
                    act.wait_ge(s(f"raw_in{j % STAGES}"), loads_counted(e, j))
                    wait_place(act, e, j)
                    sl = j % STAGES
                    act.activation(high[:, sl, :], raw[:, sl, :], ACT.Copy).then_inc(s("w_high"), 1)

                def copy_rows(n, r):
                    act.wait_ge(s("gathered"), n * 4 + r + 1)
                    dst = (xh, xl)[r % 2][:, 4 * (r // 2):4 * (r // 2) + 4, :].rearrange("p k r -> p (k r)")
                    act.activation(dst, ps[:, r % 2, :], ACT.Copy).then_inc(s("xg_ready"), 1)

                def sigmoid(e, h):
                    act.wait_ge(s("glu_ready"), e * 2 + h + 1)
                    act.activation(sg[:, h * 512:(h + 1) * 512], gl[:, h * 512:(h + 1) * 512], ACT.Sigmoid, scale=ALPHA)\
                        .then_inc(s("sig_ready"), 1)

                def turned_act(e, h):
                    act.wait_ge(s("act_turned"), e * 2 + h + 1)
                    act.activation(ah[:, 4 * h:4 * h + 4, :].rearrange("p k r -> p (k r)"), ps[:, 6 + h, :], ACT.Copy)\
                        .then_inc(s("aT_high"), 1)

                def expert(e, last):
                    for j in range(SLABS):
                        if j == 4:
                            sigmoid(e, 0)
                        if j == 5:
                            act.wait_ge(s("pm_turned"), e + 1)
                            act.activation(pmT[:], ps[:, 6, 0:SEQ], ACT.Copy).then_inc(s("pmT_ready"), 1)
                        if j == 6:
                            turned_act(e, 0)
                        if j == 8:
                            sigmoid(e, 1)
                        if j == 9:
                            if not last:
                                copy_rows(e + 1, 0)
                                copy_rows(e + 1, 1)
                            turned_act(e, 1)
                        if j == 10 and not last:
                            copy_rows(e + 1, 2)
                            copy_rows(e + 1, 3)
                        if not (last and j + LEAD >= SLABS):
                            high_part(e, j + LEAD)
                    act.wait_ge(s("slab_done"), slabs_done(e, SLABS))
                    act.wait_ge(s("gr_ready"), e + 1)
                    for h in range(2):
                        act.activation(yh[:, h * 512:(h + 1) * 512], ps[:, 4 + h, :], ACT.Copy, scale=gr[:, 0:1])\
                            .then_inc(s("ye_high"), 1)

                with condition(act):
                    for j in range(LEAD):
                        high_part(0, j)
                    for r in range(4):
                        copy_rows(0, r)
                    with act.Fori(0, NE - 1) as e:
                        expert(e, False)
                    expert(NE - 1, True)

            @block.vector
            def _(dve):
                def one_hot(n):
                    for t in range(TT):
                        ins = dve.tensor_scalar(pm[:, t, :], iota, place[:, t, bass.ds(n, 1)], None, ALU.is_equal)
                    ins.then_inc(s("pm_ready"), 1)

                def add(e, r):
                    dve.wait_ge(s("scattered"), e * 4 + r + 1)
                    acc = yacc[:, 2 * r:2 * r + 2, :].rearrange("p k t -> p (k t)")
                    dve.tensor_tensor(acc, acc, ps[:, 6 + r % 2, :], ALU.add).then_inc(s("added"), 1)

                def expert(e, last):
                    n = [0]

                    def link(ins):
                        n[0] += 1
                        ins.then_inc(s("steps"), 1)
                        dve.wait_ge(s("steps"), e * LINKS + n[0])

                    def swiglu(h):
                        a = slice(h * 512, (h + 1) * 512)
                        dve.wait_ge(s("slab_done"), slabs_done(e, 4 * h + 4))
                        dve.tensor_scalar(gl[:, a], ps[:, 2 * h, :], LIMIT, None, ALU.min).then_inc(s("glu_ready"), 1)
                        link(dve.tensor_scalar(li[:, a], ps[:, 2 * h + 1, :], LIMIT, -LIMIT, ALU.min, ALU.max))
                        dve.wait_ge(s("glu_ready"), e * 2 + h + 1)
                        link(dve.scalar_tensor_tensor(li[:, a], li[:, a], 1.0, gl[:, a], ALU.add, ALU.mult))
                        dve.wait_ge(s("sig_ready"), e * 2 + h + 1)
                        dve.tensor_tensor(gl[:, a], li[:, a], sg[:, a], ALU.mult).then_inc(s("act_ready"), 1)

                    def turned_low(h):
                        dve.wait_ge(s("aT_high"), e * 2 + h + 1)
                        at = slice(4 * h, 4 * h + 4)
                        dve.tensor_tensor(al[:, at, :].rearrange("p k r -> p (k r)"), ps[:, 6 + h, :],
                                          ah[:, at, :].rearrange("p k r -> p (k r)").bitcast(F32), ALU.subtract)\
                            .then_inc(s("aT_low"), 1)

                    for j in range(SLABS):
                        if j == 2:
                            add(e, 0)
                            add(e, 1)
                        if j in (4, 8):
                            swiglu(j // 4 - 1)
                        if j == 5:
                            dve.wait_ge(s("pm_turned"), e + 1)
                            dve.tensor_reduce(gr[:], ps[:, 7, 0:2], AX.X, ALU.add).then_inc(s("gr_ready"), 1)
                            if not last:
                                one_hot(e + 1)
                        if j == 6:
                            turned_low(0)
                        if j == 9:
                            turned_low(1)
                        if (j + LEAD) % SLABS not in POOL_SLABS and not (last and j + LEAD >= SLABS):
                            low_part(dve, e, j + LEAD, "w_low")
                        if j == 3:
                            add(e, 2)
                            add(e, 3)
                    for h in range(2):
                        a = slice(h * 512, (h + 1) * 512)
                        dve.wait_ge(s("ye_high"), e * 2 + h + 1)
                        dve.scalar_tensor_tensor(yl[:, a], ps[:, 4 + h, :], gr[:, 0:1], yh[:, a].bitcast(F32), ALU.mult,
                                                 ALU.subtract).then_inc(s("ye_low"), 1)
                    assert n[0] == LINKS, n

                with condition(dve):
                    if base:
                        dve.tensor_scalar(place[:], place[:], float(base), None, ALU.subtract).then_inc(s("filled"), 1)
                        dve.wait_ge(s("filled"), 1)
                    one_hot(0)
                    for unset in (pmT, yh, yl):
                        dve.memset(unset[:].bitcast(F32), 0.0).then_inc(s("ye_low"), 1)
                    for j in range(LEAD):
                        low_part(dve, 0, j, "w_low")
                    with dve.Fori(0, NE - 1) as e:
                        expert(e, False)
                    expert(NE - 1, True)
                    for r in range(4):
                        add(NE, r)

        with nc.Block() as block:
            experts_block(block, "", 0, True, lambda eng: nullcontext())
        with nc.Block() as block:
            experts_block(block, "more_", P, False, lambda eng: eng.If(eng.value_load(flag[0:1, 0:1], min_val=0, max_val=1)))
        moe.close()
        more_slots("second_ring", SLOTS2)

        retire(" ".join(n for n in list(sems) if n in EXPERT_SEMS or n.startswith(("more_", "up_", "down_"))))
        with ExitStack() as pg_:
            sq = sb("sqg", [P, KT, SEQ], at=pg_)
            with nc.Block() as block:
                @block.sync
                def _(sp):
                    for n in range(SLOTS2):
                        load_slab(sp, n, SLABS2[n], "b_")

                @block.tensor
                def _(pe):
                    norm_sums(pe, sq, 4, "x_summed", 4)
                    norm_sums(pe, sq, 5, "x_summed", 5)

                @block.scalar
                def _(act):
                    norm_squares(act, yacc, sq, range(KT))
                    norm_root(act, 4)
                    norm_squares(act, xT, sq, range(KT), ("x2_ready", 0))
                    norm_root(act, 5)
                    for k in range(KT):
                        act.wait_ge(sm("h_scaled"), 2 * KT + k + 1)
                        act.activation(hT[:, k, :], hT[:, k, :], ACT.Identity, bias=mod2[:, k:k + 1])\
                            .then_inc(sm("h_ready"), 1)

                @block.vector
                def _(dve):
                    V.link(dve, dve.tensor_tensor(gain[:], mod[:, 40:48], colv("g_post_ffn"), ALU.mult))
                    norm_rstd(dve, 4, (sm("x_summed"), 4))
                    for k in range(KT):
                        V.link(dve, dve.scalar_tensor_tensor(yacc[:, k, :], yacc[:, k, :], gain[:, k:k + 1], rstd[:],
                                                             ALU.mult, ALU.mult))
                        V.done(dve, dve.tensor_tensor(xT[:, k, :], xT[:, k, :], yacc[:, k, :], ALU.add), sm("x2_ready"))
                    V.link(dve, dve.scalar_tensor_tensor(gain[:], mod2[:, 8:16], 1.0, colv("norm_g_2"), ALU.add, ALU.mult))
                    norm_rstd(dve, 5, (sm("x_summed"), 5))
                    for k in range(KT):
                        dve.scalar_tensor_tensor(hT[:, k, :], xT[:, k, :], gain[:, k:k + 1], rstd[:], ALU.mult, ALU.mult)\
                            .then_inc(sm("h_scaled"), 1)

        NH = QH + KVH
        xbc = sb("xbc", [P, XBC // P, SEQ])
        azT = sb("azT", [P, KT, SEQ])
        idt = sb("idt", [P, TT, 356])
        bc = sb("bc", [P, 2 * HD + 2 * ID + 3 * SH])
        att2 = ctx.enter_context(ExitStack())
        qkv = sb("qkv", [P, TT, (NH + KVH) * HD], at=att2)
        ang = sb("ang", [P, TT, ROT // 2 + IROT // 2], at=att2)
        turns = sb("turns", [P, TT, ROT // 2 + IROT // 2], at=att2)
        sin = sb("sin", [P, TT, ROT // 2 + IROT // 2], at=att2)
        cos = sb("cos", [P, TT, ROT // 2 + IROT // 2], at=att2)
        pos = sb("pos", [P, TT], I32, at=att2)
        posf = sb("posf", [P, TT], at=att2)
        with nc.Block() as block:
            @block.sync
            def _(sp):
                for n in range(SLOTS2, SLOTS2 + M_ZA):
                    load_slab(sp, n, SLABS2[n], "b_")

            @block.scalar
            def _(act):
                for name, (at, w) in BC.items():
                    act.dma_start(bc[:, at:at + w], bass.AP(A[name].tensor, 0, [[0, P], [1, w]]))\
                        .then_inc(sm("bc_in"), 16)
                with nc.allow_non_contiguous_dma("256 positions"):
                    act.dma_start(pos[:], A["positions_2"].rearrange("(t p) a -> p (t a)", p=P)).then_inc(sm("pos_in"), 16)
                act.wait_ge(sm("angle_ready"), 1)
                S.link(act, act.activation(sin[:], ang[:], ACT.Sin))
                S.done(act, act.activation(cos[:], ang[:], ACT.Sin, scale=0.5), sm("half_sin_ready"))
                act.wait_ge(sm("bc_in"), 16 * len(BC))

            @block.tensor
            def _(pe):
                for n in range(M_ZA):
                    pe.wait_ge(sm(f"b_slab_ready{n % len(slots)}"), slab_count(SLABS2, n))
                    tokens_by_columns(pe, n, 356 if n == 3 else 512, 2 * n).then_inc(sm("b_slab_used"), 1)

            @block.vector
            def _(dve):
                dve.wait_ge(sm("pos_in"), 16)
                V.link(dve, dve.tensor_copy(posf[:], pos[:]))
                nf = ROT // 2 + IROT // 2
                V.link(dve, dve.tensor_tensor(ang[:], posf[:].unsqueeze(2).to_broadcast([P, TT, nf]),
                                              cst[:, C_FREQ:C_FREQ + nf].unsqueeze(1).to_broadcast([P, TT, nf]), ALU.mult))
                V.link(dve, dve.tensor_scalar(turns[:], ang[:], 1 / (2 * math.pi), ROUNDER, ALU.mult, ALU.add))
                V.link(dve, dve.tensor_scalar(turns[:], turns[:], ROUNDER, None, ALU.subtract))
                for part in (TWO_PI_HIGH, TWO_PI_LOW):
                    V.link(dve, dve.scalar_tensor_tensor(ang[:], turns[:], -part, ang[:], ALU.mult, ALU.add))
                V.done(dve, dve.tensor_scalar(ang[:], ang[:], 3.1415925, -3.1415925, ALU.min, ALU.max), sm("angle_ready"))
                dve.wait_ge(sm("half_sin_ready"), 1)
                V.link(dve, dve.tensor_tensor(cos[:], cos[:], cos[:], ALU.mult))
                V.link(dve, dve.tensor_scalar(cos[:], cos[:], -2.0, 1.0, ALU.mult, ALU.add))
                for n in range(M_ZA):
                    bank = 2 * n
                    dve.wait_ge(sm("b_slab_used"), n + 1)
                    if n < 3:
                        V.done(dve, dve.tensor_copy(qkv[:, :, 512 * n:512 * n + 512], ps[:, bank:bank + 2, :]),
                               sm("b_z_copied"))
                    else:
                        V.done(dve, dve.tensor_copy(idt[:], ps[:, bank:bank + 2, 0:356]), sm("b_z_copied"))

        with ExitStack() as pi:
            sq2 = sb("sq2", [P, NH * HD], at=pi)
            ssum = sb("ssum", [P, TT, NH], at=pi)
            rt = sb("rt", [P, 4, NH, ROT // 2], at=pi)
            kd = sb("kd", [P, TT, 2 * ID], at=pi)
            mean = sb("mean", [P, TT], at=pi)
            var = sb("var", [P, TT], at=pi)
            wix = sb("wix", [P, TT, IH], at=pi)
            qT = sb("qT", [P, QH, SEQ], at=pi)
            kT = sb("kT", [P, KVH, SEQ], at=pi)
            iqT = sb("iqT", [P, IH // 2, SEQ], at=pi)
            ikT = sb("ikT", [P, SEQ], at=pi)
            sc = sb("sc", [P, TT, SEQ], at=pi)
            tmp = sb("tmp", [P, SEQ], at=pi)
            top2 = sb("top2", [P, 8], at=pi)
            A1 = sb("A1", [P, QH, SEQ], at=pi)
            A0 = sq2[:, 0:QH * P].rearrange("p (h t) -> p h t", h=QH)
            nm2 = sb("nm2", [P, TT, QH], at=pi)
            es2 = sb("es2", [P, TT, QH], at=pi)
            P0 = qT
            P1 = A0
            taps = sb("taps", [P, 2, 3, 2, SEQ], at=pi)
            HALVES = 2 * (M_ZS - M_ZA)
            ZHALVES = 2 * (M_XBC - M_ZA)

            def half_made(eng, h):
                if h % 2:
                    eng.wait_ge(sm("b_slab_used"), M_ZA + h // 2 + 1)
                else:
                    eng.wait_ge(sm("half_made"), h // 2 + 1)

            def rotate(dve, x, c, s_, half, heads):
                x1, x2 = x[:, :, 0:half], x[:, :, half:2 * half]
                cb = c.unsqueeze(1).to_broadcast([P, heads, half])
                sb_ = s_.unsqueeze(1).to_broadcast([P, heads, half])
                r = [rt[:, i, 0:heads, 0:half] for i in range(4)]
                V.link(dve, dve.tensor_tensor(r[0], x1, cb, ALU.mult))
                V.link(dve, dve.tensor_tensor(r[1], x2, sb_, ALU.mult))
                V.link(dve, dve.tensor_tensor(r[2], x2, cb, ALU.mult))
                V.link(dve, dve.tensor_tensor(r[3], x1, sb_, ALU.mult))
                V.link(dve, dve.tensor_tensor(x1, r[0], r[1], ALU.subtract))
                return dve.tensor_tensor(x2, r[2], r[3], ALU.add)

            def bcv(name):
                at, w = BC[name]
                return bc[:, at:at + w]

            with nc.Block() as block:
                @block.sync
                def _(sp):
                    for n in range(SLOTS2 + M_ZA, SLOTS2 + M_ZS):
                        load_slab(sp, n, SLABS2[n], "b_")

                @block.gpsimd
                def _(pool):
                    G.done(pool, pool.memset(taps[:], 0.0), sm("taps_zero"))
                    for i in range(HALVES - ZHALVES):
                        pool.wait_ge(sm("half_taken"), ZHALVES + i + 1)
                        c = xbc[:, 2 * i:2 * i + 2, :]
                        for tap in range(3):
                            ins = pool.tensor_tensor(c, c, taps[:, i % 2, tap], ALU.add)
                            if tap == 2:
                                G.done(pool, ins, sm("b_conv_ready"))
                            else:
                                G.link(pool, ins)

                @block.scalar
                def _(act):
                    taken = [0]

                    def silu(i):
                        act.wait_ge(sm("b_conv_ready"), i + 1)
                        for j in range(2):
                            k = 2 * i + j
                            ins = act.activation(xbc[:, k, :], xbc[:, k, :], ACT.Silu, bias=col("conv_b_2", k))
                        S.done(act, ins, sm("b_silu_ready"))

                    def take(count):
                        for _ in range(count):
                            h = taken[0]
                            half_made(act, h)
                            src = ps[:, h % 2, :].rearrange("p (j t) -> p j t", j=2)
                            if h < ZHALVES:
                                S.done(act, act.activation(azT[:, 2 * h:2 * h + 2, :], src, ACT.Silu), sm("half_taken"))
                            else:
                                i = h - ZHALVES
                                if i == 0:
                                    act.wait_ge(sm("taps_zero"), 1)
                                if i >= 2:
                                    silu(i - 2)
                                for j in range(2):
                                    for tap in range(4):
                                        late = 3 - tap
                                        dst = taps[:, i % 2, tap, j, late:] if late else xbc[:, 2 * i + j, :]
                                        ins = act.activation(dst, src[:, j, 0:SEQ - late], ACT.Copy,
                                                             scale=col("conv_w_2", 24 * tap + 2 * i + j))
                                S.done(act, ins, sm("half_taken"))
                            taken[0] += 1

                    act.wait_ge(sm("var_ready"), 1)
                    S.done(act, act.activation(var[:], var[:], ACT.Sqrt), sm("dev_ready"))
                    for t in range(TT):
                        S.done(act, act.activation(sq2[:], qkv[:, t, 0:NH * HD], ACT.Square), sm("head_sq"))
                        act.wait_ge(sm("head_sums"), t + 1)
                    S.done(act, act.activation(ssum[:], ssum[:], ACT.Sqrt), sm("head_rms"))
                    take(2)
                    act.wait_ge(sm("i_turned"), 1)
                    S.link(act, act.activation(iqT[:].rearrange("p j t -> p (j t)"), ps[:, 7, :], ACT.Copy))
                    S.done(act, act.activation(ikT[:], ps[:, 6, 0:SEQ], ACT.Copy), sm("i_ready"))
                    take(3)
                    act.wait_ge(sm("q_turned"), 1)
                    S.link(act, act.activation(qT[:].rearrange("p h t -> p (h t)"),
                                               ps[:, 2:6, :].rearrange("p b n -> p (b n)"), ACT.Copy))
                    S.done(act, act.activation(kT[:].rearrange("p h t -> p (h t)"), ps[:, 6, :], ACT.Copy), sm("q_ready"))
                    def exps(t):
                        act.wait_ge(sm("b_logits"), t + 1)
                        L = A1[:] if t else A0
                        for h in range(QH):
                            ins = act.activation(L[:, h, :], L[:, h, :], ACT.Exp, bias=nm2[:, t, h:h + 1],
                                                 accum_out=es2[:, t, h:h + 1])
                        S.done(act, ins, sm("b_exp"))

                    def turned(nth, dst):
                        act.wait_ge(sm("b_p_turned"), nth)
                        S.done(act, act.activation(dst, bank2(6).rearrange("p (h t) -> p h t", h=QH), ACT.Copy),
                               sm("b_pt_ready"))

                    take(3)
                    exps(0)
                    take(2)
                    exps(1)
                    take(2)
                    turned(1, P0[:, :, 0:P])
                    take(2)
                    turned(2, P0[:, :, P:SEQ])
                    turned(3, P1)
                    take(2)
                    for i in range(HALVES - ZHALVES - 2, HALVES - ZHALVES):
                        silu(i)

                @block.tensor
                def _(pe):
                    given = [0]

                    def give(count):
                        for _ in range(count):
                            h = given[0]
                            n = M_ZA + h // 2
                            if h % 2 == 0:
                                pe.wait_ge(sm(f"b_slab_ready{n % len(slots)}"), slab_count(SLABS2, n))
                            if h >= 2:
                                pe.wait_ge(sm("half_taken"), h - 1)
                            half_slab(pe, n, h % 2, h % 2, hT).then_inc(sm("b_slab_used" if h % 2 else "half_made"), 1)
                            given[0] += 1

                    def logits(t):
                        w = (t + 1) * P
                        for h in range(IH):
                            half = slice(64 * (h % 2), 64 * (h % 2) + 64)
                            mm = pe.matmul(ps[:, 6 + h % 2, (h // 2) * w:(h // 2) * w + w], iqT[half, h // 2, t * P:(t + 1) * P],
                                           ikT[half, 0:w], start=True, stop=True)
                        mm.then_inc(sm("i_logits"), 1)

                    def scores(t):
                        w = (t + 1) * P
                        for h in range(QH):
                            at = h * w
                            mm = pe.matmul(ps[:, 2 + at // 512, at % 512:at % 512 + w],
                                           qT[:, h, t * P:(t + 1) * P], kT[:, h // (QH // KVH), 0:w], start=True, stop=True)
                        mm.then_inc(sm("b_scored"), 1)

                    def turn(t, s_):
                        L = A1 if t else A0
                        for h in range(QH):
                            mm = pe.transpose(ps[:, 6 + h // 4, (h % 4) * P:(h % 4 + 1) * P],
                                              L[:, h, s_ * P:(s_ + 1) * P], idn)
                        mm.then_inc(sm("b_p_turned"), 1)

                    give(2)
                    pe.wait_ge(sm("i_rotated"), TT)
                    for t in range(TT):
                        for j in range(2):
                            pe.transpose(ps[:, 7, j * SEQ + t * P:j * SEQ + (t + 1) * P], idt[:, t, j * P:(j + 1) * P], idn)
                        mm = pe.transpose(ps[:, 6, t * P:(t + 1) * P], kd[:, t, :], idn)
                    mm.then_inc(sm("i_turned"), 1)
                    give(3)
                    pe.wait_ge(sm("i_ready"), 1)
                    pe.wait_ge(sm("q_rotated"), TT)
                    for h in range(NH):
                        for t in range(TT):
                            dst = ps[:, 2 + h // 2, (h % 2) * SEQ + t * P:(h % 2) * SEQ + (t + 1) * P]
                            mm = pe.transpose(dst, qkv[:, t, h * HD:(h + 1) * HD], idn)
                    mm.then_inc(sm("q_turned"), 1)
                    pe.wait_ge(sm("q_ready"), 1)
                    logits(0)
                    scores(0)
                    give(3)
                    pe.wait_ge(sm("i_scored"), 1)
                    logits(1)
                    pe.wait_ge(sm("b_logits"), 1)
                    scores(1)
                    give(4)
                    pe.wait_ge(sm("i_scored"), 2)
                    pe.wait_ge(sm("b_probs"), 1)
                    turn(0, 0)
                    give(2)
                    pe.wait_ge(sm("b_pt_ready"), 1)
                    pe.wait_ge(sm("b_probs"), 2)
                    turn(1, 0)
                    pe.wait_ge(sm("b_pt_ready"), 2)
                    turn(1, 1)
                    give(2)
                    pe.wait_ge(sm("b_pt_ready"), 3)
                    for h in range(QH):
                        out_h = ps[:, 2 + h // 2, (h % 2) * SEQ:(h % 2 + 1) * SEQ]
                        v0 = (NH + h // (QH // KVH)) * HD
                        pe.matmul(out_h, qkv[:, 0, v0:v0 + HD], P0[:, h, :], start=True, stop=False)
                        mm = pe.matmul(out_h[:, P:SEQ], qkv[:, 1, v0:v0 + HD], P1[:, h, :], start=False, stop=True)
                    mm.then_inc(sm("b_att"), 1)

                @block.vector
                def _(dve):
                    for t in range(TT):
                        ki = idt[:, t, 256:320]
                        V.link(dve, dve.tensor_reduce(mean[:, t:t + 1], ki, AX.X, ALU.add))
                        V.link(dve, dve.tensor_scalar(mean[:, t:t + 1], mean[:, t:t + 1], 1.0 / ID, None, ALU.mult))
                        V.link(dve, dve.tensor_scalar(ki, ki, mean[:, t:t + 1], None, ALU.subtract))
                        V.link(dve, dve.tensor_tensor(tmp[:, 0:ID], ki, ki, ALU.mult))
                        V.link(dve, dve.tensor_reduce(var[:, t:t + 1], tmp[:, 0:ID], AX.X, ALU.add))
                    V.done(dve, dve.tensor_scalar(var[:], var[:], 1.0 / ID, EPS, ALU.mult, ALU.add), sm("var_ready"))
                    V.link(dve, dve.tensor_scalar(wix[:], idt[:, :, 320:324], IH ** -0.5 * ID ** -0.5, None, ALU.mult))
                    dve.wait_ge(sm("dev_ready"), 1)
                    V.link(dve, dve.reciprocal(var[:], var[:]))
                    for t in range(TT):
                        ki = idt[:, t, 256:320]
                        V.link(dve, dve.tensor_scalar(ki, ki, var[:, t:t + 1], None, ALU.mult))
                        V.link(dve, dve.tensor_tensor(ki, ki, bcv("idx_k_ln_g_2"), ALU.mult))
                        V.link(dve, dve.tensor_tensor(ki, ki, bcv("idx_k_ln_b_2"), ALU.add))
                        x = idt[:, t, 0:320].rearrange("p (h d) -> p h d", h=IH + 1)
                        f0 = ROT // 2
                        V.link(dve, rotate(dve, x, cos[:, t, f0:f0 + IROT // 2], sin[:, t, f0:f0 + IROT // 2],
                                           IROT // 2, IH + 1))
                        V.link(dve, dve.tensor_copy(kd[:, t, 0:ID], ki))
                        V.done(dve, dve.tensor_copy(kd[:, t, ID:], ki), sm("i_rotated"))
                    for t in range(TT):
                        dve.wait_ge(sm("head_sq"), t + 1)
                        V.link(dve, dve.tensor_reduce(ssum[:, t, :], sq2[:].rearrange("p (h d) -> p h d", h=NH), AX.X,
                                                      ALU.add))
                        V.done(dve, dve.tensor_scalar(ssum[:, t, :], ssum[:, t, :], 1.0 / HD, EPS, ALU.mult, ALU.add),
                               sm("head_sums"))
                    dve.wait_ge(sm("head_rms"), 1)
                    V.link(dve, dve.reciprocal(ssum[:], ssum[:]))
                    for t in range(TT):
                        x = qkv[:, t, 0:NH * HD].rearrange("p (h d) -> p h d", h=NH)
                        V.link(dve, dve.tensor_tensor(x, x, ssum[:, t, :].unsqueeze(2).to_broadcast([P, NH, HD]), ALU.mult))
                        V.link(dve, dve.tensor_tensor(x[:, 0:QH], x[:, 0:QH], bcv("q_norm_g_2").unsqueeze(1)
                                                      .to_broadcast([P, QH, HD]), ALU.mult))
                        V.link(dve, dve.tensor_tensor(x[:, QH:], x[:, QH:], bcv("k_norm_g_2").unsqueeze(1)
                                                      .to_broadcast([P, KVH, HD]), ALU.mult))
                        V.done(dve, rotate(dve, x, cos[:, t, 0:ROT // 2], sin[:, t, 0:ROT // 2], ROT // 2, NH),
                               sm("q_rotated"))
                    for t in range(TT):
                        w = (t + 1) * P
                        s_ = sc[:, t, 0:w]
                        dve.wait_ge(sm("i_logits"), t + 1)
                        for h in range(IH):
                            src = ps[:, 6 + h % 2, (h // 2) * w:(h // 2) * w + w]
                            dst = s_ if h == 0 else tmp[:, 0:w]
                            ins = dve.tensor_scalar(dst, src, 0.0, wix[:, t, h:h + 1], ALU.max, ALU.mult)
                            if h == IH - 1:
                                V.done(dve, ins, sm("i_scored"))
                            else:
                                V.link(dve, ins)
                            if h:
                                V.link(dve, dve.tensor_tensor(s_, s_, tmp[:, 0:w], ALU.add))
                        cm = cst[:, C_ZERO:C_ZERO + SEQ] if t else cst[:, C_CM:C_CM + P]
                        V.link(dve, dve.tensor_tensor(s_, s_, cm, ALU.add))
                        for r in range(KEEP // 8):
                            V.link(dve, dve.max(top2[:], s_))
                            V.link(dve, dve.match_replace(s_, top2[:], s_, -3e38))
                        V.link(dve, dve.tensor_single_scalar(s_, s_, -3e38, ALU.is_equal))
                        V.link(dve, dve.tensor_scalar(s_, s_, 1.0, -NEG, ALU.subtract, ALU.mult))
                        V.link(dve, dve.tensor_tensor(s_, s_, cm, ALU.add))
                        dve.wait_ge(sm("b_scored"), t + 1)
                        L = A1[:] if t else A0
                        src = (ps[:, 2:6, :] if t else ps[:, 2:4, :]).rearrange("p b n -> p (b n)")\
                            .rearrange("p (h n) -> p h n", h=QH)
                        V.link(dve, dve.scalar_tensor_tensor(L, src, HD ** -0.5, s_.unsqueeze(1).to_broadcast([P, QH, w]),
                                                             ALU.mult, ALU.add))
                        V.done(dve, dve.tensor_reduce(nm2[:, t, :], L, AX.X, ALU.max, negate=True), sm("b_logits"))
                    for t in range(TT):
                        L = A1[:] if t else A0
                        dve.wait_ge(sm("b_exp"), t + 1)
                        V.link(dve, dve.reciprocal(es2[:, t, :], es2[:, t, :]))
                        V.done(dve, dve.tensor_tensor(L, L, es2[:, t, :].unsqueeze(2).to_broadcast([P, QH, (t + 1) * P]),
                                                      ALU.mult), sm("b_probs"))
                    dve.wait_ge(sm("b_att"), 1)
                    dve.wait_ge(sm("half_taken"), ZHALVES)
                    V.link(dve, dve.tensor_tensor(azT[:].rearrange("p k t -> p (k t)"), azT[:].rearrange("p k t -> p (k t)"),
                                                  ps[:, 2:6, :].rearrange("p b n -> p (b n)"), ALU.mult))
        att2.close()

        GH = SH // SG
        GW = GH * SP
        ssm = ctx.enter_context(ExitStack())
        y = sb("y", [P, TT, DI], at=ssm)
        sgs = sb("sgs", [P, KT, SEQ], at=ssm)
        mer = sb("mer", [P, KT, SEQ], at=ssm)
        with ExitStack() as pj:
            xs = sb("xs", [P, TT, DI], at=pj)
            bt = sb("bt", [P, SG * SN], at=pj)
            xd = sb("xd", [P, GW], at=pj)
            st = sb("st", [P, GW], at=pj)
            dts = sb("dts", [P, TT, SH], at=pj)
            u_ = sb("u_", [P, TT, SH], at=pj)
            z_ = sb("z_", [P, TT, SH], at=pj)
            z2 = sb("z2", [P, TT, SH], at=pj)
            adt = sb("adt", [P, TT, SH], at=pj)
            aexp = sb("aexp", [P, SH], at=pj)
            cum = sb("cum", [P, TT, SH], at=pj)
            dec = sb("dec", [P, SH], at=pj)
            ecum = sb("ecum", [P, SH], at=pj)
            M = xbc[:, 0:8, :].rearrange("p (u k) t -> p u (k t)", u=2).rearrange("p u (h l) -> p u h l", h=GH)
            L_ = xbc[:, 8:12, :].rearrange("p k t -> p (k t)").rearrange("p (h l) -> p h l", h=GH)
            cb = sb("cb", [P, 2, P], at=pj)
            zs = sb("zs", [P, 2, 512], at=pj)
            t5 = sb("t5", [P, GW], at=pj)
            gs = sb("gs", [P, TT, SG], at=pj)

            def bcv(name):
                at, w = BC[name]
                return bc[:, at:at + w]

            def fill_made(eng, f):
                if f % 2:
                    eng.wait_ge(sm("b_slab_used"), M_ZS + f // 2 + 1)
                else:
                    eng.wait_ge(sm("fill_made"), f // 2 + 1)

            PAIRS = [(c, g) for g in range(SG) for c in range(TT)]
            with nc.Block() as block:
                @block.gpsimd
                def _(pool):
                    pool.wait_ge(sm("adt_ready"), 1)
                    pool.wait_ge(sm("xs_ready"), 9)
                    for i, (c, g) in enumerate(PAIRS):
                        if i >= 1:
                            pool.wait_ge(sm("seg_summed"), i)
                        gh = slice(g * GH, (g + 1) * GH)
                        pool.tensor_tensor(L_, cst[:, C_LATER:C_LATER + P].unsqueeze(1).to_broadcast([P, GH, P]),
                                           adt[:, c, gh].unsqueeze(2).to_broadcast([P, GH, P]), ALU.mult)\
                            .then_inc(sm("later_ready"), 1)

                @block.sync
                def _(sp):
                    for n in range(SLOTS2 + M_ZS, SLOTS2 + M_SSM):
                        load_slab(sp, n, SLABS2[n], "b_")

                @block.scalar
                def _(act):
                    S.done(act, act.activation(aexp[:], bcv("a_log_2"), ACT.Exp), sm("a_exp"))
                    act.wait_ge(sm("dt_abs"), 1)
                    S.done(act, act.activation(u_[:], u_[:], ACT.Exp), sm("dt_exp"))
                    for i in range(9):
                        act.wait_ge(sm("xs_turned"), i + 1)
                        bank = 2 * (i % 2)
                        if i < 8:
                            t, q = i // 4, i % 4
                            S.done(act, act.activation(xs[:, t, q * 512:(q + 1) * 512], ps[:, bank, :], ACT.Copy),
                                   sm("xs_ready"))
                        else:
                            S.done(act, act.activation(bt[:], ps[:, bank, :], ACT.Copy), sm("xs_ready"))
                    act.wait_ge(sm("dec_in"), 1)
                    S.link(act, act.activation(dec[:], dec[:], ACT.Exp))
                    S.done(act, act.activation(ecum[:], cum[:, 1, :], ACT.Exp), sm("dec_ready"))
                    for i, (c, g) in enumerate(PAIRS):
                        act.wait_ge(sm("seg_ready"), i + 1)
                        S.done(act, act.activation(M[:, i % 2], M[:, i % 2], ACT.Exp), sm("seg_exp"))
                        for f in (2 * i, 2 * i + 1):
                            fill_made(act, f)
                            src = ps[:, 4 + f % 2, :]
                            if c == 0:
                                if i:
                                    act.wait_ge(sm("zs_used"), i - 1 + f % 2)
                                S.done(act, act.activation(zs[:, f % 2, :], src, ACT.Silu), sm("fill_taken"))
                            else:
                                k = 4 * (g % 2) + 2 * (f % 2)
                                dst = (sgs if g < 2 else mer)[:, k:k + 2, :].rearrange("p k t -> p (k t)")
                                S.done(act, act.activation(dst, src, ACT.Sigmoid), sm("fill_taken"))
                    act.wait_ge(sm("gs_ready"), 1)
                    S.done(act, act.activation(gs[:], gs[:], ACT.Sqrt), sm("gs_rms"))

                @block.tensor
                def _(pe):
                    for i in range(9):
                        bank = 2 * (i % 2)
                        if i >= 2:
                            pe.wait_ge(sm("xs_ready"), i - 1)
                        for j in range(4):
                            t = i // 4 if i < 8 else 0
                            tile = 4 * (i % 4) + j if i < 8 else 16 + j
                            mm = pe.transpose(ps[:, bank, j * P:(j + 1) * P], xbc[:, tile, t * P:(t + 1) * P], idn)
                        mm.then_inc(sm("xs_turned"), 1)
                    tri = cst[:, C_TRI:C_TRI + P]
                    pe.wait_ge(sm("adt_ready"), 1)
                    for t in range(TT):
                        pe.matmul(ps[:, 1, t * SH:(t + 1) * SH], tri, adt[:, t, :], start=True, stop=True)
                    pe.matmul(ps[:, 1, 2 * SH:3 * SH], cst[:, C_LATER:C_LATER + P], adt[:, 0, :], start=True, stop=True)\
                        .then_inc(sm("cum_summed"), 1)
                    pe.wait_ge(sm("cum_ready"), 1)
                    def prepare(i):
                        c, g = PAIRS[i]
                        tk = slice(c * P, (c + 1) * P)
                        if i >= 1:
                            pe.wait_ge(sm("seg_ready"), i)
                        if i >= 2:
                            pe.wait_ge(sm("y_out"), i - 1)
                        pe.matmul(ps[:, 6 + i % 2, 0:P], xbc[:, 16 + g, tk], xbc[:, 20 + g, tk], start=True, stop=True)
                        pe.wait_ge(sm("later_ready"), i + 1)
                        for h in range(GH):
                            mm = pe.matmul(ps[:, 2 + h // 4, (h % 4) * P:(h % 4 + 1) * P], L_[:, h, :], tri,
                                           start=True, stop=True)
                        mm.then_inc(sm("seg_summed"), 1)

                    def fill(f):
                        n = M_ZS + f // 2
                        if f % 2 == 0:
                            pe.wait_ge(sm(f"b_slab_ready{n % len(slots)}"), slab_count(SLABS2, n))
                        if 2 <= f < 18:
                            pe.wait_ge(sm("fill_taken"), f - 1)
                        elif f >= 18:
                            pe.wait_ge(sm("att_gated"), f - 17)
                        if f < 16 and f % 4 < 2:
                            for k in range(KT):
                                mm = pe.matmul(ps[:, 4 + f % 2, :], hT[:, k, (f % 2) * P:(f % 2 + 1) * P],
                                               slots[n % len(slots)][:, k, :], start=(k == 0), stop=(k == KT - 1))
                        else:
                            mm = half_slab(pe, n, f % 2, 4 + f % 2, hT if f < 16 else azT)
                        mm.then_inc(sm("b_slab_used" if f % 2 else "fill_made"), 1)

                    pe.wait_ge(sm("xs_ready"), 9)
                    prepare(0)
                    for i, (c, g) in enumerate(PAIRS):
                        fill(2 * i)
                        if c == 0:
                            pe.wait_ge(sm("xd_ready"), g + 1)
                            pe.matmul(ps[:, 0, :], bt[:, g * SN:(g + 1) * SN], xd[:], start=True, stop=True)\
                                .then_inc(sm("st_made"), 1)
                        if i + 1 < len(PAIRS):
                            prepare(i + 1)
                        fill(2 * i + 1)
                        if c == 0:
                            pe.wait_ge(sm("st_ready"), g + 1)
                            if i:
                                pe.wait_ge(sm("y_out"), i)
                            pe.matmul(ps[:, 1, :], xbc[:, 20 + g, P:SEQ], st[:], start=True, stop=True)\
                                .then_inc(sm("off_made"), 1)
                        pe.wait_ge(sm("m_ready"), i + 1)
                        for h in range(GH):
                            mm = pe.matmul(ps[:, 6 + i % 2, h * SP:(h + 1) * SP], M[:, i % 2, h, :],
                                           y[:, c, g * GW + h * SP:g * GW + (h + 1) * SP], start=True, stop=True)
                        mm.then_inc(sm("y_made"), 1)
                    for f in range(16, 20):
                        fill(f)

                @block.vector
                def _(dve):
                    dtr = idt[:, :, 324:356]
                    V.link(dve, dve.tensor_tensor(dts[:], dtr, bcv("dt_bias_2").unsqueeze(1).to_broadcast([P, TT, SH]), ALU.add))
                    V.done(dve, dve.scalar_tensor_tensor(u_[:], dts[:], -1.0, dts[:], ALU.mult, ALU.min), sm("dt_abs"))
                    dve.wait_ge(sm("dt_exp"), 1)
                    V.link(dve, dve.tensor_scalar(z_[:], u_[:], 2.0, None, ALU.add))
                    V.link(dve, dve.reciprocal(z_[:], z_[:]))
                    V.link(dve, dve.tensor_tensor(z_[:], z_[:], u_[:], ALU.mult))
                    V.link(dve, dve.tensor_tensor(z2[:], z_[:], z_[:], ALU.mult))
                    V.link(dve, dve.tensor_scalar(u_[:], z2[:], 2.0 / 17, 2.0 / 15, ALU.mult, ALU.add))
                    for odd in (13, 11, 9, 7, 5, 3, 1):
                        V.link(dve, dve.tensor_tensor(u_[:], u_[:], z2[:], ALU.mult))
                        V.link(dve, dve.tensor_scalar(u_[:], u_[:], 2.0 / odd, None, ALU.add))
                    V.link(dve, dve.tensor_tensor(u_[:], u_[:], z_[:], ALU.mult))
                    V.link(dve, dve.scalar_tensor_tensor(dts[:], dts[:], 0.0, u_[:], ALU.max, ALU.add))
                    dve.wait_ge(sm("a_exp"), 1)
                    V.link(dve, dve.scalar_tensor_tensor(adt[:], dts[:], -1.0, aexp[:].unsqueeze(1).to_broadcast([P, TT, SH]),
                                                         ALU.mult, ALU.mult))
                    V.done(dve, dve.tensor_scalar(adt[:], adt[:], -120.0, None, ALU.max), sm("adt_ready"))
                    dve.wait_ge(sm("cum_summed"), 1)
                    V.link(dve, dve.tensor_copy(cum[:].rearrange("p t h -> p (t h)"), ps[:, 1, 0:2 * SH]))
                    V.done(dve, dve.tensor_copy(dec[:], ps[:, 1, 2 * SH:3 * SH]), sm("dec_in"))
                    dve.wait_ge(sm("xs_ready"), 8)
                    for t in range(TT):
                        yv = y[:, t, :].rearrange("p (h q) -> p h q", h=SH)
                        ins = dve.tensor_tensor(yv, xs[:, t, :].rearrange("p (h q) -> p h q", h=SH),
                                                dts[:, t, :].unsqueeze(2).to_broadcast([P, SH, SP]), ALU.mult)
                        (V.done(dve, ins, sm("cum_ready")) if t else V.link(dve, ins))
                    dve.wait_ge(sm("dec_ready"), 1)
                    for i, (c, g) in enumerate(PAIRS):
                        gw = slice(g * GW, (g + 1) * GW)
                        heads = lambda a: a.rearrange("p (h q) -> p h q", h=GH)
                        gh = slice(g * GH, (g + 1) * GH)
                        if c == 0:
                            if g:
                                dve.wait_ge(sm("st_made"), g)
                            V.done(dve, dve.tensor_tensor(heads(xd[:]), heads(y[:, 0, gw]),
                                                          dec[:, gh].unsqueeze(2).to_broadcast([P, GH, SP]), ALU.mult),
                                   sm("xd_ready"))
                        dve.wait_ge(sm("seg_summed"), i + 1)
                        seg = bank2(2).rearrange("p (h l) -> p h l", h=GH)
                        if i >= 2:
                            dve.wait_ge(sm("y_made"), i - 1)
                        Mi = M[:, i % 2]
                        V.link(dve, dve.tensor_copy(cb[:, i % 2, :], ps[:, 6 + i % 2, 0:P]))
                        V.done(dve, dve.tensor_tensor(Mi, seg, cst[:, C_CMT:C_CMT + P].unsqueeze(1).to_broadcast([P, GH, P]),
                                                      ALU.min), sm("seg_ready"))
                        if c == 0:
                            dve.wait_ge(sm("st_made"), g + 1)
                            if g:
                                dve.wait_ge(sm("off_made"), g)
                            V.done(dve, dve.tensor_copy(st[:], ps[:, 0, :]), sm("st_ready"))
                        dve.wait_ge(sm("seg_exp"), i + 1)
                        V.done(dve, dve.tensor_tensor(Mi, Mi, cb[:, i % 2, :].unsqueeze(1).to_broadcast([P, GH, P]), ALU.mult),
                               sm("m_ready"))
                        if c == 1:
                            dve.wait_ge(sm("off_made"), g + 1)
                            V.link(dve, dve.tensor_tensor(heads(t5[:]), heads(ps[:, 1, :]),
                                                          ecum[:, gh].unsqueeze(2).to_broadcast([P, GH, SP]), ALU.mult))
                        dve.wait_ge(sm("y_made"), i + 1)
                        if c == 1:
                            V.link(dve, dve.tensor_tensor(y[:, c, gw], t5[:], ps[:, 6 + i % 2, :], ALU.add))
                        else:
                            V.link(dve, dve.tensor_copy(y[:, c, gw], ps[:, 6 + i % 2, :]))
                        V.link(dve, dve.tensor_tensor(heads(t5[:]), heads(xs[:, c, gw]), bcv("d_skip_2")[:, gh].unsqueeze(2)
                                                      .to_broadcast([P, GH, SP]), ALU.mult))
                        V.done(dve, dve.tensor_tensor(y[:, c, gw], y[:, c, gw], t5[:], ALU.add), sm("y_out"))
                        dve.wait_ge(sm("fill_taken"), 4 * g + c + 1)
                        V.done(dve, dve.tensor_tensor(y[:, c, gw], y[:, c, gw], zs[:, c, :], ALU.mult), sm("zs_used"))
                        V.link(dve, dve.tensor_tensor(t5[:], y[:, c, gw], y[:, c, gw], ALU.mult))
                        V.link(dve, dve.tensor_reduce(gs[:, c, g:g + 1], t5[:], AX.X, ALU.add))
                    V.done(dve, dve.tensor_scalar(gs[:], gs[:], 1.0 / GW, EPS, ALU.mult, ALU.add), sm("gs_ready"))
                    dve.wait_ge(sm("gs_rms"), 1)
                    V.link(dve, dve.reciprocal(gs[:], gs[:]))
                    for t in range(TT):
                        yv = y[:, t, :].rearrange("p (g q) -> p g q", g=SG)
                        V.link(dve, dve.tensor_tensor(yv, yv, gs[:, t, :].unsqueeze(2).to_broadcast([P, SG, GW]), ALU.mult))
                    for f in range(16, 20):
                        fill_made(dve, f)
                        dve.wait_ge(sm("fill_taken"), 16)
                        at = slice(2 * (f - 16), 2 * (f - 16) + 2)
                        m2 = mer[:, at, :].rearrange("p k t -> p (k t)")
                        V.done(dve, dve.tensor_tensor(m2, m2, ps[:, 4 + f % 2, :], ALU.mult), sm("att_gated"))

        with ExitStack() as pk:
            yT = xbc[:, 0:2 * KT, :]
            otok = sb("otok", [P, TT, D], at=pk)
            with nc.Block() as block:
                @block.sync
                def _(sp):
                    for n in range(SLOTS2 + M_SSM, len(SLABS2)):
                        load_slab(sp, n, SLABS2[n], "b_")
                    for t in range(TT):
                        sp.wait_ge(sm(f"o_ready{t}"), 1)
                        sp.dma_start(out[t * P:(t + 1) * P, :], otok[:, t, :]).then_inc(sm("out_stored"), 16)
                    sp.wait_ge(sm("out_stored"), 16 * TT)

                @block.tensor
                def _(pe):
                    for i in range(8):
                        bank = i % 4
                        if i >= 4:
                            pe.wait_ge(sm("yT_ready"), 2 * (i - 3))
                        for j in range(2):
                            for t in range(TT):
                                k = 2 * i + j
                                mm = pe.transpose(ps[:, bank, j * SEQ + t * P:j * SEQ + (t + 1) * P],
                                                  y[:, t, k * P:(k + 1) * P], idn)
                        mm.then_inc(sm("y_turned"), 1)
                    def slab(n):
                        pe.wait_ge(sm(f"b_slab_ready{n % len(slots)}"), slab_count(SLABS2, n))
                    pe.wait_ge(sm("yT_ready"), 16)
                    for i in range(2):
                        n = M_SSM + 2 * i
                        slab(n)
                        slab(n + 1)
                        for j in range(4):
                            for k in range(2 * KT):
                                mm = pe.matmul(ps[:, 2 * i + j // 2, (j % 2) * SEQ:(j % 2 + 1) * SEQ],
                                               slots[(n + k // KT) % len(slots)][:, k % KT, j * P:(j + 1) * P], yT[:, k, :],
                                               start=(k == 0), stop=(k == 2 * KT - 1))
                        mm.then_inc(sm("b_slab_used"), 2)
                    pe.wait_ge(sm("mer_ready"), 2)
                    for i in range(2):
                        slab(M_OUT + i)
                        columns_by_tokens(pe, M_OUT + i, 4 + 2 * i, src=mer).then_inc(sm("b_slab_used"), 1)
                    for t in range(TT):
                        pe.wait_ge(sm("x3_ready"), 8)
                        for k in range(KT):
                            mm = pe.transpose(ps[:, 2 * t + k // 4, (k % 4) * P:(k % 4 + 1) * P],
                                              xT[:, k, t * P:(t + 1) * P], idn)
                        mm.then_inc(sm("o_turned"), 1)

                @block.scalar
                def _(act):
                    for i in range(8):
                        act.wait_ge(sm("y_turned"), i + 1)
                        for j in range(2):
                            kk = 2 * i + j
                            ins = act.activation(yT[:, kk, :], ps[:, i % 4, j * SEQ:(j + 1) * SEQ], ACT.Copy,
                                                 scale=col("ssm_norm_g_2", kk))
                            S.done(act, ins, sm("yT_ready"))
                    act.wait_ge(sm("o_turned"), 2)
                    S.done(act, act.activation(otok[:, 1, :], bank2(2), ACT.Copy), sm("o_ready1"))

                @block.vector
                def _(dve):
                    for i in range(2):
                        dve.wait_ge(sm("b_slab_used"), M_SSM + 2 * i + 2)
                        half = slice(4 * i, 4 * i + 4)
                        flat = lambda a: a[:, half, :].rearrange("p k t -> p (k t)")
                        V.link(dve, dve.tensor_tensor(flat(sgs), flat(sgs), bank2(2 * i), ALU.mult))
                        V.done(dve, dve.tensor_tensor(flat(mer), flat(mer), flat(sgs), ALU.add), sm("mer_ready"))
                    for k in range(KT):
                        dve.wait_ge(sm("b_slab_used"), M_OUT + 1 + k // 4)
                        V.done(dve, dve.scalar_tensor_tensor(xT[:, k, :], ps[:, 4 + k // 2, (k % 2) * SEQ:(k % 2 + 1) * SEQ],
                                                             mod2[:, 16 + k:17 + k], xT[:, k, :], ALU.mult, ALU.add),
                               sm("x3_ready"))
                    dve.wait_ge(sm("o_turned"), 1)
                    V.done(dve, dve.tensor_copy(otok[:, 0, :], bank2(0)), sm("o_ready0"))

def flat_inputs(inputs, ascontiguous):
    shapes = {
        "x": (SEQ, D), "c": (8, P), "c_2": (8, P), "w_ada": (D, 6 * D), "b_ada": (48, P), "g_pre_mix": (8, P),
        "g_post_mix": (8, P), "g_pre_ffn": (8, P), "g_post_ffn": (8, P), "w_in": (D, -1), "b_gates": (1, 8),
        "conv_qk": (32, P), "w_cmp_k": (CMP_BLOCK, AD, AD), "w_cmp_v": (CMP_BLOCK, AD, AD),
        "pos_cmp_k": (CMP_BLOCK, AD), "pos_cmp_v": (CMP_BLOCK, AD), "rel_bias": (NBUCKET, AH), "w_out": (D, D),
        "w_router": (D, NE), "b_router": (1, NE), "w_up": (NE, D, 2 * DE), "b_up": (NE, 2 * DE),
        "w_down": (NE, DE, D), "b_down": (NE, D), "positions_2": (SEQ, 1), "ada_w_2": (D, 3 * D), "ada_b_2": (24, P),
        "norm_g_2": (8, P), "w_in_2": (D, -1), "q_norm_g_2": (1, HD), "k_norm_g_2": (1, HD),
        "idx_k_ln_g_2": (1, ID), "idx_k_ln_b_2": (1, ID), "conv_w_2": (96, P), "conv_b_2": (24, P),
        "dt_bias_2": (1, SH), "a_log_2": (1, SH), "d_skip_2": (1, SH), "ssm_norm_g_2": (16, P),
        "w_branch_att_2": (D, D), "w_branch_ssm_2": (DI, D), "w_out_2": (D, D),
    }
    return {n: ascontiguous(inputs[n]).reshape(s) for n, s in shapes.items()}


def kernel(**inputs):
    import numpy as _np
    import concourse.bacc as _bacc
    from concourse import mybir as _mybir
    from concourse.bass_utils import run_bass_kernel_spmd as _run

    nc = _bacc.Bacc("TRN2", target_bir_lowering=False, num_devices=1)
    given = flat_inputs(inputs, _np.ascontiguousarray)
    arrays, aps = {}, {}
    constants, onehots = shape_constants()
    for name, a in list(given.items()) + [("constants", constants), ("onehots", onehots)]:
        arrays[f"in_{name}_dram"] = a
        aps[name] = nc.dram_tensor(f"in_{name}_dram", a.shape, _mybir.dt.from_np(a.dtype), kind="ExternalInput").ap()
    out = nc.dram_tensor("out_0_dram", (SEQ, D), _mybir.dt.float32, kind="ExternalOutput").ap()
    two_layers(nc, aps, aps["constants"], aps["onehots"], out)
    r = _run(nc, [arrays], core_ids=[0])
    return r.results[0]["out_0_dram"].reshape(1, SEQ, D)
```
